# Optimizing a Trainium2 kernel written in Bass

```python
import math
import jax, jax.numpy as jnp
from jax import lax
import numpy as np

D_MODEL = 1024
BATCH = 1
SEQ = 512
DEPTH = 2

N_MIXERS = 2
N_DIFF_LAYERS = (DEPTH + 1) // 2
N_SWA_LAYERS = DEPTH // 2

DIFF_HEADS = 8
DIFF_HEAD_DIM = D_MODEL // DIFF_HEADS // 2
DIFF_Q_BLOCK = 128

SWA_Q_HEADS = 16
SWA_KV_HEADS = 4
SWA_GROUP = SWA_Q_HEADS // SWA_KV_HEADS
SWA_HEAD_DIM = D_MODEL // SWA_Q_HEADS
WINDOW = 128
SWA_BLOCK = WINDOW

ROPE_DIM = 64
ROPE_THETA = 10000.0

D_FF = 2816
CONV_WIDTH = 3
PLE_DIM = 256
EPS = 1e-6


def rms_norm(x, g):
    xf = x.astype(jnp.float32)
    y = xf * lax.rsqrt(jnp.mean(xf * xf, axis=-1, keepdims=True) + EPS)
    return (y * g.astype(jnp.float32)).astype(x.dtype)

def rope_tables(positions):
    inv_freq = ROPE_THETA ** (-jnp.arange(0, ROPE_DIM, 2, dtype=jnp.float32) / ROPE_DIM)
    ang = positions.astype(jnp.float32)[..., None] * inv_freq
    return jnp.cos(ang), jnp.sin(ang)

def apply_rope(x, cos, sin):
    xf = x.astype(jnp.float32)
    x1, x2 = jnp.split(xf, 2, axis=-1)
    c, s = cos[:, :, None, :], sin[:, :, None, :]
    return jnp.concatenate([x1 * c - x2 * s, x2 * c + x1 * s], axis=-1).astype(x.dtype)

def diff_attention(h, w_qkv, w_o, lam, subln, cos, sin, layer_idx):
    B, S, _ = h.shape
    H, d = DIFF_HEADS, DIFF_HEAD_DIM
    q, k, v = jnp.split(h @ w_qkv, 3, axis=-1)
    q = apply_rope(q.reshape(B, S, 2 * H, d), cos, sin)
    k = apply_rope(k.reshape(B, S, 2 * H, d), cos, sin)
    v = v.reshape(B, S, H, 2 * d)
    lam_init = 0.8 - 0.6 * math.exp(-0.3 * layer_idx)
    lf = lam.astype(jnp.float32)
    lam_full = jnp.exp(jnp.sum(lf[0] * lf[1])) - jnp.exp(jnp.sum(lf[2] * lf[3])) + lam_init
    scale = d ** -0.5
    nb = S // DIFF_Q_BLOCK
    q_blocks = jnp.moveaxis(q.reshape(B, nb, DIFF_Q_BLOCK, 2 * H, d), 1, 0)

    def one_block(qb):
        s = jnp.einsum('bqhd,bkhd->bhqk', qb, k).astype(jnp.float32) * scale
        pr = jax.nn.softmax(s, axis=-1).reshape(B, H, 2, DIFF_Q_BLOCK, S)
        a = (pr[:, :, 0] - lam_full * pr[:, :, 1]).astype(v.dtype)
        return jnp.einsum('bhqk,bkhe->bqhe', a, v)

    o = lax.map(one_block, q_blocks)
    o = jnp.moveaxis(o, 0, 1).reshape(B, S, H, 2 * d)
    o = rms_norm(o, subln) * (1.0 - lam_init)
    return o.reshape(B, S, H * 2 * d) @ w_o

def windowed_gqa(h, w_qkv, w_o, sinks, cos, sin):
    B, S, _ = h.shape
    Hq, Hkv, G, d, L = SWA_Q_HEADS, SWA_KV_HEADS, SWA_GROUP, SWA_HEAD_DIM, SWA_BLOCK
    nb = S // L
    q, k, v = jnp.split(h @ w_qkv, [Hq * d, Hq * d + Hkv * d], axis=-1)
    q = apply_rope(q.reshape(B, S, Hq, d), cos, sin).reshape(B, nb, L, Hkv, G, d)
    k = apply_rope(k.reshape(B, S, Hkv, d), cos, sin)
    v = v.reshape(B, S, Hkv, d)

    def band(t):
        tp = jnp.pad(t, ((0, 0), (L, L), (0, 0), (0, 0))).reshape(B, nb + 2, L, Hkv, d)
        return jnp.concatenate([tp[:, :-2], tp[:, 1:-1], tp[:, 2:]], axis=2)

    kb, vb = band(k), band(v)
    s = jnp.einsum('bnqhgd,bnchd->bnhgqc', q, kb).astype(jnp.float32) * (d ** -0.5)
    blk = jnp.arange(nb)[:, None, None] * L
    qpos = blk + jnp.arange(L)[None, :, None]
    kpos = blk - L + jnp.arange(3 * L)[None, None, :]
    mask = (jnp.abs(kpos - qpos) <= WINDOW) & (kpos >= 0) & (kpos < S)
    s = jnp.where(mask[None, :, None, None], s, -jnp.inf)
    sink = sinks.astype(jnp.float32).reshape(1, 1, Hkv, G, 1, 1)
    m = jnp.maximum(jnp.max(s, axis=-1, keepdims=True), sink)
    e = jnp.exp(s - m)
    pr = e / (jnp.sum(e, axis=-1, keepdims=True) + jnp.exp(sink - m))
    o = jnp.einsum('bnhgqc,bnchd->bnqhgd', pr.astype(v.dtype), vb).reshape(B, S, Hq * d)
    return o @ w_o

def conv_ffn(h, w_up, conv_w, conv_b, w_down):
    S = h.shape[1]
    u = h @ w_up
    pad = CONV_WIDTH // 2
    up = jnp.pad(u, ((0, 0), (pad, pad), (0, 0)))
    u = sum(up[:, t:t + S] * conv_w[t] for t in range(CONV_WIDTH)) + conv_b
    gate, val = jnp.split(u, 2, axis=-1)
    return (jax.nn.silu(gate) * val) @ w_down

def first_inputs(seed: int = 0) -> dict:
    key = jax.random.key(seed)
    ks = jax.random.split(key, 24)
    D = D_MODEL

    def nrm(k, shape, scale):
        return jax.random.normal(k, shape, jnp.float32) * scale

    return {
        "x": nrm(ks[0], (BATCH, SEQ, D), 1.0),
        "p": nrm(ks[1], (DEPTH, BATCH, SEQ, PLE_DIM), 1.0),
        "positions": jnp.broadcast_to(jnp.arange(SEQ, dtype=jnp.int32), (BATCH, SEQ)),
        "attn_norm": 1.0 + nrm(ks[2], (DEPTH, D), 0.05),
        "ffn_norm": 1.0 + nrm(ks[3], (DEPTH, D), 0.05),
        "ple_norm": 1.0 + nrm(ks[4], (DEPTH, D), 0.05),
        "final_norm": 1.0 + nrm(ks[5], (D,), 0.05),
        "diff_w_qkv": nrm(ks[6], (N_DIFF_LAYERS, D, 3 * D), D ** -0.5),
        "diff_w_o": nrm(ks[7], (N_DIFF_LAYERS, D, D), D ** -0.5),
        "diff_lambda": nrm(ks[8], (N_DIFF_LAYERS, 4, DIFF_HEAD_DIM), 0.1),
        "diff_subln": 1.0 + nrm(ks[9], (N_DIFF_LAYERS, 2 * DIFF_HEAD_DIM), 0.05),
        "swa_w_qkv": nrm(ks[10], (N_SWA_LAYERS, D, (SWA_Q_HEADS + 2 * SWA_KV_HEADS) * SWA_HEAD_DIM), D ** -0.5),
        "swa_w_o": nrm(ks[11], (N_SWA_LAYERS, SWA_Q_HEADS * SWA_HEAD_DIM, D), D ** -0.5),
        "swa_sinks": nrm(ks[12], (N_SWA_LAYERS, SWA_Q_HEADS), 0.5),
        "ffn_w_up": nrm(ks[13], (DEPTH, D, 2 * D_FF), D ** -0.5),
        "ffn_conv_w": nrm(ks[14], (DEPTH, CONV_WIDTH, 2 * D_FF), CONV_WIDTH ** -0.5),
        "ffn_conv_b": nrm(ks[15], (DEPTH, 2 * D_FF), 0.02),
        "ffn_w_down": nrm(ks[16], (DEPTH, D_FF, D), D_FF ** -0.5),
        "ple_w_proj": nrm(ks[17], (DEPTH, PLE_DIM, D), PLE_DIM ** -0.5),
        "ple_w_gate": nrm(ks[18], (DEPTH, D, D), D ** -0.5),
    }

def first_block(x, p, positions, attn_norm, ffn_norm, ple_norm, final_norm,
              diff_w_qkv, diff_w_o, diff_lambda, diff_subln,
              swa_w_qkv, swa_w_o, swa_sinks,
              ffn_w_up, ffn_conv_w, ffn_conv_b, ffn_w_down,
              ple_w_proj, ple_w_gate):
    cos, sin = rope_tables(positions)
    h = x
    for i in range(DEPTH):
        j = i // N_MIXERS
        hn = rms_norm(h, attn_norm[i])
        if i % N_MIXERS == 0:
            mix = diff_attention(hn, diff_w_qkv[j], diff_w_o[j], diff_lambda[j], diff_subln[j], cos, sin, i)
        else:
            mix = windowed_gqa(hn, swa_w_qkv[j], swa_w_o[j], swa_sinks[j], cos, sin)
        h = h + mix
        h = h + conv_ffn(rms_norm(h, ffn_norm[i]), ffn_w_up[i], ffn_conv_w[i], ffn_conv_b[i], ffn_w_down[i])
        gate = jax.nn.sigmoid(rms_norm(h, ple_norm[i]) @ ple_w_gate[i])
        h = h + (p[i] @ ple_w_proj[i]) * gate
    return rms_norm(h, final_norm)


DEPTH_2 = 1

CONV_CH = D_MODEL // 2
CONV_WIDTH_2 = 31
N_HEADS = 8
HEAD_DIM = 64
ATTN_WIDTH = N_HEADS * HEAD_DIM
D_FF_2 = ((8 * D_MODEL // 3 + 255) // 256) * 256
Q_BLOCK = 128

COL_SIZES = (2 * CONV_CH,
             ATTN_WIDTH,
             ATTN_WIDTH,
             ATTN_WIDTH,
             N_HEADS,
             D_MODEL,
             D_MODEL)
IN_COLS = sum(COL_SIZES)
COL_SPLITS = tuple(int(s) for s in np.cumsum(COL_SIZES)[:-1])


def rmsnorm(x, g):
    xf = x.astype(jnp.float32)
    inv = lax.rsqrt(jnp.mean(xf * xf, axis=-1, keepdims=True) + EPS)
    return (xf * inv).astype(x.dtype) * g

def layernorm(x, g, b):
    xf = x.astype(jnp.float32)
    mu = jnp.mean(xf, axis=-1, keepdims=True)
    var = jnp.mean(jnp.square(xf - mu), axis=-1, keepdims=True)
    return ((xf - mu) * lax.rsqrt(var + EPS)).astype(x.dtype) * g + b

def causal_depthwise_conv(a, w, b):
    out = lax.conv_general_dilated(
        a, w[:, None, :], window_strides=(1,), padding=[(CONV_WIDTH_2 - 1, 0)],
        dimension_numbers=("NWC", "WIO", "NWC"), feature_group_count=CONV_CH)
    return out + b

def conformer_conv_branch(a_in, w_dw, b_dw, g_ln, b_ln, w_out):
    a = a_in[..., :CONV_CH] * jax.nn.sigmoid(a_in[..., CONV_CH:])
    a = causal_depthwise_conv(a, w_dw, b_dw)
    a = jax.nn.silu(layernorm(a, g_ln, b_ln))
    return a @ w_out

def forgetting_attention(q, k, v, f_logit, b_forget, g_q, g_k):
    B, S, _ = q.shape
    nb = S // Q_BLOCK
    def heads(t, g):
        t = t.reshape(B, S, N_HEADS, HEAD_DIM)
        if g is not None:
            t = rmsnorm(t, g)
        return t.transpose(0, 2, 1, 3)
    qh, kh, vh = heads(q, g_q), heads(k, g_k), heads(v, None)
    log_f = jax.nn.log_sigmoid(f_logit.astype(jnp.float32) + b_forget.astype(jnp.float32))
    c = jnp.cumsum(log_f, axis=1).transpose(0, 2, 1)
    scale = HEAD_DIM ** -0.5
    q_blocks = qh.reshape(B, N_HEADS, nb, Q_BLOCK, HEAD_DIM).transpose(2, 0, 1, 3, 4)
    c_blocks = c.reshape(B, N_HEADS, nb, Q_BLOCK).transpose(2, 0, 1, 3)
    k_pos = jnp.arange(S)

    def one_block(args):
        qi, ci, i = args
        s = jnp.einsum("bhqd,bhkd->bhqk", qi, kh).astype(jnp.float32) * scale
        s = s + ci[..., :, None] - c[:, :, None, :]
        q_pos = i * Q_BLOCK + jnp.arange(Q_BLOCK)
        s = jnp.where(k_pos[None, :] <= q_pos[:, None], s, -jnp.inf)
        p = jax.nn.softmax(s, axis=-1).astype(vh.dtype)
        return jnp.einsum("bhqk,bhkd->bhqd", p, vh)

    out = lax.map(one_block, (q_blocks, c_blocks, jnp.arange(nb)))
    return out.transpose(1, 0, 3, 2, 4).reshape(B, S, ATTN_WIDTH)

def second_inputs(seed: int = 0) -> dict:
    key = jax.random.key(seed)
    ks = jax.random.split(key, 20)
    f32 = jnp.float32
    def nrm(k, shape, fan_in):
        return jax.random.normal(k, shape, f32) * fan_in ** -0.5
    def gain(k, shape):
        return 1.0 + 0.02 * jax.random.normal(k, shape, f32)
    return {
        "x": jax.random.normal(ks[0], (BATCH, SEQ, D_MODEL), f32),
        "g_mix": gain(ks[1], (DEPTH_2, D_MODEL)),
        "w_in": nrm(ks[2], (DEPTH_2, D_MODEL, IN_COLS), D_MODEL),
        "b_forget": jax.random.uniform(ks[3], (DEPTH_2, N_HEADS), f32, 2.0, 5.0),
        "w_dw": nrm(ks[4], (DEPTH_2, CONV_WIDTH_2, CONV_CH), CONV_WIDTH_2),
        "b_dw": 0.02 * jax.random.normal(ks[5], (DEPTH_2, CONV_CH), f32),
        "g_conv_ln": gain(ks[6], (DEPTH_2, CONV_CH)),
        "b_conv_ln": 0.02 * jax.random.normal(ks[7], (DEPTH_2, CONV_CH), f32),
        "w_conv_out": nrm(ks[8], (DEPTH_2, CONV_CH, D_MODEL), CONV_CH),
        "g_q": gain(ks[9], (DEPTH_2, HEAD_DIM)),
        "g_k": gain(ks[10], (DEPTH_2, HEAD_DIM)),
        "w_attn_out": nrm(ks[11], (DEPTH_2, ATTN_WIDTH, D_MODEL), ATTN_WIDTH),
        "w_out": nrm(ks[12], (DEPTH_2, D_MODEL, D_MODEL), D_MODEL),
        "g_ffn": gain(ks[13], (DEPTH_2, D_MODEL)),
        "w_ffn_in": nrm(ks[14], (DEPTH_2, D_MODEL, 2 * D_FF_2), D_MODEL),
        "w_ffn_out": nrm(ks[15], (DEPTH_2, D_FF_2, D_MODEL), D_FF_2),
    }

def second_block(x, g_mix, w_in, b_forget, w_dw, b_dw, g_conv_ln, b_conv_ln, w_conv_out,
              g_q, g_k, w_attn_out, w_out, g_ffn, w_ffn_in, w_ffn_out):
    for l in range(DEPTH_2):
        h = rmsnorm(x, g_mix[l])
        proj = h @ w_in[l]
        a_in, q, k, v, f_logit, gate_a, gate_b = jnp.split(proj, COL_SPLITS, axis=-1)
        y_conv = conformer_conv_branch(a_in, w_dw[l], b_dw[l], g_conv_ln[l],
                                       b_conv_ln[l], w_conv_out[l])
        y_attn = forgetting_attention(q, k, v, f_logit, b_forget[l], g_q[l], g_k[l]) @ w_attn_out[l]
        merged = jax.nn.sigmoid(gate_a) * y_conv + jax.nn.sigmoid(gate_b) * y_attn
        x = x + merged @ w_out[l]
        h2 = rmsnorm(x, g_ffn[l])
        gu = h2 @ w_ffn_in[l]
        x = x + (jax.nn.silu(gu[..., :D_FF_2]) * gu[..., D_FF_2:]) @ w_ffn_out[l]
    return x


def setup_inputs(seed=0):
    out = dict(first_inputs(seed))
    for name, value in second_inputs(seed + 1).items():
        if name != "x":
            out[name + "_2"] = value
    return out


def reference(
    x, p, positions, attn_norm, ffn_norm, ple_norm, final_norm, diff_w_qkv, diff_w_o,
    diff_lambda, diff_subln, swa_w_qkv, swa_w_o, swa_sinks, ffn_w_up, ffn_conv_w, ffn_conv_b,
    ffn_w_down, ple_w_proj, ple_w_gate, g_mix_2, w_in_2, b_forget_2, w_dw_2, b_dw_2,
    g_conv_ln_2, b_conv_ln_2, w_conv_out_2, g_q_2, g_k_2, w_attn_out_2, w_out_2, g_ffn_2,
    w_ffn_in_2, w_ffn_out_2,
):
    x = first_block(
        x, p, positions, attn_norm, ffn_norm, ple_norm, final_norm, diff_w_qkv, diff_w_o,
        diff_lambda, diff_subln, swa_w_qkv, swa_w_o, swa_sinks, ffn_w_up, ffn_conv_w,
        ffn_conv_b, ffn_w_down, ple_w_proj, ple_w_gate,
    )
    return second_block(
        x, g_mix_2, w_in_2, b_forget_2, w_dw_2, b_dw_2, g_conv_ln_2, b_conv_ln_2, w_conv_out_2,
        g_q_2, g_k_2, w_attn_out_2, w_out_2, g_ffn_2, w_ffn_in_2, w_ffn_out_2,
    )


_drawn_inputs = setup_inputs


def setup_inputs(seed=0):
    import zlib

    import numpy as np

    out = dict(_drawn_inputs(seed))
    spreads = {}
    factors = {'ple_norm': 5.292,
     'swa_sinks': 8.0,
     'ffn_conv_b': 3.106,
     'g_mix_2': 5.589,
     'b_dw_2': 4.161,
     'g_conv_ln_2': 22.287,
     'b_conv_ln_2': 23.206,
     'g_q_2': 8.0,
     'g_k_2': 8.0,
     'g_ffn_2': 10.949}
    for name, (base, spread) in spreads.items():
        noise = np.random.default_rng([zlib.crc32(name.encode()), seed]).standard_normal(out[name].shape)
        drawn = base * np.exp(spread * noise) if base else spread * noise
        out[name] = __import__('jax').numpy.asarray(drawn.astype(out[name].dtype))
    for name, factor in factors.items():
        out[name] = (out[name] * factor).astype(out[name].dtype)
    return out
```

```python
from contextlib import ExitStack

import numpy as np

import concourse.bass as bass
from concourse import mybir

ALU = mybir.AluOpType
ACT = mybir.ActivationFunctionType
F32 = mybir.dt.float32
F32R = mybir.dt.float32r
I32 = mybir.dt.int32
AX = mybir.AxisListType.X

P = 128
T = 512
TB = T // P
D = 1024
KC = D // P
FC = 2816 // P
PARTS = (8, 8, 6)
PART0 = (0, 8, 16)
RING = 4
RAWS = 2
BANKS = 4
EPS = 1e-6
TAPS = 31
CONV = 512
CT = CONV // P
PADW = T + TAPS - 1
LAM_INIT = 0.8 - 0.6 * float(np.exp(-0.3 * 0))
QSCALE = 64.0 ** -0.5
NEG = -1e30

STAGES = [("v1", 8, 8), ("qk1", 16, 16), ("o1", 8, 8)]
for _l in range(3):
    if _l == 1:
        STAGES += [("v2", 2, 4), ("k2", 2, 2), ("q2", 8, 8), ("o2", 8, 8)]
    if _l == 2:
        STAGES += [("a3", 8, 8), ("ga3", 8, 8), ("v3", 4, 4), ("co3", 4, 8), ("qk3", 8, 8),
                   ("gb3", 8, 8), ("ao3", 4, 8), ("out3", 8, 8)]
    for _p, _n in enumerate(PARTS):
        STAGES += [(f"up{_l}.{_p}", 2 * _n, 2 * _n), (f"down{_l}.{_p}", 8, 8)]
    if _l < 2:
        STAGES += [(f"pp{_l}", 2, 8), (f"gate{_l}", 8, 8)]
SLAB0, TILE0 = {}, {}
_s = _t = 0
for _name, _ns, _nt in STAGES:
    SLAB0[_name], TILE0[_name] = _s, _t
    _s, _t = _s + _ns, _t + _nt
SLABS = _s
assert SLABS % RING == 0

PCOLS = {}
_c = 0
for _name, _n in (("attn_norm", 16), ("ffn_norm", 16), ("ple_norm", 16), ("final_norm", 8),
                  ("g_mix", 8), ("g_ffn", 8), ("subln", 1), ("conv_w", 2 * 4 * 2 * FC),
                  ("sinks", 16), ("b_forget", 8), ("w_dw", TAPS * CT), ("b_dw", CT),
                  ("g_ln", CT), ("b_ln", CT), ("g_q", 1), ("g_k", 1), ("w_f", KC * 8)):
    PCOLS[_name] = (_c, _c + _n)
    _c += _n
NPAR = _c
CCOLS = {}
_c = 0
for _name, _n in (("ident", P), ("before", P), ("after", P), ("ones", P), ("heads", P), ("upto", P),
                  ("pick", 16), ("minus", 8), ("freq", 1), ("sign", 1), ("lam", 0)):
    CCOLS[_name] = (_c, _c + _n)
    _c += _n
NCON = _c


def constants():
    c = np.zeros((P, NCON), np.float32)
    i = np.arange(P)

    def put(name, a):
        c[:, CCOLS[name][0]:CCOLS[name][1]] = a

    put("ident", np.eye(P))
    put("before", np.where(i[None, :] >= i[:, None], 0, NEG))
    put("after", np.where(i[None, :] <= i[:, None], 0, NEG))
    put("ones", 1)
    put("heads", i[:, None] // 64 == i[None, :] // 64)
    put("upto", i[:, None] <= i[None, :])
    put("pick", np.arange(16)[None, :] == 7)
    minus = np.zeros((P, 8))
    for h in range(8):
        minus[h, h] = minus[32 + h, h] = -1
    put("minus", minus)
    inv = np.float32(10000.0) ** (-np.arange(0, 64, 2, dtype=np.float32) / np.float32(64))
    put("freq", inv.astype(np.float32)[i % 32][:, None])
    put("sign", np.where(i % 64 < 32, -1, 1)[:, None])
    return c


class Own:

    def __init__(self, eng, sem):
        self.eng, self.sem, self.n = eng, sem, 0

    def step(self, ins):
        ins.then_inc(self.sem, 1)
        self.n = self.n + 1

    def wait(self):
        self.eng.wait_ge(self.sem, self.n)

    def rounds(self, first, end, per, body):
        base = self.n
        if end - first == 1:
            body(first)
        else:
            with self.eng.Fori(first, end) as i:
                self.n = base + (i - first) * per if per else base
                body(i)
        self.n = base + (end - first) * per


def slab_of(stage, i, j):
    s = SLAB0[stage] + j
    return s + 4 * i, s % RING, s // RAWS + (4 // RAWS) * i


def tile_of(stage, i, j, per=4):
    t = TILE0[stage] + j
    assert per == 4
    return t % BANKS, t // BANKS + i


def build(nc, xT, pT, posd, wts, par, con, lamd, outT):
    ctx = ExitStack()
    with ctx:
        def sb(name, shape, dt=F32):
            return ctx.enter_context(nc.sbuf_tensor(name, shape, dt))

        def sem(name):
            return ctx.enter_context(nc.semaphore(name))

        raw = sb("raw", [P, RAWS, D])
        whi = sb("whi", [P, RING, D], F32R)
        wlo = sb("wlo", [P, RING, D], F32R)
        X = sb("X", [P, KC, T])
        Bhi = [sb(f"Bhi{n}", [P, KC * T], F32R) for n in range(2)]
        Blo = [sb(f"Blo{n}", [P, KC * T], F32R) for n in range(2)]
        qkhi = sb("qkhi", [P, 2, 2, T], F32R)
        qklo = sb("qklo", [P, 2, 2, T], F32R)
        pthi = sb("pthi", [P, 4, T], F32R)
        ptlo = sb("ptlo", [P, 4, T], F32R)
        R = sb("R", [P, T])
        acc = sb("acc", [P, T])
        sq = sb("sq", [P, 2, T])
        cosT = sb("cosT", [P, T])
        sinT = sb("sinT", [P, T])
        AR = sb("AR", [P, 9344])
        par_sb = sb("par_sb", [P, NPAR])
        con_sb = sb("con_sb", [P, NCON])
        constR = sb("constR", [P, 3, P], F32R)
        minusR = sb("minusR", [P, 8, P], F32R)
        cc = sb("cc", [P, T], F32R)
        wfhi = sb("wfhi", [P, KC * 8], F32R)
        wflo = sb("wflo", [P, KC * 8], F32R)
        nmax = sb("nmax", [P, 8])
        rsum = sb("rsum", [P, 8])
        rinv = sb("rinv", [P, 8])
        rcol = sb("rcol", [P, TB])
        lam = sb("lam", [P, 8])
        gs = sb("gs", [P, 4])
        fl = sb("fl", [P, 4, TB * 8])
        eps = sb("eps", [P, 1])
        credit = sb("credit", [P, BANKS + 2])
        PS = ctx.enter_context(nc.psum_tensor("PS", [P, 8, T], F32))

        def chunks(b):
            return b[:, :].rearrange("p (k t) -> p k t", k=KC)

        def ar(off, n=1):
            v = AR[:, off:off + n * T]
            return v.rearrange("p (n t) -> p n t", n=n)

        def cpar(name, k=0, n=1):
            o = PCOLS[name][0]
            return par_sb[:, o + k:o + k + n]

        def gain(name, col, m):
            o = PCOLS[name][0] + col
            return par_sb[:, bass.ds(o + m, 1)]

        def ccon(name, a=0, b=None):
            o, e = CCOLS[name]
            return con_sb[:, o + a:(e if b is None else o + b)]

        def f32(a):
            return a.bitcast(F32)

        conv_w = par_sb[:, PCOLS["conv_w"][0]:PCOLS["conv_w"][1]]\
            .rearrange("p (l t u c) -> p l t u c", l=2, t=4, u=2)
        identR, beforeR, afterR = constR[:, 0, :], constR[:, 1, :], constR[:, 2, :]
        ident = f32(identR)
        ones = ccon("ones")

        rC, rS = ar(0)[:, 0, :], ar(512)[:, 0, :]
        swap, qraw = ar(1024, 2), ar(2048, 2)
        prob = ar(3072, 4)
        OA = ar(5120, 8)
        us, cv, av = ar(0, 4), ar(2048, 4), ar(4096, 2)
        PT = ar(8192, 2)
        gt, gu, pp = ar(0, 2), ar(1024, 2), ar(4096, 8)
        apad = AR[:, 0:CT * PADW].rearrange("p (c t) -> p c t", c=CT)
        cvo = ar(2176, 4)
        t3 = ar(4224, 2)
        G = ar(5248, 8)
        atmp = ar(5248, 3)
        prob3, qraw3, OA3 = ar(0, 4), ar(2048, 2), ar(3072, 4)
        G2 = ar(0, 8)
        angs = ar(0, 6)

        raw_ready = [sem(f"raw_ready{n}") for n in range(RAWS)]
        hi_ready = sem("hi_ready")
        lo_ready = sem("lo_ready")
        slab_done = sem("slab_done")
        tile_free = [sem(f"tile_free{n}") for n in range(BANKS)]
        par_in, x_in, pos_in, p_in = sem("par_in"), sem("x_in"), sem("pos_in"), sem("p_in")
        consts_ready = sem("consts_ready")
        trig_ready = sem("trig_ready")
        sq_ready, sq_used = sem("sq_ready"), sem("sq_used")
        xhi_ready, x_split = sem("xhi_ready"), sem("x_split")
        ss_done, root_ready, r_ready = sem("ss_done"), sem("root_ready"), sem("r_ready")
        rcol_done, rcol_ready = sem("rcol_done"), sem("rcol_ready")
        vhi_ready, pad_ready = sem("vhi_ready"), sem("pad_ready")
        swap_ready, rope_ready, qhi_ready, q_ready = (
            sem("swap_ready"), sem("rope_ready"), sem("qhi_ready"), sem("q_ready"))
        score_done, max_ready, exp_ready, prob_ready = (
            sem("score_done"), sem("max_ready"), sem("exp_ready"), sem("prob_ready"))
        trans_done, pthi_ready, pt_ready, pv_done, o_ready = (
            sem("trans_done"), sem("pthi_ready"), sem("pt_ready"), sem("pv_done"), sem("o_ready"))
        osq_ready, osum_done, oroot_ready, orinv_ready = (
            sem("osq_ready"), sem("osum_done"), sem("oroot_ready"), sem("orinv_ready"))
        obc_done, onorm_ready, ohi_ready, o_split = (
            sem("obc_done"), sem("onorm_ready"), sem("ohi_ready"), sem("o_split"))
        mid_ready, conv_done, silu_ready, act_ready, ahi_ready, act_split = (
            sem("mid_ready"), sem("conv_done"), sem("silu_ready"), sem("act_ready"),
            sem("ahi_ready"), sem("act_split"))
        phi_ready, p_split, pp_ready = sem("phi_ready"), sem("p_split"), sem("pp_ready")
        sig_ready, sink_ready = sem("sig_ready"), sem("sink_ready")
        ple_added = sem("ple_added")
        y_ready = sem("y_ready")
        asig_ready, a_ready, taps_done, cv_ready = (
            sem("asig_ready"), sem("a_ready"), sem("taps_done"), sem("cv_ready"))
        mean_done, cen_ready, csq_ready, var_done, croot_ready, cn_ready, cs_ready = (
            sem("mean_done"), sem("cen_ready"), sem("csq_ready"), sem("var_done"),
            sem("croot_ready"), sem("cn_ready"), sem("cs_ready"))
        chi_ready, c_split = sem("chi_ready"), sem("c_split")
        f_done, f_lin, f_exp, f_log, cum_done, cum_ready, cumT_done, cchi_ready, cc_ready = (
            sem("f_done"), sem("f_lin"), sem("f_exp"), sem("f_log"), sem("cum_done"),
            sem("cum_ready"), sem("cumT_done"), sem("cchi_ready"), sem("cc_ready"))
        hsum_done, hsq_ready, hroot_ready = sem("hsum_done"), sem("hsq_ready"), sem("hroot_ready")
        dve_step, act_step = sem("dve_step"), sem("act_step")
        out_stored = sem("out_stored")
        block = ctx.enter_context(nc.Block())

        NORMS = ["attn0", "ffn0", "ple0", "attn1", "ffn1", "ple1", "final", "mix", "ffn2"]
        SPLITS = [n for n in NORMS if n != "final"]
        GAIN = {"attn0": ("attn_norm", 0), "attn1": ("attn_norm", 8), "ffn0": ("ffn_norm", 0),
                "ffn1": ("ffn_norm", 8), "ple0": ("ple_norm", 0), "ple1": ("ple_norm", 8),
                "mix": ("g_mix", 0), "ffn2": ("g_ffn", 0)}
        BUF = {"attn0": 0, "ffn0": 0, "ple0": 0, "attn1": 1, "ffn1": 1, "ple1": 1, "mix": 0, "ffn2": 0}
        OBUF = {1: 1, 2: 0}
        ABUF = {0: 1, 1: 0, 2: 1}

        PAIRS = {1: 8, 2: 8, 3: 4}

        def padded(stage, B, src, t):
            vb, nh = (0, 4) if stage == "v2" else (1, 8)
            v = B[vb][:, 0:TB * nh * P].rearrange("p (k n c) -> p k n c", k=TB, n=nh)[:, t]
            v = v.rearrange("p (n two) c -> p n two c", two=2)
            s = src.rearrange("p (n two c) -> p n two c", two=2, c=64)
            return [(v[:, :, u, 64 * u:64 * u + 64], s[:, :, u, :]) for u in range(2)]

        def band(kind, qb):
            if kind == 2:
                lo, hi = max(qb - 1, 0), min(qb + 1, TB - 1)
                masks = [(qb - 1 - lo, beforeR)] * (qb > 0) + [(qb + 1 - lo, afterR)] * (qb < TB - 1)
                return lo, hi - lo + 1, masks
            return 0, qb + 1, [(qb, afterR)]

        SC0 = {1: 0, 2: 64, 3: 128}
        PB0 = {1: 0, 2: 32, 3: 96}
        PV0 = {1: 0, 2: 8, 3: 16}
        QT0 = {1: 0, 2: 16, 3: 26}

        @block.sync
        def _(sp):
            def load(s, slot, freed):
                if freed is not None:
                    sp.wait_ge(lo_ready, freed)
                sp.dma_start(raw[:, slot, :], wts[s]).then_inc(raw_ready[slot], 16)

            for s in range(4):
                load(s, s % RAWS, s - 1 if s >= RAWS else None)
            with sp.Fori(1, SLABS // 4) as i:
                for j in range(4):
                    load(4 * i + j, j % RAWS, 4 * i + j - 1)
            for m in range(KC):
                bank, before = tile_of("down2.2", m // 4, m % 4)
                sp.wait_ge(tile_free[bank], before + 2)
                sp.dma_start(outT[:, m, :], X[:, m, :]).then_inc(out_stored, 16)
            sp.wait_ge(out_stored, 16 * KC)

        @block.gpsimd
        def _(pool):
            with pool.Fori(0, SLABS // 4) as i:
                for j in range(4):
                    pool.wait_ge(hi_ready, 4 * i + j + 1)
                    pool.tensor_tensor(wlo[:, j, :], raw[:, j % RAWS, :], f32(whi[:, j, :]),
                                       ALU.subtract).then_inc(lo_ready, 1)

        @block.tensor
        def _(pe):
            def mm(out, w, x, start, stop):
                return pe.matmul(out, w, x, start=start, stop=stop)

            def mm3(out, ahi, alo, bhi, blo, start, stop):
                mm(out, ahi, bhi, start, False)
                mm(out, ahi, blo, False, False)
                return mm(out, alo, bhi, False, stop)

            def weights(s):
                pe.wait_ge(lo_ready, s + 1)

            def open_tile(stage, i, j):
                bank, before = tile_of(stage, i, j)
                pe.wait_ge(tile_free[bank], before + 1)
                return PS[:, bank, :]

            def tile(stage, i, j, hi, lo, nk, ready=None):
                s, slot, _ = slab_of(stage, i, j)
                weights(s)
                out = open_tile(stage, i, j)
                for k in range(nk):
                    if ready is not None:
                        pe.wait_ge(ready[0], ready[1] + k + 1)
                    last = mm3(out, whi[:, slot, k * P:k * P + P], wlo[:, slot, k * P:k * P + P],
                               hi[:, k, :], lo[:, k, :], k == 0, k == nk - 1)
                last.then_inc(slab_done, 1)

            def norm_sum(norm):
                pe.wait_ge(sq_used, KC * (NORMS.index(norm) + 1))
                mm(PS[:, 7, :], ones, acc[:, :], True, True).then_inc(ss_done, 1)

            def tiles(stage, n, hi, lo, nk, ready, norm=None):
                for j in range(4):
                    tile(stage, 0, j, hi, lo, nk, ready if j == 0 else None)
                    if j == 0 and norm:
                        norm_sum(norm)
                if n > 8:
                    with pe.Fori(1, n // 4) as i:
                        for j in range(4):
                            tile(stage, i, j, hi, lo, nk)
                elif n > 4:
                    for j in range(4):
                        tile(stage, 1, j, hi, lo, nk)

            def split_of(norm):
                b = BUF[norm]
                return chunks(Bhi[b]), chunks(Blo[b]), (x_split, KC * SPLITS.index(norm))

            def values(stage, norm, halves, slabs, width):
                hi, lo, ready = split_of(norm)
                kk = KC // slabs
                for hf in range(halves):
                    for q in range(slabs):
                        s, slot, _ = slab_of(stage, 0, hf * slabs + q)
                        weights(s)
                        for t in range(TB):
                            if q == 0:
                                open_tile(stage, 0, hf * TB + t)
                            out = PS[:, tile_of(stage, 0, hf * TB + t)[0], 0:width]
                            for k in range(q * kk, q * kk + kk):
                                if hf == 0 and t == 0:
                                    pe.wait_ge(ready[0], ready[1] + k + 1)
                                c = (k - q * kk) * width
                                tk = slice(t * P, t * P + P)
                                w, v = whi[:, slot, c:c + width], wlo[:, slot, c:c + width]
                                last = mm3(out, hi[:, k, tk], lo[:, k, tk], w, v, k == 0, k == KC - 1)
                        last.then_inc(slab_done, 1)
                        if hf == 0 and q == slabs // 2 and stage != "v3":
                            norm_sum(norm)
                    if hf == 0 and stage != "v3":
                        row_to_column()

            def row_to_column():
                row_to_column.n += 1
                pe.wait_ge(r_ready, row_to_column.norms[row_to_column.n - 1] + 1)
                for t in range(TB):
                    last = mm(PS[:, 7, t:t + 1], R[0:1, t * P:t * P + P], ones[0:1, 0:1], True, True)
                last.then_inc(rcol_done, 1)
            row_to_column.n = 0
            row_to_column.norms = [NORMS.index(n) for n in ("attn0", "attn1", "mix")]

            def project_qk(stage, norm, h, which):
                hi, lo, _ = split_of(norm)
                tile(stage, 0, h, hi, lo, KC)

            def scores1(h, qb):
                if qb == 0:
                    pe.wait_ge(q_ready, 2 * h + 2)
                b = h % 2
                for s in range(2):
                    n = 8 * h + 2 * qb + s
                    if n >= 2:
                        pe.wait_ge(exp_ready, n - 1)
                    rows, cols = slice(64 * s, 64 * s + 64), slice(qb * P, qb * P + P)
                    mm3(PS[:, 4 + n % 2, :], qkhi[rows, b, 0, cols], qklo[rows, b, 0, cols],
                        qkhi[rows, b, 1, :], qklo[rows, b, 1, :], True, True).then_inc(score_done, 1)

            def transposes(n, source, blocks):
                pe.wait_ge(prob_ready, n + 1)
                if n:
                    pe.wait_ge(pt_ready, n)
                for k in range(blocks):
                    last = pe.transpose(PS[:, 6, k * P:k * P + P], source[:, k * P:k * P + P], ident)
                last.then_inc(trans_done, 1)

            def all_values(stage, halves):
                bank, before = tile_of(stage, 0, halves * TB - 1)
                pe.wait_ge(tile_free[bank], before + 2)

            def pv1(h):
                pe.wait_ge(pt_ready, 4 * h + 4)
                if h == 0:
                    all_values("v1", 2)
                else:
                    pe.wait_ge(o_ready, h)
                vhi = Bhi[1][:, :].rearrange("p (k n) -> p k n", k=TB)
                vlo = Blo[1][:, :].rearrange("p (k n) -> p k n", k=TB)
                for k in range(TB):
                    last = mm3(PS[:, 7, :], vhi[:, k, h * P:h * P + P], vlo[:, k, h * P:h * P + P],
                               pthi[:, k, :], ptlo[:, k, :], k == 0, k == TB - 1)
                last.then_inc(pv_done, 1)

            def band_scores(kind, j, qb):
                b = j % 2
                kb = b if kind == 3 else j // 4
                first, nb, masks = band(kind, qb)
                if qb == 0:
                    pe.wait_ge(q_ready, QT0[kind] + (2 + j + 1 if kind == 2 else 2 * j + 2))
                    if kind == 3 and j == 0:
                        pe.wait_ge(cc_ready, 1)
                for s in range(2):
                    n = SC0[kind] + 8 * j + 2 * qb + s
                    pe.wait_ge(exp_ready, n - 1)
                    rows, cols = slice(64 * s, 64 * s + 64), slice(qb * P, qb * P + P)
                    keys = slice(first * P, (first + nb) * P)
                    out = PS[:, 4 + n % 2, 0:nb * P]
                    mm3(out, qkhi[rows, b, 0, cols], qklo[rows, b, 0, cols],
                        qkhi[rows, kb, 1, keys], qklo[rows, kb, 1, keys], True, False)
                    if kind == 3:
                        mm(out, minusR[:, 2 * j + s, :], cc[:, keys], False, False)
                    for q, (at, mask) in enumerate(masks):
                        last = mm(out[:, at * P:at * P + P], identR, mask, False, q == len(masks) - 1)
                    last.then_inc(score_done, 1)

            def band_transposes(kind, j, qb):
                _, nb, _ = band(kind, qb)
                pr = prob if kind == 2 else prob3
                for s in range(2):
                    transposes(PB0[kind] + 8 * j + 2 * qb + s, pr[:, 2 * (qb % 2) + s, :], nb)

            def band_pv(kind, j, qb):
                first, nb, _ = band(kind, qb)
                pe.wait_ge(pt_ready, PB0[kind] + 8 * j + 2 * qb + 2)
                if qb == 0:
                    pe.wait_ge(o_ready, PV0[kind] + j)
                    if j == 0:
                        all_values(f"v{kind}", 1)
                vb, nh = (0, 4) if kind == 2 else (1, 8)
                vhi = Bhi[vb][:, 0:TB * nh * P].rearrange("p (k n c) -> p k n c", k=TB, n=nh)
                vlo = Blo[vb][:, 0:TB * nh * P].rearrange("p (k n c) -> p k n c", k=TB, n=nh)
                for s in range(2):
                    head = 2 * (j // 4) + s if kind == 2 else 2 * j + s
                    at = 2 * (qb % 2) + s
                    for k in range(nb):
                        last = mm3(PS[:, 7, qb * P:qb * P + P], vhi[:, first + k, head, :],
                                   vlo[:, first + k, head, :], pthi[:, at, k * P:k * P + P],
                                   ptlo[:, at, k * P:k * P + P], s == 0 and k == 0,
                                   s == 1 and k == nb - 1)
                last.then_inc(pv_done, 1)

            def band_attention(kind, j):
                stage, norm = {2: ("q2", "attn1"), 3: ("qk3", "mix")}[kind]

                def between(qb):
                    if j + 1 < PAIRS[kind]:
                        if kind == 3 and qb < 2:
                            project_qk(stage, norm, 2 * (j + 1) + qb, qb)
                            head_sums(2 * (j + 1) + qb)
                        if kind == 2 and qb == 0:
                            project_qk(stage, norm, j + 1, 0)
                band_scores(kind, j, 0)
                for qb in range(TB):
                    if qb + 1 < TB:
                        band_scores(kind, j, qb + 1)
                    between(qb)
                    band_transposes(kind, j, qb)
                    if qb:
                        band_pv(kind, j, qb - 1)
                band_pv(kind, j, TB - 1)

            def head_sums(t):
                bank, before = tile_of("qk3", 0, t)
                pe.wait_ge(hsq_ready, t + 1)
                mm(PS[:, bank, :], ccon("heads"), sq[:, t % 2, :], True, True).then_inc(hsum_done, 1)

            def feed_forward(l):
                norm = f"ffn{l}"
                hi, lo, ready = split_of(norm)
                ab = ABUF[l]
                for p, n in enumerate(PARTS):
                    tiles(f"up{l}.{p}", 2 * n, hi, lo, KC, ready if p == 0 else None,
                          norm if p == 0 else None)
                    tiles(f"down{l}.{p}", KC, chunks(Bhi[ab]), chunks(Blo[ab]), n,
                          (act_split, l * FC + PART0[p]))

            def embedding(l):
                stage = f"pp{l}"
                pe.wait_ge(p_split, 2 * l + 2)
                for q in range(2):
                    s, slot, _ = slab_of(stage, 0, q)
                    weights(s)
                    for m in range(4):
                        out = open_tile(stage, 0, 4 * q + m)
                        for k in range(2):
                            c = (2 * m + k) * P
                            last = mm3(out, whi[:, slot, c:c + P], wlo[:, slot, c:c + P],
                                       qkhi[:, 0, k, :], qklo[:, 0, k, :], k == 0, k == 1)
                    last.then_inc(slab_done, 1)
                hi, lo, ready = split_of(f"ple{l}")
                tiles(f"gate{l}", KC, hi, lo, KC, ready, f"ple{l}")

            pe.wait_ge(consts_ready, 3)
            values("v1", "attn0", 2, 4, T)
            project_qk("qk1", "attn0", 0, 0)
            project_qk("qk1", "attn0", 1, 1)
            for h in range(8):
                scores1(h, 0)
                for qb in range(TB):
                    if qb + 1 < TB:
                        scores1(h, qb + 1)
                    if h < 7 and qb < 2:
                        project_qk("qk1", "attn0", 2 * (h + 1) + qb, qb)
                    transposes(4 * h + qb, prob[:, 2 * (qb % 2) + 1, :], TB)
                pv1(h)
            for h in range(8):
                pe.wait_ge(osq_ready, h + 1)
                last = mm(PS[0:8, 4, :], ccon("pick", 7 - h, 15 - h), sq[:, h % 2, :], h == 0, h == 7)
                last.then_inc(osum_done, 1)
            pe.wait_ge(orinv_ready, 1)
            for h in range(8):
                if h >= 2:
                    pe.wait_ge(onorm_ready, h - 1)
                mm(PS[:, 5 + h % 2, :], con_sb[0:8, CCOLS["ident"][0] + h:CCOLS["ident"][0] + h + 1]
                   .broadcast_to((8, P)), acc[0:8, :], True, True).then_inc(obc_done, 1)
            tiles("o1", KC, chunks(Bhi[1]), chunks(Blo[1]), KC, (o_split, 0))
            feed_forward(0)
            embedding(0)
            values("v2", "attn1", 1, 2, 256)
            project_qk("k2", "attn1", 0, 0)
            project_qk("k2", "attn1", 1, 0)
            project_qk("q2", "attn1", 0, 0)
            for j in range(8):
                band_attention(2, j)
            tiles("o2", KC, chunks(Bhi[0]), chunks(Blo[0]), KC, (o_split, 8))
            feed_forward(1)
            embedding(1)
            norm_sum("final")
            hi, lo, ready = split_of("mix")
            tiles("a3", 8, hi, lo, KC, ready, "mix")
            tiles("ga3", 8, hi, lo, KC, None)
            row_to_column()
            values("v3", "mix", 1, 4, T)
            pe.wait_ge(rcol_ready, 3)
            pe.wait_ge(p_split, 5)
            pe.wait_ge(cv_ready, 1)
            for t in range(TB):
                tk = slice(t * P, t * P + P)
                for k in range(KC):
                    last = mm3(PS[:, 4, 8 * t:8 * t + 8], hi[:, k, tk], lo[:, k, tk],
                               wfhi[:, 8 * k:8 * k + 8], wflo[:, 8 * k:8 * k + 8], k == 0, k == KC - 1)
            last.then_inc(f_done, 1)
            for c in range(CT):
                pe.wait_ge(cv_ready, CT)
                last = mm(PS[:, 5, :], ones, cvo[:, c, :], c == 0, c == CT - 1)
            last.then_inc(mean_done, 1)
            for c in range(CT):
                pe.wait_ge(csq_ready, c + 1)
                last = mm(PS[:, 6, :], ones, sq[:, c % 2, :], c == 0, c == CT - 1)
                last.then_inc(var_done, 1)
            pe.wait_ge(f_log, 1)
            for t in range(TB):
                for u in range(t + 1):
                    last = mm(PS[:, 7, 8 * t:8 * t + 8], ccon("upto") if u == t else ones,
                              fl[:, 2, 8 * u:8 * u + 8], u == 0, u == t)
            last.then_inc(cum_done, 1)
            pe.wait_ge(cum_ready, 1)
            for t in range(TB):
                last = pe.transpose(PS[0:8, 7, t * P:t * P + P], fl[:, 3, 8 * t:8 * t + 8], ident)
            last.then_inc(cumT_done, 1)

            def four_chunk_tiles(stage, ready0):
                for q in range(4):
                    s, slot, _ = slab_of(stage, 0, q)
                    weights(s)
                    for m in range(2):
                        out = open_tile(stage, 0, 2 * q + m)
                        for k in range(4):
                            if q == 0 and m == 0:
                                pe.wait_ge(ready0[0], ready0[1] + k + 1)
                            c = (4 * m + k) * P
                            last = mm3(out, whi[:, slot, c:c + P], wlo[:, slot, c:c + P],
                                       pthi[:, k, :], ptlo[:, k, :], k == 0, k == 3)
                    last.then_inc(slab_done, 1)
            four_chunk_tiles("co3", (c_split, 0))
            for t in range(2):
                project_qk("qk3", "mix", t, t)
                head_sums(t)
            for j in range(4):
                band_attention(3, j)
            tiles("gb3", 8, hi, lo, KC, None)
            four_chunk_tiles("ao3", (o_split, 16))
            tiles("out3", 8, chunks(Bhi[1]), chunks(Blo[1]), KC, (c_split, 4))
            feed_forward(2)

        @block.scalar
        def _(act):
            own = Own(act, act_step)

            def high(s, slot, half):
                act.wait_ge(raw_ready[slot % RAWS], 16 * half + 16)
                act.activation(whi[:, slot, :], raw[:, slot % RAWS, :], ACT.Copy)\
                   .then_inc(hi_ready, 1)

            def used(stage, i, j, more=True):
                s, slot, half = slab_of(stage, i, j)
                act.wait_ge(slab_done, s + 1)
                if more:
                    high(s + RING, slot, half + RING // RAWS)

            def freed(stage, i, j):
                bank, before = tile_of(stage, i, j)
                act.wait_ge(tile_free[bank], before + 2)

            def square_and_high(norm, m):
                n = NORMS.index(norm)
                c = KC * n + m
                act.wait_ge(sq_used, c - 1) if not (n == 0 and isinstance(m, int) and m < 2) else None
                act.activation(sq[:, square_and_high.slot, :], X[:, m, :], ACT.Square)\
                   .then_inc(sq_ready, 1)
                if norm in GAIN:
                    name, col = GAIN[norm]
                    act.activation(chunks(Bhi[BUF[norm]])[:, m, :], X[:, m, :], ACT.Copy,
                                   scale=gain(name, col, m)).then_inc(xhi_ready, 1)

            def root(norm):
                n = NORMS.index(norm)
                act.wait_ge(ss_done, n + 1)
                act.activation(sq[:, 0, :], PS[:, 7, :], ACT.Sqrt, scale=1.0 / D, bias=eps[:, 0:1])\
                   .then_inc(root_ready, 1)

            def rounds(n, body):
                if n == 1:
                    body(0)
                elif n == 2:
                    body(0)
                    body(1)
                else:
                    with act.Fori(0, n) as i:
                        body(i)

            def residual(stage, norm, last=False):
                if norm:
                    act.wait_ge(r_ready, NORMS.index(norm))

                def body(i):
                    for j in range(4):
                        used(stage, i, j, not (last and i == 1))
                        if norm:
                            freed(stage, i, j)
                            square_and_high.slot = j % 2
                            square_and_high(norm, 4 * i + j)
                rounds(2, body)

            def values(stage, halves, slabs, width):
                for hf in range(halves):
                    for q in range(slabs):
                        used(stage, 0, hf * slabs + q)
                    if hf == 0:
                        act.wait_ge(rcol_ready, {"v1": 1, "v2": 2, "v3": 3}[stage])
                        if stage != "v1":
                            act.wait_ge(pad_ready, {"v2": 4, "v3": 8}[stage])
                    for t in range(TB):
                        bank, _ = tile_of(stage, 0, hf * TB + t)
                        if stage == "v1":
                            outs = [(Bhi[1][:, :].rearrange("p (k n) -> p k n", k=TB)
                                     [:, t, hf * T:hf * T + T], PS[:, bank, :])]
                        else:
                            outs = padded(stage, Bhi, PS[:, bank, 0:width], t)
                        for out, src in outs:
                            last = act.activation(out, src, ACT.Copy, scale=rcol[:, t:t + 1])
                        last.then_inc(vhi_ready, 1)

            def swap_halves(stage, t, n, b):
                used(stage, 0, t)
                bank, _ = tile_of(stage, 0, t)
                if n >= 2:
                    act.wait_ge(rope_ready, n - 1)
                for to, of in ((0, 32), (32, 0), (64, 96), (96, 64)):
                    last = act.activation(swap[to:to + 32, b, :], PS[of:of + 32, bank, :], ACT.Copy)
                last.then_inc(swap_ready, 1)

            def q_high(n, out, src, scale, ready):
                act.wait_ge(ready, n + 1)
                act.activation(out, src, ACT.Copy, scale=scale).then_inc(qhi_ready, 1)

            def exps(kind, j, qb, s):
                n = SC0[kind] + 8 * j + 2 * qb + s
                nb = TB if kind == 1 else band(kind, qb)[1]
                pr = prob3 if kind == 3 else prob
                act.wait_ge(max_ready, n + 1)
                if kind == 1 and 4 * j + qb >= 2:
                    act.wait_ge(trans_done, 4 * j + qb - 1)
                elif kind > 1:
                    act.wait_ge(trans_done, PB0[kind] + 8 * j + 2 * qb + s - 3)
                act.activation(pr[:, 2 * (qb % 2) + s, 0:nb * P], PS[:, 4 + n % 2, 0:nb * P], ACT.Exp,
                               bias=nmax[:, n % 4:n % 4 + 1], accum_out=rsum[:, n % 4:n % 4 + 1])\
                   .then_inc(exp_ready, 1)

            def sink_exps(j, qb):
                for s in range(2):
                    n = SC0[2] + 8 * j + 2 * qb + s
                    head = (j if j < 4 else j + 4) + 4 * s
                    last = act.activation(rsum[:, 4 + n % 4:5 + n % 4], cpar("sinks", head), ACT.Exp,
                                          bias=nmax[:, n % 4:n % 4 + 1])
                last.then_inc(sink_ready, 1)

            def prob_high(n, out, blocks, free):
                act.wait_ge(trans_done, n + 1)
                if free:
                    act.wait_ge(pv_done, free)
                act.activation(out, PS[:, 6, 0:blocks * P].rearrange("p (k q) -> p k q", k=blocks)
                               if len(out.shape) == 3 else PS[:, 6, 0:blocks * P], ACT.Copy)\
                   .then_inc(pthi_ready, 1)

            def evacuate(n, count, out):
                act.wait_ge(pv_done, count)
                act.activation(out, PS[:, 7, :], ACT.Copy).then_inc(o_ready, 1)

            def band_attention(kind, j):
                def between(qb):
                    if j + 1 == PAIRS[kind]:
                        return
                    if kind == 2 and qb == 0:
                        swap_halves("q2", j + 1, QT0[2] + 2 + j + 1, (j + 1) % 2)
                    if kind == 2 and qb == 2:
                        q_high(QT0[2] + 2 + j + 1, qkhi[:, (j + 1) % 2, 0, :],
                               qraw[:, (j + 1) % 2, :], QSCALE, rope_ready)
                    if kind == 3 and qb < 2:
                        head_norm(2 * (j + 1) + qb)
                    if kind == 3 and qb == 2:
                        for u in range(2):
                            head_high(2 * (j + 1) + u)

                def highs(qb):
                    nb = band(kind, qb)[1]
                    for s in range(2):
                        n = PB0[kind] + 8 * j + 2 * qb + s
                        at = 2 * (qb % 2) + s
                        done = PVQ[kind] + 4 * j + qb - 1
                        prob_high(n, pthi[:, at, 0:nb * P], nb, done)
                for s in range(2):
                    exps(kind, j, 0, s)
                if kind == 2:
                    sink_exps(j, 0)
                for qb in range(TB):
                    if qb + 1 < TB:
                        for s in range(2):
                            exps(kind, j, qb + 1, s)
                        if kind == 2:
                            sink_exps(j, qb + 1)
                    between(qb)
                    highs(qb)
                evacuate(j, PVQ[kind] + 4 * j + 4, (OA if kind == 2 else OA3)[:, j, :])

            PVQ = {2: 8, 3: 8 + 32}

            def output_high(kind, n, buf, src):
                for c in range(n):
                    act.activation(buf(c), src[:, c, :], ACT.Copy).then_inc(ohi_ready, 1)

            def feed_forward(l, last=False):
                root(f"ffn{l}")
                n0 = l * FC
                for p, n in enumerate(PARTS):
                    stage = f"up{l}.{p}"

                    def body(i):
                        for pair in range(2):
                            q = PART0[p] + 2 * i + pair
                            for u in range(2):
                                used(stage, i, 2 * pair + u)
                                if l < 2:
                                    freed(stage, i, 2 * pair + u)
                                    act.activation(cv[:, 2 * pair + u, :], us[:, 2 * pair + u, :],
                                                   ACT.Identity, scale=conv_w[:, l, 1, u, bass.ds(q, 1)],
                                                   bias=conv_w[:, l, 3, u, bass.ds(q, 1)])\
                                       .then_inc(mid_ready, 1)
                            if l < 2:
                                act.wait_ge(conv_done, 2 * (n0 + q) + 1)
                                src = cv
                            else:
                                freed(stage, i, 2 * pair)
                                src = us
                            act.activation(us[:, 2 * pair, :] if l < 2 else cv[:, 2 * pair, :],
                                           src[:, 2 * pair, :], ACT.Silu).then_inc(silu_ready, 1)
                            act.wait_ge(act_ready, n0 + q + 1)
                            act.activation(chunks(Bhi[ABUF[l]])[:, 2 * i + pair, :], av[:, pair, :],
                                           ACT.Copy).then_inc(ahi_ready, 1)
                    rounds(n // 2, body)
                    norm = {0: "ple0", 1: "ple1", 2: None}[l] if p == 2 else None
                    residual(f"down{l}.{p}", norm, last=(l == 2 and p == 2))

            def embedding(l, nxt):
                for k in range(2):
                    act.activation(qkhi[:, 0, k, :], PT[:, k, :], ACT.Copy).then_inc(phi_ready, 1)
                for q in range(2):
                    used(f"pp{l}", 0, q)
                    for m in range(4):
                        bank, _ = tile_of(f"pp{l}", 0, 4 * q + m)
                        act.activation(pp[:, 4 * q + m, :], PS[:, bank, :], ACT.Copy)\
                           .then_inc(tile_free[bank], 1)
                root(f"ple{l}")
                act.wait_ge(r_ready, NORMS.index(nxt))

                def body(i):
                    for j in range(4):
                        m = 4 * i + j
                        used(f"gate{l}", i, j)
                        freed(f"gate{l}", i, j)
                        act.activation(gt[:, j % 2, :], gt[:, j % 2, :], ACT.Sigmoid)\
                           .then_inc(sig_ready, 1)
                        act.wait_ge(ple_added, KC * l + m + 1)
                        square_and_high.slot = j % 2
                        square_and_high(nxt, m)
                rounds(2, body)

            def fetch_p(l):
                act.dma_start(PT, pT[l]).then_inc(p_in, 16)

            act.dma_start(par_sb[:, :], par).then_inc(par_in, 16)
            act.dma_start(con_sb[:, :], con).then_inc(par_in, 16)
            act.dma_start(AR[:, 4096:4096 + 256], lamd).then_inc(par_in, 16)
            act.dma_start(AR[:, 0:T].bitcast(I32), posd).then_inc(pos_in, 16)
            act.dma_start(X[:, :, :], xT).then_inc(x_in, 16)
            for s in range(RING):
                high(s, s, s // RAWS)
            act.wait_ge(par_in, 48)
            act.wait_ge(x_in, 16)
            for m in range(KC):
                square_and_high.slot = m % 2
                square_and_high("attn0", m)
            act.wait_ge(consts_ready, 4)
            act.activation(sinT[:, :], angs[:, 1, :], ACT.Sin).then_inc(trig_ready, 1)
            act.activation(cosT[:, :], angs[:, 2, :], ACT.Sin).then_inc(trig_ready, 1)
            act.activation(lam[:, 2:4], lam[:, 0:2], ACT.Exp).then_inc(trig_ready, 1)
            root("attn0")
            values("v1", 2, 4, T)
            for u in range(2):
                swap_halves("qk1", u, u, u)
            for u in range(2):
                q_high(u, qkhi[:, 0, u, :], qraw[:, u, :], (QSCALE, 1.0)[u], rope_ready)
            for h in range(8):
                for s in range(2):
                    exps(1, h, 0, s)
                for qb in range(TB):
                    if qb + 1 < TB:
                        for s in range(2):
                            exps(1, h, qb + 1, s)
                    if h < 7 and qb < 2:
                        swap_halves("qk1", 2 * h + 2 + qb, 2 * h + 2 + qb, qb)
                    if h < 7 and qb == 2:
                        for u in range(2):
                            q_high(2 * h + 2 + u, qkhi[:, (h + 1) % 2, u, :], qraw[:, u, :],
                                   (QSCALE, 1.0)[u], rope_ready)
                    prob_high(4 * h + qb, pthi[:, :, qb * P:qb * P + P], TB, h)
                evacuate(h, h + 1, OA[:, h, :])
            for h in range(8):
                if h >= 2:
                    act.wait_ge(osum_done, h - 1)
                else:
                    act.wait_ge(o_ready, 8)
                act.activation(sq[:, h % 2, :], OA[:, h, :], ACT.Square).then_inc(osq_ready, 1)
            act.wait_ge(osum_done, 8)
            act.activation(sq[0:8, 0, :], PS[0:8, 4, :], ACT.Sqrt, scale=1.0 / P, bias=eps[0:8, 0:1])\
               .then_inc(oroot_ready, 1)
            for h in range(8):
                act.wait_ge(onorm_ready, h + 1)
                act.activation(chunks(Bhi[1])[:, h, :], OA[:, h, :], ACT.Copy, scale=gs[:, 0:1])\
                   .then_inc(ohi_ready, 1)
            residual("o1", "ffn0")
            fetch_p(0)
            feed_forward(0)
            act.wait_ge(p_in, 16)
            embedding(0, "attn1")
            root("attn1")
            values("v2", 1, 2, 256)
            for u in range(2):
                swap_halves("k2", u, QT0[2] + u, u)
            for u in range(2):
                q_high(QT0[2] + u, qkhi[:, u, 1, :], qraw[:, u, :], 1.0, rope_ready)
            swap_halves("q2", 0, QT0[2] + 2, 0)
            q_high(QT0[2] + 2, qkhi[:, 0, 0, :], qraw[:, 0, :], QSCALE, rope_ready)
            for j in range(8):
                band_attention(2, j)
            act.wait_ge(o_ready, 16)
            output_high(2, 8, lambda c: chunks(Bhi[0])[:, c, :], OA)
            residual("o2", "ffn1")
            fetch_p(1)
            feed_forward(1)
            act.wait_ge(p_in, 32)
            embedding(1, "final")
            root("final")
            for m in range(KC):
                act.wait_ge(y_ready, m + 1)
                square_and_high.slot = (m + 1) % 2
                square_and_high("mix", m)
            for q in range(4):
                for u in range(2):
                    used("a3", 0, 2 * q + u)
                if q == 0:
                    root("mix")
                freed("a3", 0, 2 * q + 1)
                act.activation(atmp[:, 2, :], atmp[:, 1, :], ACT.Sigmoid).then_inc(asig_ready, 1)
            for m in range(8):
                used("ga3", 0, m)
                freed("ga3", 0, m)
                act.activation(G[:, m, :], t3[:, m % 2, :], ACT.Sigmoid).then_inc(sig_ready, 1)
            values("v3", 1, 4, T)
            act.activation(wfhi[:, :], cpar("w_f", 0, KC * 8), ACT.Copy).then_inc(phi_ready, 1)
            for c in range(CT):
                act.wait_ge(taps_done, c + 1)
                act.activation(cvo[:, c, :], PS[:, 4 + c, :], ACT.Copy).then_inc(cv_ready, 1)
            act.wait_ge(f_lin, 1)
            own.step(act.activation(fl[:, 1, :], fl[:, 0, :], ACT.Abs))
            own.wait()
            own.step(act.activation(fl[:, 1, :], fl[:, 1, :], ACT.Exp, scale=-1.0))
            own.wait()
            act.activation(fl[:, 1, :], fl[:, 1, :], ACT.Ln, bias=1.0).then_inc(f_exp, 1)
            for c in range(CT):
                act.wait_ge(cen_ready, c + 1)
                if c >= 2:
                    act.wait_ge(var_done, c - 1)
                act.activation(sq[:, c % 2, :], cvo[:, c, :], ACT.Square).then_inc(csq_ready, 1)
            act.wait_ge(var_done, CT)
            act.activation(t3[:, 0, :], PS[:, 6, :], ACT.Sqrt, scale=1.0 / CONV, bias=eps[:, 0:1])\
               .then_inc(croot_ready, 1)
            for c in range(CT):
                act.wait_ge(cn_ready, c + 1)
                own.step(act.activation(cvo[:, c, :], cvo[:, c, :], ACT.Silu,
                                        scale=cpar("g_ln", c), bias=cpar("b_ln", c)))
                own.wait()
                act.activation(pthi[:, c, :], cvo[:, c, :], ACT.Copy).then_inc(chi_ready, 1)
            act.wait_ge(cumT_done, 1)
            act.activation(cc[0:8, :], PS[0:8, 7, :], ACT.Copy).then_inc(cchi_ready, 1)
            for q in range(4):
                used("co3", 0, q)

            def head_norm(t):
                used("qk3", 0, t)
                act.wait_ge(rope_ready, QT0[3] + t + 1)
                if t >= 2:
                    act.wait_ge(hsum_done, t - 1)
                act.activation(sq[:, t % 2, :], qraw3[:, t % 2, :], ACT.Square).then_inc(hsq_ready, 1)
                bank, _ = tile_of("qk3", 0, t)
                act.wait_ge(hsum_done, t + 1)
                if t:
                    act.wait_ge(orinv_ready, 1 + t)
                act.activation(sinT[:, :], PS[:, bank, :], ACT.Sqrt, scale=1.0 / 64, bias=eps[:, 0:1])\
                   .then_inc(tile_free[bank], 1)

            def head_high(t):
                b, u = (t // 2) % 2, t % 2
                q_high(t, qkhi[:, b, u, :], qraw3[:, u, :], gs[:, 1 + u:2 + u], obc_n)

            obc_n = hroot_ready
            for t in range(2):
                head_norm(t)
            for t in range(2):
                head_high(t)
            for j in range(4):
                band_attention(3, j)
            act.wait_ge(o_ready, 20)
            output_high(3, 4, lambda c: pthi[:, c, :], OA3)
            for m in range(8):
                used("gb3", 0, m)
                freed("gb3", 0, m)
                act.activation(G2[:, m, :], t3[:, m % 2, :], ACT.Sigmoid).then_inc(sig_ready, 1)
            for m in range(8):
                if m % 2 == 0:
                    used("ao3", 0, m // 2)
                act.wait_ge(a_ready, CT + m + 1)
                act.activation(chunks(Bhi[1])[:, m, :], G[:, m, :], ACT.Copy).then_inc(chi_ready, 1)
            residual("out3", "ffn2")
            feed_forward(2)

        @block.vector
        def _(dve):
            own = Own(dve, dve_step)
            tt, stt, ts = dve.tensor_tensor, dve.scalar_tensor_tensor, dve.tensor_scalar

            def done(stage, i, j):
                dve.wait_ge(slab_done, slab_of(stage, i, j)[0] + 1)

            def scaled(out, stage, i, j):
                bank, _ = tile_of(stage, i, j)
                tt(out, PS[:, bank, :], R[:, :], ALU.mult).then_inc(tile_free[bank], 1)

            def add_and_low(norm, m, slot):
                n = NORMS.index(norm)
                c = KC * n + m
                dve.wait_ge(sq_ready, c + 1)
                tt(acc[:, :], acc[:, :], sq[:, slot, :], ALU.add).then_inc(sq_used, 1)
                dve.wait_ge(sq_used, c + 1)
                if norm in GAIN:
                    name, col = GAIN[norm]
                    k = KC * SPLITS.index(norm) + m
                    dve.wait_ge(xhi_ready, k + 1)
                    b = BUF[norm]
                    stt(chunks(Blo[b])[:, m, :], X[:, m, :], gain(name, col, m),
                        f32(chunks(Bhi[b])[:, m, :]), ALU.mult, ALU.subtract).then_inc(x_split, 1)

            def clear_sum():
                own.step(dve.memset(acc[:, :], 0.0))
                own.wait()

            def factor(norm):
                n = NORMS.index(norm)
                dve.wait_ge(root_ready, n + 1)
                dve.reciprocal(R[:, :], sq[:, 0, :]).then_inc(r_ready, 1)
                dve.wait_ge(r_ready, n + 1)

            def rounds(n, per, body):
                if n <= 2:
                    for i in range(n):
                        body(i)
                else:
                    own.rounds(0, n, per, body)

            def residual(stage, norm):
                if norm:
                    clear_sum()

                def body(i):
                    for j in range(4):
                        m = 4 * i + j
                        done(stage, i, j)
                        bank, before = tile_of(stage, i, j)
                        tt(X[:, m, :], X[:, m, :], PS[:, bank, :], ALU.add)\
                            .then_inc(tile_free[bank], 1)
                        if norm:
                            add_and_low(norm, m, j % 2)
                rounds(2, 0, body)

            def columns(n):
                dve.wait_ge(rcol_done, n)
                dve.tensor_copy(rcol[:, :], PS[:, 7, 0:TB]).then_inc(rcol_ready, 1)
                dve.wait_ge(rcol_ready, n)

            def values_low(stage, halves, width):
                n0 = {"v1": 0, "v2": 2 * TB, "v3": 3 * TB}[stage]
                for hf in range(halves):
                    for t in range(TB):
                        bank, _ = tile_of(stage, 0, hf * TB + t)
                        dve.wait_ge(vhi_ready, n0 + hf * TB + t + 1)
                        if stage == "v1":
                            v = [b[:, :].rearrange("p (k n) -> p k n", k=TB)[:, t, hf * T:hf * T + T]
                                 for b in (Blo[1], Bhi[1])]
                            parts = [(v[0], PS[:, bank, :], v[1])]
                        else:
                            lo = padded(stage, Blo, PS[:, bank, 0:width], t)
                            hi = padded(stage, Bhi, PS[:, bank, 0:width], t)
                            parts = [(a, s, b) for (a, s), (b, _) in zip(lo, hi)]
                        for q, (out, src, hi) in enumerate(parts):
                            ins = stt(out, src, rcol[:, t:t + 1], f32(hi), ALU.mult, ALU.subtract)
                            if q == 0 and len(parts) == 2:
                                own.step(ins)
                        ins.then_inc(tile_free[bank], 1)

            def zero_padding(stage):
                vb, nh = (0, 4) if stage == "v2" else (1, 8)
                for b in (Bhi[vb], Blo[vb]):
                    v = b[:, 0:TB * nh * P].rearrange("p (k two c) -> p k two c", two=2, c=P)
                    for u in range(2):
                        dve.memset(f32(v[:, :, u, 64 - 64 * u:P - 64 * u]), 0.0).then_inc(pad_ready, 1)

            def rope(stage, t, n, b):
                bank, before = tile_of(stage, 0, t)
                dve.wait_ge(swap_ready, n + 1)
                if n >= 2:
                    dve.wait_ge(q_ready, n - 1)
                    dve.wait_ge(qhi_ready, n - 1)
                tt(qraw[:, b, :], PS[:, bank, :], rC, ALU.mult).then_inc(tile_free[bank], 1)
                own.step(tt(swap[:, b, :], swap[:, b, :], rS, ALU.mult))
                own.wait()
                dve.wait_ge(tile_free[bank], before + 2)
                tt(qraw[:, b, :], qraw[:, b, :], swap[:, b, :], ALU.add).then_inc(rope_ready, 1)

            def q_low(n, lo, hi, src, scale, have=qhi_ready):
                dve.wait_ge(have, n + 1)
                stt(lo, src, scale, f32(hi), ALU.mult, ALU.subtract).then_inc(q_ready, 1)

            def maxima(kind, j, qb):
                for s in range(2):
                    n = SC0[kind] + 8 * j + 2 * qb + s
                    nb = TB if kind == 1 else band(kind, qb)[1]
                    dve.wait_ge(score_done, n + 1)
                    src, out = PS[:, 4 + n % 2, 0:nb * P], nmax[:, n % 4:n % 4 + 1]
                    if kind == 2:
                        head = (j if j < 4 else j + 4) + 4 * s
                        own.step(dve.tensor_reduce(nmax[:, 4 + n % 4:5 + n % 4], src, AX, ALU.max))
                        own.wait()
                        ts(out, nmax[:, 4 + n % 4:5 + n % 4], cpar("sinks", head), -1.0,
                           ALU.max, ALU.mult).then_inc(max_ready, 1)
                    else:
                        dve.tensor_reduce(out, src, AX, ALU.max, negate=True).then_inc(max_ready, 1)

            def combine1(h, qb):
                n = 8 * h + 2 * qb
                dve.wait_ge(exp_ready, n + 2)
                c = n % 4
                b = 2 * (qb % 2)
                own.step(dve.reciprocal(rinv[:, c:c + 2], rsum[:, c:c + 2]))
                own.wait()
                own.step(tt(rinv[:, c + 1:c + 2], rinv[:, c + 1:c + 2], lam[:, 5:6], ALU.mult))
                own.step(ts(prob[:, b, :], prob[:, b, :], rinv[:, c:c + 1], None, ALU.mult))
                own.wait()
                stt(prob[:, b + 1, :], prob[:, b + 1, :], rinv[:, c + 1:c + 2], prob[:, b, :],
                    ALU.mult, ALU.add).then_inc(prob_ready, 1)

            def normalise(kind, j, qb):
                n = SC0[kind] + 8 * j + 2 * qb
                nb = band(kind, qb)[1]
                pr = prob if kind == 2 else prob3
                c = n % 4
                dve.wait_ge(exp_ready, n + 2)
                if kind == 2:
                    dve.wait_ge(sink_ready, 4 * j + qb + 1)
                    own.step(tt(rsum[:, c:c + 2], rsum[:, c:c + 2], rsum[:, 4 + c:6 + c], ALU.add))
                    own.wait()
                own.step(dve.reciprocal(rinv[:, c:c + 2], rsum[:, c:c + 2]))
                own.wait()
                for s in range(2):
                    v = pr[:, 2 * (qb % 2) + s, 0:nb * P]
                    ts(v, v, rinv[:, c + s:c + s + 1], None, ALU.mult).then_inc(prob_ready, 1)

            def prob_low(n, lo, hi, blocks):
                dve.wait_ge(pthi_ready, n + 1)
                src = PS[:, 6, 0:blocks * P]
                if len(lo.shape) == 3:
                    src = src.rearrange("p (k q) -> p k q", k=blocks)
                tt(lo, src, f32(hi), ALU.subtract).then_inc(pt_ready, 1)

            def band_attention(kind, j):
                def between(qb):
                    if j + 1 == PAIRS[kind]:
                        return
                    b = (j + 1) % 2
                    if kind == 2 and qb == 0:
                        rope("q2", j + 1, QT0[2] + 2 + j + 1, b)
                    if kind == 2 and qb == 2:
                        q_low(QT0[2] + 2 + j + 1, qklo[:, b, 0, :], qkhi[:, b, 0, :],
                              qraw[:, b, :], QSCALE)
                    if kind == 3 and qb < 2:
                        head_norm(2 * (j + 1) + qb)
                    if kind == 3 and qb == 2:
                        for u in range(2):
                            head_low(2 * (j + 1) + u)

                def lows(qb):
                    nb = band(kind, qb)[1]
                    for s in range(2):
                        n = PB0[kind] + 8 * j + 2 * qb + s
                        at = 2 * (qb % 2) + s
                        prob_low(n, ptlo[:, at, 0:nb * P], pthi[:, at, 0:nb * P], nb)
                maxima(kind, j, 0)
                for qb in range(TB):
                    if qb + 1 < TB:
                        maxima(kind, j, qb + 1)
                    normalise(kind, j, qb)
                    between(qb)
                    lows(qb)

            def output_low(n0, n, lo, hi, src, scale):
                for c in range(n):
                    dve.wait_ge(ohi_ready, n0 + c + 1)
                    if scale is None:
                        tt(lo(c), src[:, c, :], f32(hi(c)), ALU.subtract).then_inc(o_split, 1)
                    else:
                        stt(lo(c), src[:, c, :], scale, f32(hi(c)), ALU.mult, ALU.subtract)\
                            .then_inc(o_split, 1)

            def feed_forward(l):
                factor(f"ffn{l}")
                n0 = l * FC
                for p, n in enumerate(PARTS):
                    stage = f"up{l}.{p}"

                    def body(i):
                        for pair in range(2):
                            q = PART0[p] + 2 * i + pair
                            for u in range(2):
                                done(stage, i, 2 * pair + u)
                                scaled(us[:, 2 * pair + u, :], stage, i, 2 * pair + u)
                            if l < 2:
                                for u in range(2):
                                    c, x = cv[:, 2 * pair + u, :], us[:, 2 * pair + u, :]
                                    dve.wait_ge(mid_ready, 2 * (n0 + q) + u + 1)
                                    own.step(stt(c[:, 1:T], x[:, 0:T - 1], conv_w[:, l, 0, u, bass.ds(q, 1)],
                                                 c[:, 1:T], ALU.mult, ALU.add))
                                    own.wait()
                                    stt(c[:, 0:T - 1], x[:, 1:T], conv_w[:, l, 2, u, bass.ds(q, 1)],
                                        c[:, 0:T - 1], ALU.mult, ALU.add).then_inc(conv_done, 1)
                                dve.wait_ge(conv_done, 2 * (n0 + q) + 2)
                            dve.wait_ge(silu_ready, n0 + q + 1)
                            if l < 2:
                                g, v = us[:, 2 * pair, :], cv[:, 2 * pair + 1, :]
                            else:
                                g, v = cv[:, 2 * pair, :], us[:, 2 * pair + 1, :]
                                bank, before = tile_of(stage, i, 2 * pair + 1)
                                dve.wait_ge(tile_free[bank], before + 2)
                            own.wait()
                            tt(av[:, pair, :], g, v, ALU.mult).then_inc(act_ready, 1)
                            dve.wait_ge(ahi_ready, n0 + q + 1)
                            k = 2 * i + pair
                            b = ABUF[l]
                            tt(chunks(Blo[b])[:, k, :], av[:, pair, :], f32(chunks(Bhi[b])[:, k, :]),
                               ALU.subtract).then_inc(act_split, 1)
                            dve.wait_ge(act_split, n0 + q + 1)
                    rounds(n // 2, 4 if l < 2 else 0, body)
                    norm = {0: "ple0", 1: "ple1", 2: None}[l] if p == 2 else None
                    residual(f"down{l}.{p}", norm)

            def embedding(l, nxt):
                for k in range(2):
                    dve.wait_ge(phi_ready, 2 * l + k + 1)
                    tt(qklo[:, 0, k, :], PT[:, k, :], f32(qkhi[:, 0, k, :]), ALU.subtract)\
                        .then_inc(p_split, 1)
                factor(f"ple{l}")
                clear_sum()

                def body(i):
                    for j in range(4):
                        m = 4 * i + j
                        done(f"gate{l}", i, j)
                        scaled(gt[:, j % 2, :], f"gate{l}", i, j)
                        dve.wait_ge(sig_ready, KC * l + m + 1)
                        own.step(tt(gu[:, j % 2, :], gt[:, j % 2, :], pp[:, m, :], ALU.mult))
                        own.wait()
                        tt(X[:, m, :], X[:, m, :], gu[:, j % 2, :], ALU.add).then_inc(ple_added, 1)
                        dve.wait_ge(ple_added, KC * l + m + 1)
                        add_and_low(nxt, m, j % 2)
                rounds(2, 0, body)

            for b in range(BANKS):
                dve.memset(credit[:, b:b + 1], 0.0).then_inc(tile_free[b], 1)
            own.step(dve.memset(f32(cc[:, :]), 0.0))
            dve.memset(eps[:, :], EPS).then_inc(consts_ready, 1)
            dve.wait_ge(par_in, 48)
            dve.tensor_copy(constR[:, :, :], con_sb[:, 0:3 * P].rearrange("p (n c) -> p n c", n=3))\
               .then_inc(consts_ready, 1)
            dve.tensor_copy(minusR[:, :, :], con_sb[:, CCOLS["minus"][0]:CCOLS["minus"][1]]
                            .rearrange("p (n c) -> p n c", c=1).broadcast_to((P, 8, P)))\
               .then_inc(consts_ready, 1)
            dve.wait_ge(consts_ready, 3)
            clear_sum()
            for m in range(KC):
                add_and_low("attn0", m, m % 2)
            dve.wait_ge(pos_in, 16)
            A = angs
            MAGIC = 1.5 * 2.0 ** 23
            own.step(dve.tensor_copy(A[:, 1, :], A[:, 0, :].bitcast(I32)))
            own.wait()
            own.step(ts(A[:, 1, :], A[:, 1, :], ccon("freq"), None, ALU.mult))
            own.wait()
            own.step(ts(A[:, 3, :], A[:, 1, :], 1.0 / (2 * np.pi), MAGIC, ALU.mult, ALU.add))
            own.wait()
            own.step(ts(A[:, 3, :], A[:, 3, :], MAGIC, None, ALU.subtract))
            own.wait()
            c1 = 6.28125
            c2 = float(np.float32(int((2 * np.pi - c1) * 2 ** 20) / 2 ** 20))
            c3 = 2 * np.pi - c1 - c2
            for c in (c1, c2, c3):
                own.step(stt(A[:, 1, :], A[:, 3, :], -c, A[:, 1, :], ALU.mult, ALU.add))
                own.wait()
            own.step(ts(A[:, 1, :], A[:, 1, :], float(np.float32(3.1415925)),
                        float(np.float32(-3.1415925)), ALU.min, ALU.max))
            own.wait()
            own.step(ts(A[:, 2, :], A[:, 1, :], -1.0, None, ALU.mult))
            own.wait()
            own.step(tt(A[:, 2, :], A[:, 1, :], A[:, 2, :], ALU.max))
            own.wait()
            own.step(ts(A[:, 2, :], A[:, 2, :], -1.0, np.pi / 2, ALU.mult, ALU.add))
            L = AR[:, 4096:4096 + 256].rearrange("p (a b c) -> p a b c", a=2, b=2)
            M = AR[:, 4608:4608 + 128].rearrange("p (a c) -> p a c", a=2)
            own.step(tt(M, L[:, :, 0, :], L[:, :, 1, :], ALU.mult))
            own.wait()
            dve.tensor_reduce(lam[:, 0:2], M, AX, ALU.add).then_inc(consts_ready, 1)
            dve.wait_ge(trig_ready, 3)
            own.step(tt(lam[:, 4:5], lam[:, 3:4], lam[:, 2:3], ALU.subtract))
            own.wait()
            own.step(ts(lam[:, 5:6], lam[:, 4:5], -LAM_INIT, None, ALU.add))
            own.step(ts(gs[:, 0:1], cpar("subln"), 1.0 - LAM_INIT, None, ALU.mult))
            own.step(ts(gs[:, 1:2], cpar("g_q"), QSCALE, None, ALU.mult))
            own.step(dve.tensor_copy(gs[:, 2:3], cpar("g_k")))
            own.step(ts(sinT[:, :], sinT[:, :], ccon("sign"), None, ALU.mult))
            own.wait()

            def rope_tables():
                own.step(tt(rC, cosT[:, :], R[:, :], ALU.mult))
                own.step(tt(rS, sinT[:, :], R[:, :], ALU.mult))
                own.wait()

            factor("attn0")
            rope_tables()
            columns(1)
            values_low("v1", 2, T)
            for u in range(2):
                rope("qk1", u, u, u)
            for u in range(2):
                q_low(u, qklo[:, 0, u, :], qkhi[:, 0, u, :], qraw[:, u, :], (QSCALE, 1.0)[u])
            for h in range(8):
                maxima(1, h, 0)
                for qb in range(TB):
                    if qb + 1 < TB:
                        maxima(1, h, qb + 1)
                    combine1(h, qb)
                    if h < 7 and qb < 2:
                        rope("qk1", 2 * h + 2 + qb, 2 * h + 2 + qb, qb)
                    if h < 7 and qb == 2:
                        for u in range(2):
                            b = (h + 1) % 2
                            q_low(2 * h + 2 + u, qklo[:, b, u, :], qkhi[:, b, u, :], qraw[:, u, :],
                                  (QSCALE, 1.0)[u])
                    prob_low(4 * h + qb, ptlo[:, :, qb * P:qb * P + P], pthi[:, :, qb * P:qb * P + P],
                             TB)
            dve.wait_ge(oroot_ready, 1)
            dve.reciprocal(acc[0:8, :], sq[0:8, 0, :]).then_inc(orinv_ready, 1)
            for h in range(8):
                dve.wait_ge(obc_done, h + 1)
                tt(OA[:, h, :], OA[:, h, :], PS[:, 5 + h % 2, :], ALU.mult).then_inc(onorm_ready, 1)
                if h:
                    dve.wait_ge(ohi_ready, h)
                    stt(chunks(Blo[1])[:, h - 1, :], OA[:, h - 1, :], gs[:, 0:1],
                        f32(chunks(Bhi[1])[:, h - 1, :]), ALU.mult, ALU.subtract).then_inc(o_split, 1)
            dve.wait_ge(ohi_ready, 8)
            stt(chunks(Blo[1])[:, 7, :], OA[:, 7, :], gs[:, 0:1], f32(chunks(Bhi[1])[:, 7, :]),
                ALU.mult, ALU.subtract).then_inc(o_split, 1)
            residual("o1", "ffn0")
            feed_forward(0)
            embedding(0, "attn1")
            zero_padding("v2")
            factor("attn1")
            rope_tables()
            columns(2)
            values_low("v2", 1, 256)
            for u in range(2):
                rope("k2", u, QT0[2] + u, u)
            for u in range(2):
                q_low(QT0[2] + u, qklo[:, u, 1, :], qkhi[:, u, 1, :], qraw[:, u, :], 1.0)
            rope("q2", 0, QT0[2] + 2, 0)
            q_low(QT0[2] + 2, qklo[:, 0, 0, :], qkhi[:, 0, 0, :], qraw[:, 0, :], QSCALE)
            for j in range(8):
                band_attention(2, j)
            output_low(8, 8, lambda c: chunks(Blo[0])[:, c, :], lambda c: chunks(Bhi[0])[:, c, :],
                       OA, None)
            residual("o2", "ffn1")
            feed_forward(1)
            embedding(1, "final")
            factor("final")
            clear_sum()
            for m in range(KC):
                stt(X[:, m, :], X[:, m, :], cpar("final_norm", m), R[:, :], ALU.mult, ALU.mult)\
                    .then_inc(y_ready, 1)
                if m:
                    add_and_low("mix", m - 1, m % 2)
            add_and_low("mix", KC - 1, KC % 2)
            own.step(dve.memset(apad[:, :, 0:TAPS - 1], 0.0))
            own.wait()
            queue = [(c, w) for c in range(CT) for w in range(TAPS)]

            def taps(n):
                for _ in range(min(n, len(queue))):
                    c, w = queue.pop(0)
                    src, out = apad[:, c, w:w + T], PS[:, 4 + c, :]
                    k = cpar("w_dw", w * CT + c)
                    own.wait()
                    if w == 0:
                        ins = ts(out, src, k, cpar("b_dw", c), ALU.mult, ALU.add)
                    else:
                        ins = stt(out, src, k, out, ALU.mult, ALU.add)
                    if w == TAPS - 1:
                        ins.then_inc(taps_done, 1)
                    else:
                        own.step(ins)

            for q in range(4):
                if q == 0:
                    factor("mix")
                for u in range(2):
                    done("a3", 0, 2 * q + u)
                    if u == 0 and q:
                        dve.wait_ge(a_ready, q)
                    scaled(atmp[:, u, :], "a3", 0, 2 * q + u)
                dve.wait_ge(asig_ready, q + 1)
                tt(apad[:, q, TAPS - 1:], atmp[:, 0, :], atmp[:, 2, :], ALU.mult).then_inc(a_ready, 1)
                dve.wait_ge(a_ready, q + 1)
                if q and q < 3:
                    taps(10 if q == 1 else 12)
            zero_padding("v3")
            for m in range(8):
                done("ga3", 0, m)
                if m >= 2:
                    dve.wait_ge(sig_ready, 2 * KC + m - 1)
                scaled(t3[:, m % 2, :], "ga3", 0, m)
                if m < 7:
                    taps(8)
            columns(3)
            taps(len(queue))
            values_low("v3", 1, T)
            dve.wait_ge(phi_ready, 5)
            tt(wflo[:, :], cpar("w_f", 0, KC * 8), f32(wfhi[:, :]), ALU.subtract).then_inc(p_split, 1)
            dve.wait_ge(f_done, 1)
            for t in range(TB):
                c = slice(8 * t, 8 * t + 8)
                own.step(stt(fl[:, 0, c], PS[:, 4, c], rcol[:, t:t + 1], cpar("b_forget", 0, 8),
                             ALU.mult, ALU.add))
            own.wait()
            ts(fl[:, 2, :], fl[:, 0, :], 0.0, None, ALU.min).then_inc(f_lin, 1)
            dve.wait_ge(f_lin, 1)
            dve.wait_ge(mean_done, 1)
            for c in range(CT):
                stt(cvo[:, c, :], PS[:, 5, :], -1.0 / CONV, cvo[:, c, :], ALU.mult, ALU.add)\
                    .then_inc(cen_ready, 1)
            dve.wait_ge(f_exp, 1)
            tt(fl[:, 2, :], fl[:, 2, :], fl[:, 1, :], ALU.subtract).then_inc(f_log, 1)
            dve.wait_ge(croot_ready, 1)
            own.step(dve.reciprocal(cosT[:, :], t3[:, 0, :]))
            own.wait()
            dve.wait_ge(cen_ready, CT)
            for c in range(CT):
                tt(cvo[:, c, :], cvo[:, c, :], cosT[:, :], ALU.mult).then_inc(cn_ready, 1)
            dve.wait_ge(cum_done, 1)
            dve.tensor_copy(fl[:, 3, :], PS[:, 7, 0:TB * 8]).then_inc(cum_ready, 1)
            for c in range(CT):
                dve.wait_ge(chi_ready, c + 1)
                tt(ptlo[:, c, :], cvo[:, c, :], f32(pthi[:, c, :]), ALU.subtract).then_inc(c_split, 1)
            dve.wait_ge(cchi_ready, 1)
            tt(cc[32:40, :], PS[0:8, 7, :], f32(cc[0:8, :]), ALU.subtract).then_inc(cc_ready, 1)
            dve.wait_ge(sig_ready, 3 * KC)
            for m in range(8):
                if m % 2 == 0:
                    done("co3", 0, m // 2)
                bank, _ = tile_of("co3", 0, m)
                tt(G[:, m, :], G[:, m, :], PS[:, bank, :], ALU.mult).then_inc(tile_free[bank], 1)

            def head_norm(t):
                done("qk3", 0, t)
                bank, before = tile_of("qk3", 0, t)
                if t >= 2:
                    dve.wait_ge(q_ready, QT0[3] + t - 1)
                tt(qraw3[:, t % 2, :], PS[:, bank, :], R[:, :], ALU.mult).then_inc(rope_ready, 1)
                dve.wait_ge(tile_free[bank], before + 2)
                if t:
                    dve.wait_ge(hroot_ready, t)
                dve.reciprocal(cosT[:, :], sinT[:, :]).then_inc(orinv_ready, 1)
                dve.wait_ge(orinv_ready, t + 2)
                dve.wait_ge(rope_ready, QT0[3] + t + 1)
                tt(qraw3[:, t % 2, :], qraw3[:, t % 2, :], cosT[:, :], ALU.mult).then_inc(hroot_ready, 1)

            def head_low(t):
                b, u = (t // 2) % 2, t % 2
                dve.wait_ge(hroot_ready, t + 1)
                q_low(QT0[3] + t, qklo[:, b, u, :], qkhi[:, b, u, :], qraw3[:, u, :],
                      gs[:, 1 + u:2 + u])

            for t in range(2):
                head_norm(t)
            for t in range(2):
                head_low(t)
            for j in range(4):
                band_attention(3, j)
            output_low(16, 4, lambda c: ptlo[:, c, :], lambda c: pthi[:, c, :], OA3, None)
            dve.wait_ge(o_split, 20)
            for m in range(8):
                done("gb3", 0, m)
                if m >= 2:
                    dve.wait_ge(sig_ready, 3 * KC + m - 1)
                scaled(t3[:, m % 2, :], "gb3", 0, m)
            dve.wait_ge(sig_ready, 4 * KC)
            for m in range(8):
                if m % 2 == 0:
                    done("ao3", 0, m // 2)
                bank, before = tile_of("ao3", 0, m)
                tt(G2[:, m, :], G2[:, m, :], PS[:, bank, :], ALU.mult).then_inc(tile_free[bank], 1)
                dve.wait_ge(tile_free[bank], before + 2)
                tt(G[:, m, :], G[:, m, :], G2[:, m, :], ALU.add).then_inc(a_ready, 1)
                dve.wait_ge(chi_ready, CT + m + 1)
                tt(chunks(Blo[1])[:, m, :], G[:, m, :], f32(chunks(Bhi[1])[:, m, :]), ALU.subtract)\
                    .then_inc(c_split, 1)
            residual("out3", "ffn2")
            feed_forward(2)


def slabs_of(inputs):
    out = np.empty((SLABS, P, D), np.float32)
    at = [0]

    def put(a):
        out[at[0]] = a.reshape(P, -1)
        at[0] += 1

    def tiles(w, cols, nk=KC, rows=None):
        w = w[:, cols] if rows is None else w[rows][:, cols]
        w = w.reshape(nk, P, P).transpose(1, 0, 2)
        s = np.zeros((P, KC, P), np.float32)
        s[:, :nk] = w
        put(s)

    def wide(w, cols, slabs):
        w = w[:, cols]
        kk = KC // slabs
        for q in range(slabs):
            put(w[q * kk * P:(q + 1) * kk * P].reshape(kk, P, -1).transpose(1, 0, 2))

    def group(w, nk, per):
        n = w.shape[1] // P
        v = w.reshape(nk, P, n, P).transpose(1, 2, 0, 3)
        for q in range(0, n, per):
            put(v[:, q:q + per])

    col = lambda m, base=0: slice(base + m * P, base + m * P + P)

    def feed(up, down):
        ff = FC * P
        for p, n in enumerate(PARTS):
            for c in range(PART0[p], PART0[p] + n):
                tiles(up, col(c))
                tiles(up, col(c, ff))
            for m in range(KC):
                tiles(down, col(m), n, slice(PART0[p] * P, (PART0[p] + n) * P))

    def layer_tail(l):
        feed(inputs["ffn_w_up"][l], inputs["ffn_w_down"][l])
        group(inputs["ple_w_proj"][l], 2, 4)
        for m in range(KC):
            tiles(inputs["ple_w_gate"][l], col(m))

    w = inputs["diff_w_qkv"][0]
    for hf in range(2):
        wide(w, slice(2 * D + hf * T, 2 * D + hf * T + T), 4)
    for h in range(8):
        tiles(w, col(h))
        tiles(w, col(h, D))
    for m in range(KC):
        tiles(inputs["diff_w_o"][0], col(m))
    layer_tail(0)
    pairs = [(j, j + 4) if j < 4 else (j + 4, j + 8) for j in range(8)]
    order = np.concatenate([np.arange(64) + 64 * h for pair in pairs for h in pair])
    w = inputs["swa_w_qkv"][0]
    wide(w, slice(1280, 1536), 2)
    for m in range(2):
        tiles(w, col(m, D))
    for m in range(8):
        tiles(w, order[m * P:m * P + P])
    for m in range(KC):
        tiles(inputs["swa_w_o"][0][order], col(m))
    layer_tail(1)
    w = inputs["w_in_2"][0]
    for c in range(CT):
        tiles(w, col(c))
        tiles(w, col(c, CONV))
    for m in range(KC):
        tiles(w, col(m, 2568))
    wide(w, slice(2048, 2560), 4)
    group(inputs["w_conv_out_2"][0], 4, 2)
    for j in range(4):
        tiles(w, col(j, 1024))
        tiles(w, col(j, 1536))
    for m in range(KC):
        tiles(w, col(m, 3592))
    group(inputs["w_attn_out_2"][0], 4, 2)
    for m in range(KC):
        tiles(inputs["w_out_2"][0], col(m))
    feed(inputs["w_ffn_in_2"][0], inputs["w_ffn_out_2"][0])
    assert at[0] == SLABS
    return out


def small_parameters(inputs):
    out = np.empty((P, NPAR), np.float32)

    def put(name, a):
        lo, hi = PCOLS[name]
        out[:, lo:hi] = a.reshape(P, hi - lo)

    def columns(v):
        return v.reshape(-1, P).T

    def spread(v):
        return np.broadcast_to(v.reshape(1, -1), (P, v.size))

    for name in ("attn_norm", "ffn_norm", "ple_norm", "final_norm"):
        put(name, columns(inputs[name]))
    put("g_mix", columns(inputs["g_mix_2"]))
    put("g_ffn", columns(inputs["g_ffn_2"]))
    put("subln", columns(inputs["diff_subln"]))
    cw = np.concatenate([inputs["ffn_conv_w"], inputs["ffn_conv_b"][:, None]], axis=1)
    put("conv_w", columns(cw))
    put("sinks", spread(inputs["swa_sinks"]))
    put("b_forget", spread(inputs["b_forget_2"]))
    put("w_dw", columns(inputs["w_dw_2"]))
    put("b_dw", columns(inputs["b_dw_2"]))
    put("g_ln", columns(inputs["g_conv_ln_2"]))
    put("b_ln", columns(inputs["b_conv_ln_2"]))
    put("g_q", np.concatenate([inputs["g_q_2"][0]] * 2)[:, None])
    put("g_k", np.concatenate([inputs["g_k_2"][0]] * 2)[:, None])
    put("w_f", inputs["w_in_2"][0][:, 2560:2568].reshape(KC, P, 8).transpose(1, 0, 2))
    return out


def kernel(**inputs):
    import concourse.bacc as _bacc
    from concourse.bass_utils import run_bass_kernel_spmd as _run

    inputs = {k: np.asarray(v) for k, v in inputs.items()}
    arrays = {
        "xT": np.ascontiguousarray(inputs["x"][0].T.reshape(KC, P, T).transpose(1, 0, 2)),
        "pT": np.ascontiguousarray(
            inputs["p"][:, 0].transpose(0, 2, 1).reshape(2, 2, P, T).transpose(0, 2, 1, 3)),
        "positions": np.ascontiguousarray(np.broadcast_to(inputs["positions"], (P, T))),
        "weights": slabs_of(inputs),
        "parameters": small_parameters(inputs),
        "constants": constants(),
        "lambdas": np.ascontiguousarray(
            np.broadcast_to(inputs["diff_lambda"].reshape(1, 256), (P, 256))),
    }
    nc = _bacc.Bacc("TRN2", target_bir_lowering=False, num_devices=1, dynamic_dma_scratch_size=4096)
    args = [nc.dram_tensor(f"in_{name}", a.shape, mybir.dt.from_np(a.dtype), kind="ExternalInput").ap()
            for name, a in arrays.items()]
    out = nc.dram_tensor("out_0", (P, KC, T), F32, kind="ExternalOutput").ap()
    build(nc, *args, out)
    r = _run(nc, [{f"in_{name}": a for name, a in arrays.items()}], core_ids=[0])
    got = r.results[0]["out_0"]
    return np.ascontiguousarray(got.transpose(2, 1, 0).reshape(1, T, D))
```

```python
from contextlib import ExitStack

import numpy as np

import concourse.bass as bass
from concourse import mybir

ALU = mybir.AluOpType
ACT = mybir.ActivationFunctionType
F32 = mybir.dt.float32
F32R = mybir.dt.float32r
I32 = mybir.dt.int32
AX = mybir.AxisListType.X

P = 128
T = 512
TB = T // P
D = 1024
KC = D // P
FC = 2816 // P
PARTS = (8, 8, 6)
PART0 = (0, 8, 16)
RING = 4
RAWS = 2
BANKS = 6
EPS = 1e-6
TAPS = 31
CONV = 512
CT = CONV // P
PADW = T + TAPS - 1
LAM_INIT = 0.8 - 0.6 * float(np.exp(-0.3 * 0))
QSCALE = 64.0 ** -0.5
NEG = -1e30

STAGES = [("qk1a", 2, 2), ("v1", 8, 8), ("qk1", 14, 14), ("o1", 8, 8)]
for _l in range(3):
    if _l == 1:
        STAGES += [("kq2a", 2, 2), ("v2", 2, 4), ("kq2", 8, 8), ("o2", 8, 8)]
    if _l == 2:
        STAGES += [("a3", 8, 8), ("v3", 4, 4), ("qk3", 8, 8), ("gb3", 8, 8), ("ao3", 4, 8),
                   ("gc3", 12, 16), ("out3", 8, 8)]
    for _p, _n in enumerate(PARTS):
        STAGES += [(f"up{_l}.{_p}", 2 * _n, 2 * _n), (f"down{_l}.{_p}", 8, 8)]
    if _l < 2:
        STAGES += [(f"pp{_l}", 2, 8), (f"gate{_l}", 8, 8)]
STAGE_BANKS = {"qk1a": (4, 5), "kq2a": (4, 5), "qk1": (0, 1), "kq2": (0, 1), "qk3": (0, 1),
               "a3": (0, 1, 2, 3, 4, 5)}
SLAB0, BEFORE = {}, {}
_s, _count = 0, [0] * BANKS
for _name, _ns, _nt in STAGES:
    SLAB0[_name] = _s
    BEFORE[_name] = tuple(_count)
    _s = _s + _ns
    _banks = STAGE_BANKS.get(_name, (0, 1, 2, 3))
    for _t in range(_nt):
        _count[_banks[_t % len(_banks)]] += 1
SLABS = _s
assert SLABS % RING == 0

PCOLS = {}
_c = 0
for _name, _n in (("attn_norm", 16), ("ffn_norm", 16), ("ple_norm", 16), ("final_norm", 8),
                  ("g_mix", 8), ("g_ffn", 8), ("subln", 1), ("conv_w", 2 * 4 * 2 * FC),
                  ("sinks", 16), ("b_forget", 8), ("w_dw", TAPS * CT), ("b_dw", CT),
                  ("g_ln", CT), ("b_ln", CT), ("g_q", 1), ("g_k", 1), ("w_f", KC * 8)):
    PCOLS[_name] = (_c, _c + _n)
    _c += _n
NPAR = _c
CCOLS = {}
_c = 0
for _name, _n in (("ident", P), ("before", P), ("after", P), ("ones", P), ("heads", P), ("upto", P),
                  ("pick", 16), ("minus", 8), ("freq", 1), ("sign", 1), ("lam", 0)):
    CCOLS[_name] = (_c, _c + _n)
    _c += _n
NCON = _c


def constants():
    c = np.zeros((P, NCON), np.float32)
    i = np.arange(P)

    def put(name, a):
        c[:, CCOLS[name][0]:CCOLS[name][1]] = a

    put("ident", np.eye(P))
    put("before", np.where(i[None, :] >= i[:, None], 0, NEG))
    put("after", np.where(i[None, :] <= i[:, None], 0, NEG))
    put("ones", 1)
    put("heads", i[:, None] // 64 == i[None, :] // 64)
    put("upto", i[:, None] <= i[None, :])
    put("pick", np.arange(16)[None, :] == 7)
    minus = np.zeros((P, 8))
    for h in range(8):
        minus[h, h] = minus[32 + h, h] = -1
    put("minus", minus)
    inv = np.float32(10000.0) ** (-np.arange(0, 64, 2, dtype=np.float32) / np.float32(64))
    put("freq", inv.astype(np.float32)[i % 32][:, None])
    put("sign", np.where(i % 64 < 32, -1, 1)[:, None])
    return c


class Own:

    def __init__(self, eng, sem):
        self.eng, self.sem, self.n = eng, sem, 0

    def step(self, ins):
        ins.then_inc(self.sem, 1)
        self.n = self.n + 1

    def wait(self):
        self.eng.wait_ge(self.sem, self.n)

    def rounds(self, first, end, per, body):
        base = self.n
        if end - first == 1:
            body(first)
        else:
            with self.eng.Fori(first, end) as i:
                self.n = base + (i - first) * per if per else base
                body(i)
        self.n = base + (end - first) * per


def slab_of(stage, i, j):
    s = SLAB0[stage] + j
    return s + 4 * i, s % RING, s // RAWS + (4 // RAWS) * i


def tile_of(stage, i, j):
    banks = STAGE_BANKS.get(stage, (0, 1, 2, 3))
    bank = banks[j % len(banks)]
    return bank, BEFORE[stage][bank] + j // len(banks) + i * (4 // len(banks))


def build(nc, xT, pT, posd, wts, par, con, lamd, outT):
    ctx = ExitStack()
    with ctx:
        def sb(name, shape, dt=F32):
            return ctx.enter_context(nc.sbuf_tensor(name, shape, dt))

        def sem(name):
            return ctx.enter_context(nc.semaphore(name))

        raw = sb("raw", [P, RAWS, D])
        whi = sb("whi", [P, RING, D], F32R)
        wlo = sb("wlo", [P, RING, D], F32R)
        X = sb("X", [P, KC, T])
        Bhi = [sb(f"Bhi{n}", [P, KC * T], F32R) for n in range(2)]
        Blo = [sb(f"Blo{n}", [P, KC * T], F32R) for n in range(2)]
        qkhi = sb("qkhi", [P, 2, 2, T], F32R)
        qklo = sb("qklo", [P, 2, 2, T], F32R)
        pthi = sb("pthi", [P, 4, T], F32R)
        ptlo = sb("ptlo", [P, 4, T], F32R)
        R = sb("R", [P, T])
        acc = sb("acc", [P, T])
        sq = sb("sq", [P, 2, T])
        cosT = sb("cosT", [P, T])
        sinT = sb("sinT", [P, T])
        AR = sb("AR", [P, 9344])
        par_sb = sb("par_sb", [P, NPAR])
        con_sb = sb("con_sb", [P, NCON])
        constR = sb("constR", [P, 3, P], F32R)
        minusR = sb("minusR", [P, 8, P], F32R)
        cc = sb("cc", [P, T], F32R)
        wfhi = sb("wfhi", [P, KC * 8], F32R)
        wflo = sb("wflo", [P, KC * 8], F32R)
        nmax = sb("nmax", [P, 8])
        rsum = sb("rsum", [P, 8])
        rinv = sb("rinv", [P, 8])
        rcol = sb("rcol", [P, TB])
        lam = sb("lam", [P, 8])
        gs = sb("gs", [P, 4])
        fl = sb("fl", [P, 4, TB * 8])
        eps = sb("eps", [P, 1])
        gfm = sb("gfm", [P, KC])
        credit = sb("credit", [P, BANKS + 2])
        PS = ctx.enter_context(nc.psum_tensor("PS", [P, 8, T], F32))

        def chunks(b):
            return b[:, :].rearrange("p (k t) -> p k t", k=KC)

        def ar(off, n=1):
            v = AR[:, off:off + n * T]
            return v.rearrange("p (n t) -> p n t", n=n)

        def cpar(name, k=0, n=1):
            o = PCOLS[name][0]
            return par_sb[:, o + k:o + k + n]

        def gain(name, col, m):
            if name == "both":
                return gfm[:, bass.ds(m, 1)]
            return par_sb[:, bass.ds(PCOLS[name][0] + col + m, 1)]

        def ccon(name, a=0, b=None):
            o, e = CCOLS[name]
            return con_sb[:, o + a:(e if b is None else o + b)]

        def f32(a):
            return a.bitcast(F32)

        conv_w = par_sb[:, PCOLS["conv_w"][0]:PCOLS["conv_w"][1]]\
            .rearrange("p (l t u c) -> p l t u c", l=2, t=4, u=2)
        identR, beforeR, afterR = constR[:, 0, :], constR[:, 1, :], constR[:, 2, :]
        ident = f32(identR)
        ones = ccon("ones")

        rC, rS = ar(0)[:, 0, :], ar(512)[:, 0, :]
        swap, qraw = ar(1024, 2), ar(2048, 2)
        prob = ar(3072, 4)
        OA = ar(5120, 8)
        us, cv, av = ar(0, 4), ar(2048, 4), ar(4096, 2)
        PT = ar(8192, 2)
        gt, gu, pp = ar(0, 2), ar(1024, 2), ar(4096, 8)
        atmp, prob3, qraw3, OA3 = ar(0, 3), ar(0, 4), ar(2048, 2), ar(3072, 4)
        G, t3 = ar(0, 8), ar(4096, 2)
        apad = AR[:, 5120:5120 + CT * PADW].rearrange("p (c t) -> p c t", c=CT)
        cvo = ar(7296, 4)
        angs = ar(0, 6)

        raw_ready = [sem(f"raw_ready{n}") for n in range(RAWS)]
        hi_ready = sem("hi_ready")
        lo_ready = sem("lo_ready")
        slab_done = sem("slab_done")
        tile_free = [sem(f"tile_free{n}") for n in range(BANKS)]
        par_in, con_in, pos_in, lam_in, p_in = (
            sem("par_in"), sem("con_in"), sem("pos_in"), sem("lam_in"), sem("p_in"))
        x_in = [sem(f"x_in{n}") for n in range(4)]
        consts_ready = sem("consts_ready")
        trig_ready = sem("trig_ready")
        sq_ready, sq_used = sem("sq_ready"), sem("sq_used")
        xhi_ready, x_split = sem("xhi_ready"), sem("x_split")
        ss_done, root_ready, r_ready = sem("ss_done"), sem("root_ready"), sem("r_ready")
        rcol_done, rcol_ready = sem("rcol_done"), sem("rcol_ready")
        vhi_ready, pad_ready = sem("vhi_ready"), sem("pad_ready")
        swap_ready, rope_ready, qhi_ready, q_ready = (
            sem("swap_ready"), sem("rope_ready"), sem("qhi_ready"), sem("q_ready"))
        score_done, max_ready, exp_ready, prob_ready = (
            sem("score_done"), sem("max_ready"), sem("exp_ready"), sem("prob_ready"))
        trans_done, pthi_ready, pt_ready, pv_done, o_ready = (
            sem("trans_done"), sem("pthi_ready"), sem("pt_ready"), sem("pv_done"), sem("o_ready"))
        osq_ready, osum_done, oroot_ready, orinv_ready = (
            sem("osq_ready"), sem("osum_done"), sem("oroot_ready"), sem("orinv_ready"))
        obc_done, onorm_ready, ohi_ready, o_split = (
            sem("obc_done"), sem("onorm_ready"), sem("ohi_ready"), sem("o_split"))
        mid_ready, conv_done, silu_ready, act_ready, ahi_ready, act_split = (
            sem("mid_ready"), sem("conv_done"), sem("silu_ready"), sem("act_ready"),
            sem("ahi_ready"), sem("act_split"))
        phi_ready, p_split, pp_ready = sem("phi_ready"), sem("p_split"), sem("pp_ready")
        sig_ready, sink_ready = sem("sig_ready"), sem("sink_ready")
        ple_added = sem("ple_added")
        y_ready = sem("y_ready")
        asig_ready, a_ready, taps_done, cv_ready = (
            sem("asig_ready"), sem("a_ready"), sem("taps_done"), sem("cv_ready"))
        mean_done, cen_ready, csq_ready, var_done, croot_ready, cn_ready, cs_ready = (
            sem("mean_done"), sem("cen_ready"), sem("csq_ready"), sem("var_done"),
            sem("croot_ready"), sem("cn_ready"), sem("cs_ready"))
        chi_ready, c_split = sem("chi_ready"), sem("c_split")
        f_done, f_lin, f_exp, f_log, cum_done, cum_ready, cumT_done, cchi_ready, cc_ready = (
            sem("f_done"), sem("f_lin"), sem("f_exp"), sem("f_log"), sem("cum_done"),
            sem("cum_ready"), sem("cumT_done"), sem("cchi_ready"), sem("cc_ready"))
        hsum_done, hsq_ready, hroot_ready = sem("hsum_done"), sem("hsq_ready"), sem("hroot_ready")
        dve_tap = [sem(f"dve_tap{c}") for c in range(CT)]
        dve_step, act_step = sem("dve_step"), sem("act_step")
        out_stored = sem("out_stored")
        block = ctx.enter_context(nc.Block())

        NORMS = ["attn0", "ffn0", "ple0", "attn1", "ffn1", "ple1", "final", "mix", "ffn2"]
        SPLITS = [n for n in NORMS if n != "mix"]
        GAIN = {"attn0": ("attn_norm", 0), "attn1": ("attn_norm", 8), "ffn0": ("ffn_norm", 0),
                "ffn1": ("ffn_norm", 8), "ple0": ("ple_norm", 0), "ple1": ("ple_norm", 8),
                "final": ("both", 0), "ffn2": ("g_ffn", 0)}
        BUF = {"attn0": 0, "ffn0": 1, "ple0": 1, "attn1": 0, "ffn1": 1, "ple1": 1, "final": 0, "ffn2": 0}
        TAPS_A_STEP = 2
        ABUF = {0: 0, 1: 0, 2: 1}

        PAIRS = {1: 8, 2: 8, 3: 4}

        def padded(stage, B, src, t):
            nh = 4 if stage == "v2" else 8
            v = B[1][:, 0:TB * nh * P].rearrange("p (k n c) -> p k n c", k=TB, n=nh)[:, t]
            v = v.rearrange("p (n two) c -> p n two c", two=2)
            s = src.rearrange("p (n two c) -> p n two c", two=2, c=64)
            return [(v[:, :, u, 64 * u:64 * u + 64], s[:, :, u, :]) for u in range(2)]

        def band(kind, qb):
            if kind == 1:
                return 0, TB, []
            if kind == 2:
                lo, hi = max(qb - 1, 0), min(qb + 1, TB - 1)
                masks = [(qb - 1 - lo, beforeR)] * (qb > 0) + [(qb + 1 - lo, afterR)] * (qb < TB - 1)
                return lo, hi - lo + 1, masks
            return 0, qb + 1, [(qb, afterR)]

        SC0 = {1: 0, 2: 64, 3: 128}
        PB0 = {1: 0, 2: 32, 3: 96}
        PV0 = {1: 0, 2: 32, 3: 64}
        OP0 = {1: 0, 2: 8, 3: 16}
        QT0 = {1: 0, 2: 16, 3: 26}

        PIECE = {
            1: lambda g: (2 * (g // 4) + (1, 1, 2, 2)[g % 4], g % 2, 2),
            2: lambda g: (g // 4 + (1, 1, 2, 2)[g % 4], (2, 3, 0, 1)[g % 4], 4),
            3: lambda g: (2 * ((g + 3) // 4) + 2 + ((g + 3) % 4 >= 2), (g + 1) % 2, 2)}
        PROJ = {1: "qk1", 2: "kq2", 3: "qk3"}
        HP = {1: 1, 2: 2, 3: 2}
        OFIRST = 6
        SPREAD = {28: (0, 1), 29: (2, 3), 30: (4, 5)}
        OSPLIT = {29: (0, 1, 2), 30: (3, 4), 31: (5, 6)}
        BEGUN = {1: {-1: 0}, 2: {-1: 0}, 3: {-2: 2}}
        NPROJ = {1: 14, 2: 8, 3: 8}

        def piece(kind, g):
            t, part, parts = PIECE[kind](g)
            return (t, part, parts) if t < NPROJ[kind] else None

        def score_bank(kind, n):
            return 4 + n % 2 if kind == 1 else 4 + (n - SC0[kind]) % 3

        def spread_bank(h):
            return h % 2 + (0 if h < OFIRST else 4)

        def finished(kind, g):
            if g < 0:
                return BEGUN[kind].get(g)
            p = piece(kind, g)
            return p[0] if p and p[1] == p[2] - 1 else None

        def probs(kind):
            return prob3 if kind == 3 else prob

        def place_of(kind, t):
            if kind == 1:
                return t + 2, (t // 2 + 1) % 2, t % 2
            if kind == 2:
                return QT0[2] + 2 + t, t % 2 if t else 1, 0 if t else 1
            return QT0[3] + t, (t // 2) % 2, t % 2

        def head_of(j, s):
            return (j if j < 4 else j + 4) + 4 * s

        @block.sync
        def _(sp):
            def load(s, slot, freed):
                if freed is not None:
                    sp.wait_ge(lo_ready, freed)
                sp.dma_start(raw[:, slot, :], wts[s]).then_inc(raw_ready[slot], 16)

            for s in range(4):
                load(s, s % RAWS, s - 1 if s >= RAWS else None)
            with sp.Fori(1, SLABS // 4) as i:
                for j in range(4):
                    load(4 * i + j, j % RAWS, 4 * i + j - 1)
            for m in range(KC):
                bank, before = tile_of("down2.2", m // 4, m % 4)
                sp.wait_ge(tile_free[bank], before + 2)
                sp.dma_start(outT[:, m, :], X[:, m, :]).then_inc(out_stored, 16)
            sp.wait_ge(out_stored, 16 * KC)

        @block.gpsimd
        def _(pool):
            with pool.Fori(0, SLABS // 4) as i:
                for j in range(4):
                    pool.wait_ge(hi_ready, 4 * i + j + 1)
                    pool.tensor_tensor(wlo[:, j, :], raw[:, j % RAWS, :], f32(whi[:, j, :]),
                                       ALU.subtract).then_inc(lo_ready, 1)

        @block.tensor
        def _(pe):
            def mm(out, w, x, start, stop):
                return pe.matmul(out, w, x, start=start, stop=stop)

            def mm3(out, ahi, alo, bhi, blo, start, stop):
                mm(out, ahi, bhi, start, False)
                mm(out, ahi, blo, False, False)
                return mm(out, alo, bhi, False, stop)

            def weights(s):
                pe.wait_ge(lo_ready, s + 1)

            def open_tile(stage, i, j):
                bank, before = tile_of(stage, i, j)
                pe.wait_ge(tile_free[bank], before + 1)
                return PS[:, bank, :]

            def tile(stage, i, j, hi, lo, nk, ready=None):
                s, slot, _ = slab_of(stage, i, j)
                weights(s)
                out = open_tile(stage, i, j)
                for k in range(nk):
                    if ready is not None:
                        pe.wait_ge(ready[0], ready[1] + k + 1)
                    last = mm3(out, whi[:, slot, k * P:k * P + P], wlo[:, slot, k * P:k * P + P],
                               hi[:, k, :], lo[:, k, :], k == 0, k == nk - 1)
                last.then_inc(slab_done, 1)

            def norm_sum(norm):
                pe.wait_ge(sq_used, KC * (NORMS.index(norm) + 1))
                mm(PS[:, 7, :], ones, acc[:, :], True, True).then_inc(ss_done, 1)

            def tiles(stage, n, hi, lo, nk, ready, norm=None, lead=2, late=1,
                      meanwhile=None):
                if ready is None:
                    lead = 0
                outs = []
                for ks in (range(nk - late), range(nk - late, nk)):
                    for j in range(lead):
                        s, slot, _ = slab_of(stage, 0, j)
                        if len(outs) < lead:
                            weights(s)
                            outs.append(open_tile(stage, 0, j))
                        for k in ks:
                            if j == 0:
                                pe.wait_ge(ready[0], ready[1] + k + 1)
                            last = mm3(outs[j], whi[:, slot, k * P:k * P + P],
                                       wlo[:, slot, k * P:k * P + P],
                                       hi[:, k, :], lo[:, k, :], k == 0, k == nk - 1)
                        if ks[-1] == nk - 1:
                            last.then_inc(slab_done, 1)
                    if ks[0] == 0 and meanwhile:
                        meanwhile()
                if norm:
                    norm_sum(norm)
                for j in range(lead, 4):
                    tile(stage, 0, j, hi, lo, nk)
                if n > 8:
                    with pe.Fori(1, n // 4) as i:
                        for j in range(4):
                            tile(stage, i, j, hi, lo, nk)
                elif n > 4:
                    for j in range(4):
                        tile(stage, 1, j, hi, lo, nk)

            def split_of(norm):
                b = BUF[norm]
                return chunks(Bhi[b]), chunks(Blo[b]), (x_split, KC * SPLITS.index(norm))

            def values(stage, norm, halves, slabs, width):
                hi, lo, _ = split_of(norm)
                kk = KC // slabs
                for hf in range(halves):
                    for q in range(slabs):
                        s, slot, _ = slab_of(stage, 0, hf * slabs + q)
                        weights(s)
                        for t in range(TB):
                            if q == 0:
                                open_tile(stage, 0, hf * TB + t)
                            out = PS[:, tile_of(stage, 0, hf * TB + t)[0], 0:width]
                            for k in range(q * kk, q * kk + kk):
                                c = (k - q * kk) * width
                                tk = slice(t * P, t * P + P)
                                w, v = whi[:, slot, c:c + width], wlo[:, slot, c:c + width]
                                last = mm3(out, hi[:, k, tk], lo[:, k, tk], w, v, k == 0, k == KC - 1)
                        last.then_inc(slab_done, 1)
                        if hf == 0 and q == 0 and stage == "v1":
                            norm_sum(norm)
                    if hf == 0 and stage != "v3":
                        row_to_column()

            def row_to_column():
                row_to_column.n += 1
                pe.wait_ge(r_ready, row_to_column.norms[row_to_column.n - 1] + 1)
                for t in range(TB):
                    last = mm(PS[:, 7, t:t + 1], R[0:1, t * P:t * P + P], ones[0:1, 0:1], True, True)
                last.then_inc(rcol_done, 1)
            row_to_column.n = 0
            row_to_column.norms = [NORMS.index(n) for n in ("attn0", "attn1", "mix")]

            def project_qk(stage, norm, t, part=0, parts=1):
                hi, lo, _ = split_of(norm)
                s, slot, _ = slab_of(stage, 0, t)
                out = PS[:, tile_of(stage, 0, t)[0], :]
                if part == 0:
                    weights(s)
                    open_tile(stage, 0, t)
                for k in range(part * KC // parts, (part + 1) * KC // parts):
                    last = mm3(out, whi[:, slot, k * P:k * P + P], wlo[:, slot, k * P:k * P + P],
                               hi[:, k, :], lo[:, k, :], k == 0, k == KC - 1)
                if part == parts - 1:
                    last.then_inc(slab_done, 1)

            def first_pair(stage, norm):
                hi, lo, ready = split_of(norm)
                for k in range(KC):
                    pe.wait_ge(ready[0], ready[1] + k + 1)
                    for t in range(2):
                        s, slot, _ = slab_of(stage, 0, t)
                        if k == 0:
                            weights(s)
                            open_tile(stage, 0, t)
                        c = slice(k * P, k * P + P)
                        last = mm3(PS[:, tile_of(stage, 0, t)[0], :], whi[:, slot, c],
                                   wlo[:, slot, c], hi[:, k, :], lo[:, k, :], k == 0, k == KC - 1)
                        if k == KC - 1:
                            last.then_inc(slab_done, 1)

            def all_values(stage, last):
                for t in (last - 1, last):
                    bank, before = tile_of(stage, 0, t)
                    pe.wait_ge(tile_free[bank], before + 2)

            def scores(kind, g):
                j, qb = g // 4, g % 4
                b = j % 2
                kb = j // 4 if kind == 2 else b
                first, nb, masks = band(kind, qb)
                if qb == 0:
                    pe.wait_ge(q_ready, QT0[kind] + {1: 2 * j + 2, 2: 2 if j == 0 else j + 3,
                                                     3: 2 * j + 2}[kind])
                    if kind == 3 and j == 0:
                        pe.wait_ge(cc_ready, 1)
                for s in range(2):
                    n = SC0[kind] + 2 * g + s
                    back = 2 if kind == 1 else 3
                    if n >= back:
                        pe.wait_ge(exp_ready, n - back + 1)
                    rows, cols = slice(64 * s, 64 * s + 64), slice(qb * P, qb * P + P)
                    keys = slice(first * P, (first + nb) * P)
                    out = PS[:, score_bank(kind, n), 0:nb * P]
                    last = mm3(out, qkhi[rows, b, 0, cols], qklo[rows, b, 0, cols],
                               qkhi[rows, kb, 1, keys], qklo[rows, kb, 1, keys], True, kind == 1)
                    if kind == 3:
                        mm(out, minusR[:, 2 * j + s, :], cc[:, keys], False, False)
                    for q, (at, mask) in enumerate(masks):
                        last = mm(out[:, at * P:at * P + P], identR, mask, False, q == len(masks) - 1)
                    last.then_inc(score_done, 1)

            def transposes(kind, g):
                nb = band(kind, g % 4)[1]
                if g == 0:
                    all_values(f"v{kind}", {1: 7, 2: 3, 3: 3}[kind])
                for s in range(HP[kind]):
                    n = PB0[kind] + HP[kind] * g + s
                    pe.wait_ge(prob_ready, n + 1)
                    if n >= 2:
                        pe.wait_ge(pt_ready, n - 1)
                    source = probs(kind)[:, 2 * (g % 2) + (1 if kind == 1 else s), :]
                    for k in range(nb):
                        last = pe.transpose(PS[:, 2 + n % 2, k * P:k * P + P],
                                            source[:, k * P:k * P + P], ident)
                    last.then_inc(trans_done, 1)

            def outputs(kind, g):
                j, qb = g // 4, g % 4
                first, nb, _ = band(kind, qb)
                heads = HP[kind]
                n = PB0[kind] + heads * g
                pe.wait_ge(pt_ready, n + heads)
                if qb == 0 and OP0[kind] + j:
                    pe.wait_ge(o_ready, OP0[kind] + j)
                nh = {1: 8, 2: 4, 3: 8}[kind]
                vhi = Bhi[1][:, 0:TB * nh * P].rearrange("p (k n c) -> p k n c", k=TB, n=nh)
                vlo = Blo[1][:, 0:TB * nh * P].rearrange("p (k n c) -> p k n c", k=TB, n=nh)
                for s in range(heads):
                    head = {1: j, 2: 2 * (j // 4) + s, 3: 2 * j + s}[kind]
                    at = (n + s) % 4
                    for k in range(nb):
                        last = mm3(PS[:, 7, qb * P:qb * P + P], vhi[:, first + k, head, :],
                                   vlo[:, first + k, head, :], pthi[:, at, k * P:k * P + P],
                                   ptlo[:, at, k * P:k * P + P], s == 0 and k == 0,
                                   s == heads - 1 and k == nb - 1)
                last.then_inc(pv_done, 1)

            def output_squares(h):
                if h == OFIRST:
                    pe.wait_ge(oroot_ready, 1)
                pe.wait_ge(osq_ready, h + 1)
                mm(PS[0:8, 6, :], ccon("pick", 7 - h, 15 - h), sq[:, h % 2, :],
                   h in (0, OFIRST), h in (OFIRST - 1, 7)).then_inc(osum_done, 1)

            def spread_factor(h):
                pe.wait_ge(orinv_ready, 1 if h < OFIRST else 2)
                if h >= 2:
                    pe.wait_ge(onorm_ready, h - 1)
                row = CCOLS["ident"][0] + h
                mm(PS[:, spread_bank(h), :], con_sb[0:8, row:row + 1].broadcast_to((8, P)),
                   (R if h < OFIRST else acc)[0:8, :], True, True).then_inc(obc_done, 1)

            def attention(kind, norm):
                steps = 4 * PAIRS[kind]
                scores(kind, 0)
                for g in range(steps):
                    if g + 1 < steps:
                        scores(kind, g + 1)
                    if piece(kind, g):
                        project_qk(PROJ[kind], norm, *piece(kind, g))
                    if kind == 1:
                        if g % 4 == 1 and g > 4:
                            output_squares(g // 4 - 1)
                        for h in SPREAD.get(g, ()):
                            spread_factor(h)
                    transposes(kind, g)
                    if g:
                        outputs(kind, g - 1)
                    if kind == 3 and finished(kind, g - 1) is not None:
                        head_sums(finished(kind, g - 1))
                outputs(kind, steps - 1)

            def head_sums(t):
                bank, before = tile_of("qk3", 0, t)
                pe.wait_ge(hsq_ready, t + 1)
                mm(PS[:, bank, :], ccon("heads"), sq[:, t % 2, :], True, True).then_inc(hsum_done, 1)

            def feed_forward(l):
                norm = f"ffn{l}"
                hi, lo, ready = split_of(norm)
                ab = ABUF[l]
                for p, n in enumerate(PARTS):
                    tiles(f"up{l}.{p}", 2 * n, hi, lo, KC, ready if p == 0 else None,
                          norm if p == 0 else None)
                    tiles(f"down{l}.{p}", KC, chunks(Bhi[ab]), chunks(Blo[ab]), n,
                          (act_split, l * FC + PART0[p]))

            def embedding(l):
                stage = f"pp{l}"
                pe.wait_ge(p_split, 2 * l + 2)
                for q in range(2):
                    s, slot, _ = slab_of(stage, 0, q)
                    weights(s)
                    for m in range(4):
                        out = open_tile(stage, 0, 4 * q + m)
                        for k in range(2):
                            c = (2 * m + k) * P
                            last = mm3(out, whi[:, slot, c:c + P], wlo[:, slot, c:c + P],
                                       qkhi[:, 0, k, :], qklo[:, 0, k, :], k == 0, k == 1)
                    last.then_inc(slab_done, 1)
                hi, lo, ready = split_of(f"ple{l}")
                tiles(f"gate{l}", KC, hi, lo, KC, ready, f"ple{l}")

            first_pair("qk1a", "attn0")
            pe.wait_ge(consts_ready, 3)
            values("v1", "attn0", 2, 4, T)
            project_qk("qk1", "attn0", 0)
            attention(1, "attn0")
            output_squares(7)
            tiles("o1", KC, chunks(Bhi[0]), chunks(Blo[0]), KC, (o_split, 0), lead=3,
                  late=8 - OFIRST, meanwhile=lambda: [spread_factor(h) for h in range(OFIRST, 8)])
            feed_forward(0)
            embedding(0)
            first_pair("kq2a", "attn1")
            norm_sum("attn1")
            values("v2", "attn1", 1, 2, 256)
            project_qk("kq2", "attn1", 0)
            for part in range(2):
                project_qk("kq2", "attn1", 1, part, 4)
            attention(2, "attn1")
            tiles("o2", KC, chunks(Bhi[0]), chunks(Blo[0]), KC, (o_split, 8))
            feed_forward(1)
            embedding(1)
            hi, lo, ready = split_of("final")
            tiles("a3", 4, hi, lo, KC, ready, "final")
            tile("a3", 0, 4, hi, lo, KC)
            norm_sum("mix")
            for t in range(5, 8):
                tile("a3", 0, t, hi, lo, KC)
            row_to_column()
            values("v3", "final", 1, 4, T)
            pe.wait_ge(p_split, 5)
            for t in range(TB):
                tk = slice(t * P, t * P + P)
                for k in range(KC):
                    last = mm3(PS[:, 6, 8 * t:8 * t + 8], hi[:, k, tk], lo[:, k, tk],
                               wfhi[:, 8 * k:8 * k + 8], wflo[:, 8 * k:8 * k + 8], k == 0, k == KC - 1)
            last.then_inc(f_done, 1)
            for t in range(2):
                project_qk("qk3", "final", t)
            pe.wait_ge(rcol_ready, 3)
            pe.wait_ge(f_log, 1)
            for t in range(TB):
                for u in range(t + 1):
                    last = mm(PS[:, 7, 8 * t:8 * t + 8], ccon("upto") if u == t else ones,
                              fl[:, 2, 8 * u:8 * u + 8], u == 0, u == t)
            last.then_inc(cum_done, 1)
            head_sums(0)
            project_qk("qk3", "final", 2)
            head_sums(1)
            pe.wait_ge(cum_ready, 1)
            for t in range(TB):
                last = pe.transpose(PS[0:8, 7, t * P:t * P + P], fl[:, 3, 8 * t:8 * t + 8], ident)
            last.then_inc(cumT_done, 1)
            project_qk("qk3", "final", 3, 0, 2)
            head_sums(2)
            attention(3, "final")
            tiles("gb3", 8, hi, lo, KC, None)
            for c in range(CT):
                pe.wait_ge(taps_done, c + 1)
                last = mm(PS[:, 5, :], ones, cvo[:, c, :], c == 0, c == CT - 1)
            last.then_inc(mean_done, 1)

            def variance():
                for c in range(CT):
                    pe.wait_ge(csq_ready, c + 1)
                    last = mm(PS[:, 6, :], ones, sq[:, c % 2, :], c == 0, c == CT - 1)
                    last.then_inc(var_done, 1)

            def two_tiles(stage, s, slot, first, xhi, xlo):
                weights(s)
                for m in range(2):
                    out = open_tile(stage, 0, first + m)
                    for k in range(4):
                        c = (4 * m + k) * P
                        last = mm3(out, whi[:, slot, c:c + P], wlo[:, slot, c:c + P],
                                   xhi(k), xlo(k), k == 0, k == 3)
                last.then_inc(slab_done, 1)
            pe.wait_ge(o_split, 20)
            for q in range(4):
                s, slot, _ = slab_of("ao3", 0, q)
                two_tiles("ao3", s, slot, 2 * q, lambda k: pthi[:, k, :], lambda k: ptlo[:, k, :])
                if q == 0:
                    variance()
            for q in range(4):
                for u in range(2):
                    s, slot, _ = slab_of("gc3", 0, 3 * q + u)
                    weights(s)
                    out = open_tile("gc3", 0, 4 * q + u)
                    for k in range(KC):
                        c = slice(k * P, k * P + P)
                        last = mm3(out, whi[:, slot, c], wlo[:, slot, c], hi[:, k, :], lo[:, k, :],
                                   k == 0, k == KC - 1)
                    last.then_inc(slab_done, 1)
                if q == 0:
                    pe.wait_ge(c_split, CT)
                s, slot, _ = slab_of("gc3", 0, 3 * q + 2)
                two_tiles("gc3", s, slot, 4 * q + 2, lambda k: qkhi[:, k // 2, k % 2, :],
                          lambda k: qklo[:, k // 2, k % 2, :])
            tiles("out3", 8, chunks(Bhi[1]), chunks(Blo[1]), KC, (c_split, CT))
            feed_forward(2)

        @block.scalar
        def _(act):
            own = Own(act, act_step)

            def high(s, slot, half):
                act.wait_ge(raw_ready[slot % RAWS], 16 * half + 16)
                act.activation(whi[:, slot, :], raw[:, slot % RAWS, :], ACT.Copy)\
                   .then_inc(hi_ready, 1)

            def used(stage, i, j, more=True):
                s, slot, half = slab_of(stage, i, j)
                act.wait_ge(slab_done, s + 1)
                if more:
                    high(s + RING, slot, half + RING // RAWS)

            def freed(stage, i, j):
                bank, before = tile_of(stage, i, j)
                act.wait_ge(tile_free[bank], before + 2)

            def square_and_high(norm, m, slot):
                n = NORMS.index(norm)
                c = KC * n + m
                if norm in GAIN:
                    name, col = GAIN[norm]
                    act.activation(chunks(Bhi[BUF[norm]])[:, m, :], X[:, m, :], ACT.Copy,
                                   scale=gain(name, col, m)).then_inc(xhi_ready, 1)
                if not (n == 0 and m < 2):
                    act.wait_ge(sq_used, c - 1)
                act.activation(sq[:, slot, :], X[:, m, :], ACT.Square).then_inc(sq_ready, 1)

            def root(norm):
                n = NORMS.index(norm)
                act.wait_ge(ss_done, n + 1)
                act.activation(sq[:, 0, :], PS[:, 7, :], ACT.Sqrt, scale=1.0 / D, bias=eps[:, 0:1])\
                   .then_inc(root_ready, 1)

            def rounds(n, body):
                if n == 1:
                    body(0)
                elif n == 2:
                    body(0)
                    body(1)
                else:
                    with act.Fori(0, n) as i:
                        body(i)

            def residual(stage, norm, last=False):
                if norm:
                    act.wait_ge(r_ready, NORMS.index(norm))

                def body(i):
                    for j in range(4):
                        used(stage, i, j, not (last and i == 1))
                        if norm:
                            freed(stage, i, j)
                            square_and_high(norm, 4 * i + j, j % 2)
                rounds(2, body)

            def values(stage, halves, slabs, width):
                for hf in range(halves):
                    for q in range(slabs):
                        used(stage, 0, hf * slabs + q)
                    if hf == 0:
                        act.wait_ge(rcol_ready, {"v1": 1, "v2": 2, "v3": 3}[stage])
                        if stage != "v1":
                            act.wait_ge(pad_ready, {"v2": 4, "v3": 8}[stage])
                    for t in range(TB):
                        bank, _ = tile_of(stage, 0, hf * TB + t)
                        if stage == "v1":
                            outs = [(Bhi[1][:, :].rearrange("p (k n) -> p k n", k=TB)
                                     [:, t, hf * T:hf * T + T], PS[:, bank, :])]
                        else:
                            outs = padded(stage, Bhi, PS[:, bank, 0:width], t)
                        for out, src in outs:
                            last = act.activation(out, src, ACT.Copy, scale=rcol[:, t:t + 1])
                        last.then_inc(vhi_ready, 1)
                    if stage == "v1" and hf == 0:
                        for t in range(2):
                            swap_halves("qk1a", t, t)
                        for t in range(2):
                            q_high(t, 0, t)

            def swap_halves(stage, t, n):
                if stage not in ("qk1a", "kq2a"):
                    used(stage, 0, t)
                bank, _ = tile_of(stage, 0, t)
                if n >= 2:
                    act.wait_ge(rope_ready, n - 1)
                for to, of in ((0, 32), (32, 0), (64, 96), (96, 64)):
                    last = act.activation(swap[to:to + 32, n % 2, :], PS[of:of + 32, bank, :], ACT.Copy)
                last.then_inc(swap_ready, 1)

            def q_high(n, b, which):
                act.wait_ge(rope_ready, n + 1)
                act.activation(qkhi[:, b, which, :], qraw[:, n % 2, :], ACT.Copy,
                               scale=(QSCALE, 1.0)[which]).then_inc(qhi_ready, 1)

            def exps(kind, g):
                for s in range(2):
                    n = SC0[kind] + 2 * g + s
                    nb = band(kind, g % 4)[1]
                    act.wait_ge(max_ready, n + 1)
                    if g >= 2:
                        act.wait_ge(trans_done, PB0[kind] + HP[kind] * (g - 2)
                                    + (s + 1 if HP[kind] == 2 else 1))
                    act.activation(probs(kind)[:, 2 * (g % 2) + s, 0:nb * P],
                                   PS[:, score_bank(kind, n), 0:nb * P], ACT.Exp,
                                   bias=nmax[:, n % 4:n % 4 + 1], accum_out=rsum[:, n % 4:n % 4 + 1])\
                       .then_inc(exp_ready, 1)
                if kind == 2:
                    for s in range(2):
                        n = SC0[2] + 2 * g + s
                        last = act.activation(rsum[:, 4 + n % 4:5 + n % 4],
                                              cpar("sinks", head_of(g // 4, s)), ACT.Exp,
                                              bias=nmax[:, n % 4:n % 4 + 1])
                    last.then_inc(sink_ready, 1)

            def prob_high(kind, g):
                blocks = band(kind, g % 4)[1]
                for s in range(HP[kind]):
                    n = PB0[kind] + HP[kind] * g + s
                    act.wait_ge(trans_done, n + 1)
                    back = 4 // HP[kind]
                    if kind > 1 or g >= back:
                        act.wait_ge(pv_done, PV0[kind] + g - back + 1)
                    act.activation(pthi[:, n % 4, 0:blocks * P], PS[:, 2 + n % 2, 0:blocks * P],
                                   ACT.Copy).then_inc(pthi_ready, 1)

            def evacuate(kind, j):
                act.wait_ge(pv_done, PV0[kind] + 4 * j + 4)
                act.activation((OA3 if kind == 3 else OA)[:, j, :], PS[:, 7, :], ACT.Copy)\
                   .then_inc(o_ready, 1)

            def output_square(h):
                act.wait_ge(o_ready, h + 1)
                if h >= 2:
                    act.wait_ge(osum_done, h - 1)
                act.activation(sq[:, h % 2, :], OA[:, h, :], ACT.Square).then_inc(osq_ready, 1)

            def output_root(last):
                act.wait_ge(osum_done, 8 if last else OFIRST)
                if last:
                    act.wait_ge(orinv_ready, 1)
                act.activation(acc[0:8, :], PS[0:8, 6, :], ACT.Sqrt, scale=1.0 / P,
                               bias=eps[0:8, 0:1]).then_inc(oroot_ready, 1)

            def normed_high(h):
                act.wait_ge(onorm_ready, h + 1)
                act.activation(chunks(Bhi[0])[:, h, :], OA[:, h, :], ACT.Copy, scale=gs[:, 0:1])\
                   .then_inc(ohi_ready, 1)

            def attention(kind):
                steps = 4 * PAIRS[kind]
                exps(kind, 0)
                for g in range(steps):
                    begun, halfway = finished(kind, g - 1), finished(kind, g - 2)
                    if kind < 3 and begun is not None:
                        q_high(*place_of(kind, begun))
                    if kind == 3 and begun is not None:
                        head_square(begun)
                    if kind == 3 and halfway is not None:
                        head_high(halfway)
                    if g + 1 < steps:
                        exps(kind, g + 1)
                    prob_high(kind, g)
                    if kind == 2:
                        for c in OSPLIT.get(g, ()):
                            output_high(OA, c)
                    if g % 4 == 0 and g:
                        evacuate(kind, g // 4 - 1)
                        if kind == 1:
                            output_square(g // 4 - 1)
                    if kind == 1:
                        for h in SPREAD.get(g, ()):
                            normed_high(h)
                        if g == 4 * OFIRST + 1:
                            output_root(False)
                    if kind == 3 and begun is not None:
                        head_root(begun)
                    done = finished(kind, g)
                    if done is not None and kind < 3:
                        swap_halves(PROJ[kind], done, place_of(kind, done)[0])
                    if done is not None and kind == 3:
                        used("qk3", 0, done)
                evacuate(kind, PAIRS[kind] - 1)

            def output_high(src, c):
                hi = pthi[:, c, :] if src is OA3 else chunks(Bhi[0])[:, c, :]
                act.wait_ge(o_ready, (OP0[3] if src is OA3 else OP0[2]) + c + 1)
                act.activation(hi, src[:, c, :], ACT.Copy).then_inc(ohi_ready, 1)

            def feed_forward(l, last=False):
                root(f"ffn{l}")
                n0 = l * FC
                for p, n in enumerate(PARTS):
                    stage = f"up{l}.{p}"

                    def body(i):
                        for pair in range(2):
                            q = PART0[p] + 2 * i + pair
                            for u in range(2):
                                used(stage, i, 2 * pair + u)
                                if l < 2:
                                    freed(stage, i, 2 * pair + u)
                                    act.activation(cv[:, 2 * pair + u, :], us[:, 2 * pair + u, :],
                                                   ACT.Identity, scale=conv_w[:, l, 1, u, bass.ds(q, 1)],
                                                   bias=conv_w[:, l, 3, u, bass.ds(q, 1)])\
                                       .then_inc(mid_ready, 1)
                            if l < 2:
                                act.wait_ge(conv_done, 2 * (n0 + q) + 1)
                                src = cv
                            else:
                                freed(stage, i, 2 * pair)
                                src = us
                            act.activation(us[:, 2 * pair, :] if l < 2 else cv[:, 2 * pair, :],
                                           src[:, 2 * pair, :], ACT.Silu).then_inc(silu_ready, 1)
                            act.wait_ge(act_ready, n0 + q + 1)
                            act.activation(chunks(Bhi[ABUF[l]])[:, 2 * i + pair, :], av[:, pair, :],
                                           ACT.Copy).then_inc(ahi_ready, 1)
                    rounds(n // 2, body)
                    if p == 0 and l < 2:
                        split_p(l)
                    norm = {0: "ple0", 1: "ple1", 2: None}[l] if p == 2 else None
                    residual(f"down{l}.{p}", norm, last=(l == 2 and p == 2))

            def embedding(l, nxt):
                for q in range(2):
                    used(f"pp{l}", 0, q)
                    for m in range(4):
                        bank, _ = tile_of(f"pp{l}", 0, 4 * q + m)
                        act.activation(pp[:, 4 * q + m, :], PS[:, bank, :], ACT.Copy)\
                           .then_inc(tile_free[bank], 1)
                root(f"ple{l}")
                act.wait_ge(r_ready, NORMS.index(nxt))

                def body(i):
                    for j in range(4):
                        m = 4 * i + j
                        used(f"gate{l}", i, j)
                        freed(f"gate{l}", i, j)
                        act.activation(gt[:, j % 2, :], gt[:, j % 2, :], ACT.Sigmoid)\
                           .then_inc(sig_ready, 1)
                        act.wait_ge(ple_added, KC * l + m + 1)
                        square_and_high(nxt, m, j % 2)
                rounds(2, body)

            def split_p(l):
                act.wait_ge(p_in, 16 * l + 16)
                for k in range(2):
                    act.activation(qkhi[:, 0, k, :], PT[:, k, :], ACT.Copy).then_inc(phi_ready, 1)

            def fetch_p(l):
                act.dma_start(PT, pT[l]).then_inc(p_in, 16)

            act.dma_start(par_sb[:, :], par).then_inc(par_in, 16)
            for q in range(4):
                act.dma_start(X[:, 2 * q:2 * q + 2, :], xT[:, 2 * q:2 * q + 2, :]).then_inc(x_in[q], 16)
            act.dma_start(con_sb[:, :], con).then_inc(con_in, 16)
            act.dma_start(AR[:, 0:T].bitcast(I32), posd).then_inc(pos_in, 16)
            act.dma_start(AR[:, 4096:4096 + 256], lamd).then_inc(lam_in, 16)
            act.wait_ge(par_in, 16)
            for m in range(KC):
                if m % 2 == 0:
                    act.wait_ge(x_in[m // 2], 16)
                    high(m // 2, m // 2, m // 2 // RAWS)
                square_and_high("attn0", m, m % 2)
            act.wait_ge(consts_ready, 4)
            act.activation(sinT[:, :], angs[:, 1, :], ACT.Sin).then_inc(trig_ready, 1)
            act.activation(cosT[:, :], angs[:, 2, :], ACT.Sin).then_inc(trig_ready, 1)
            act.activation(lam[:, 2:4], lam[:, 0:2], ACT.Exp).then_inc(trig_ready, 1)
            root("attn0")
            for t in range(2):
                used("qk1a", 0, t)
            values("v1", 2, 4, T)
            swap_halves("qk1", 0, 2)
            attention(1)
            output_square(7)
            output_root(True)
            for h in (6, 7):
                normed_high(h)
            residual("o1", "ffn0")
            fetch_p(0)
            feed_forward(0)
            embedding(0, "attn1")
            for t in range(2):
                used("kq2a", 0, t)
                if t == 0:
                    root("attn1")
            values("v2", 1, 2, 256)
            for t in range(2):
                swap_halves("kq2a", t, QT0[2] + t)
            for t in range(2):
                q_high(QT0[2] + t, 0, 1 - t)
            swap_halves("kq2", 0, QT0[2] + 2)
            attention(2)
            output_high(OA, 7)
            residual("o2", "ffn1")
            fetch_p(1)
            feed_forward(1)
            embedding(1, "final")
            for t in range(2):
                used("a3", 0, t)
            root("final")
            for m in range(KC):
                act.wait_ge(y_ready, m + 1)
                square_and_high("mix", m, (m + 1) % 2)
            for t in range(2, 5):
                used("a3", 0, t)
            root("mix")
            for t in range(5, 8):
                used("a3", 0, t)
            for q in range(4):
                freed("a3", 0, 2 * q + 1)
                act.activation(atmp[:, 2, :], atmp[:, 1, :], ACT.Sigmoid).then_inc(asig_ready, 1)
            act.activation(wfhi[:, :], cpar("w_f", 0, KC * 8), ACT.Copy).then_inc(phi_ready, 1)
            values("v3", 1, 4, T)
            act.wait_ge(f_lin, 1)
            own.step(act.activation(fl[:, 1, :], fl[:, 0, :], ACT.Abs))
            own.wait()
            own.step(act.activation(fl[:, 1, :], fl[:, 1, :], ACT.Exp, scale=-1.0))
            own.wait()
            act.activation(fl[:, 1, :], fl[:, 1, :], ACT.Ln, bias=1.0).then_inc(f_exp, 1)

            def head_square(t):
                act.wait_ge(rope_ready, QT0[3] + t + 1)
                if t >= 2:
                    act.wait_ge(hsum_done, t - 1)
                act.activation(sq[:, t % 2, :], qraw3[:, t % 2, :], ACT.Square).then_inc(hsq_ready, 1)

            def head_root(t):
                bank, _ = tile_of("qk3", 0, t)
                act.wait_ge(hsum_done, t + 1)
                if t:
                    act.wait_ge(orinv_ready, 2 + t)
                act.activation(sinT[:, :], PS[:, bank, :], ACT.Sqrt, scale=1.0 / 64, bias=eps[:, 0:1])\
                   .then_inc(tile_free[bank], 1)

            def head_high(t):
                _, b, u = place_of(3, t)
                act.wait_ge(hroot_ready, t + 1)
                act.activation(qkhi[:, b, u, :], qraw3[:, u, :], ACT.Copy, scale=gs[:, 1 + u:2 + u])\
                   .then_inc(qhi_ready, 1)

            for t in range(2):
                used("qk3", 0, t)
                head_square(t)
            head_root(0)
            used("qk3", 0, 2)
            head_root(1)
            act.wait_ge(cumT_done, 1)
            act.activation(cc[0:8, :], PS[0:8, 7, :], ACT.Copy).then_inc(cchi_ready, 1)
            for t in range(2):
                head_high(t)
            head_square(2)
            head_root(2)
            attention(3)
            for c in range(4):
                output_high(OA3, c)
            for m in range(8):
                used("gb3", 0, m)
                freed("gb3", 0, m)
                act.activation(G[:, m, :], t3[:, m % 2, :], ACT.Sigmoid).then_inc(sig_ready, 1)
            for c in range(CT):
                act.wait_ge(cen_ready, c + 1)
                if c >= 2:
                    act.wait_ge(var_done, c - 1)
                act.activation(sq[:, c % 2, :], cvo[:, c, :], ACT.Square).then_inc(csq_ready, 1)
            used("ao3", 0, 0)
            act.wait_ge(var_done, CT)
            act.activation(sinT[:, :], PS[:, 6, :], ACT.Sqrt, scale=1.0 / CONV, bias=eps[:, 0:1])\
               .then_inc(croot_ready, 1)
            used("ao3", 0, 1)
            for c in range(CT):
                act.wait_ge(cn_ready, c + 1)
                own.step(act.activation(cvo[:, c, :], cvo[:, c, :], ACT.Silu,
                                        scale=cpar("g_ln", c), bias=cpar("b_ln", c)))
            own.wait()
            for c in range(CT):
                act.activation(qkhi[:, c // 2, c % 2, :], cvo[:, c, :], ACT.Copy)\
                   .then_inc(chi_ready, 1)
            for q in range(2, 4):
                used("ao3", 0, q)
            for q in range(4):
                for u in range(2):
                    used("gc3", 0, 3 * q + u)
                    freed("gc3", 0, 4 * q + u)
                    act.activation(t3[:, u, :], t3[:, u, :], ACT.Sigmoid).then_inc(sig_ready, 1)
                used("gc3", 0, 3 * q + 2)
                for m in (2 * q, 2 * q + 1):
                    act.wait_ge(a_ready, CT + m + 1)
                    act.activation(chunks(Bhi[1])[:, m, :], G[:, m, :], ACT.Copy)\
                       .then_inc(chi_ready, 1)
            residual("out3", "ffn2")
            feed_forward(2)

        @block.vector
        def _(dve):
            own = Own(dve, dve_step)
            tt, stt, ts = dve.tensor_tensor, dve.scalar_tensor_tensor, dve.tensor_scalar

            def done(stage, i, j):
                dve.wait_ge(slab_done, slab_of(stage, i, j)[0] + 1)

            def scaled(out, stage, i, j):
                bank, _ = tile_of(stage, i, j)
                tt(out, PS[:, bank, :], R[:, :], ALU.mult).then_inc(tile_free[bank], 1)

            def add_and_low(norm, m, slot):
                n = NORMS.index(norm)
                c = KC * n + m
                if norm in GAIN:
                    name, col = GAIN[norm]
                    k = KC * SPLITS.index(norm) + m
                    dve.wait_ge(xhi_ready, k + 1)
                    b = BUF[norm]
                    stt(chunks(Blo[b])[:, m, :], X[:, m, :], gain(name, col, m),
                        f32(chunks(Bhi[b])[:, m, :]), ALU.mult, ALU.subtract).then_inc(x_split, 1)
                dve.wait_ge(sq_ready, c + 1)
                tt(acc[:, :], acc[:, :], sq[:, slot, :], ALU.add).then_inc(sq_used, 1)
                dve.wait_ge(sq_used, c + 1)

            def clear_sum():
                own.step(dve.memset(acc[:, :], 0.0))
                own.wait()

            def factor(norm):
                n = NORMS.index(norm)
                dve.wait_ge(root_ready, n + 1)
                dve.reciprocal(R[:, :], sq[:, 0, :]).then_inc(r_ready, 1)
                dve.wait_ge(r_ready, n + 1)

            def rounds(n, per, body):
                if n <= 2:
                    for i in range(n):
                        body(i)
                else:
                    own.rounds(0, n, per, body)

            def residual(stage, norm):
                if norm:
                    clear_sum()

                def body(i):
                    for j in range(4):
                        m = 4 * i + j
                        done(stage, i, j)
                        bank, before = tile_of(stage, i, j)
                        tt(X[:, m, :], X[:, m, :], PS[:, bank, :], ALU.add)\
                            .then_inc(tile_free[bank], 1)
                        if norm:
                            add_and_low(norm, m, j % 2)
                rounds(2, 0, body)

            def columns(n):
                dve.wait_ge(rcol_done, n)
                dve.tensor_copy(rcol[:, :], PS[:, 7, 0:TB]).then_inc(rcol_ready, 1)
                dve.wait_ge(rcol_ready, n)

            def values_low(stage, halves, width):
                n0 = {"v1": 0, "v2": 2 * TB, "v3": 3 * TB}[stage]
                for hf in range(halves):
                    for t in range(TB):
                        bank, _ = tile_of(stage, 0, hf * TB + t)
                        dve.wait_ge(vhi_ready, n0 + hf * TB + t + 1)
                        if stage == "v1":
                            v = [b[:, :].rearrange("p (k n) -> p k n", k=TB)[:, t, hf * T:hf * T + T]
                                 for b in (Blo[1], Bhi[1])]
                            parts = [(v[0], PS[:, bank, :], v[1])]
                        else:
                            lo = padded(stage, Blo, PS[:, bank, 0:width], t)
                            hi = padded(stage, Bhi, PS[:, bank, 0:width], t)
                            parts = [(a, s, b) for (a, s), (b, _) in zip(lo, hi)]
                        for q, (out, src, hi) in enumerate(parts):
                            ins = stt(out, src, rcol[:, t:t + 1], f32(hi), ALU.mult, ALU.subtract)
                            if q == 0 and len(parts) == 2:
                                own.step(ins)
                        ins.then_inc(tile_free[bank], 1)
                    if stage == "v1" and hf == 0:
                        for t in range(2):
                            rope("qk1a", t, t)
                        for t in range(2):
                            q_low(t, 0, t)

            def zero_padding(stage):
                nh = 4 if stage == "v2" else 8
                for b in (Bhi[1], Blo[1]):
                    v = b[:, 0:TB * nh * P].rearrange("p (k two c) -> p k two c", two=2, c=P)
                    for u in range(2):
                        dve.memset(f32(v[:, :, u, 64 - 64 * u:P - 64 * u]), 0.0).then_inc(pad_ready, 1)

            def rope(stage, t, n):
                bank, before = tile_of(stage, 0, t)
                b = n % 2
                dve.wait_ge(swap_ready, n + 1)
                if n >= 2:
                    dve.wait_ge(q_ready, n - 1)
                    dve.wait_ge(qhi_ready, n - 1)
                tt(qraw[:, b, :], PS[:, bank, :], rC, ALU.mult).then_inc(tile_free[bank], 1)
                own.step(tt(swap[:, b, :], swap[:, b, :], rS, ALU.mult))
                own.wait()
                dve.wait_ge(tile_free[bank], before + 2)
                tt(qraw[:, b, :], qraw[:, b, :], swap[:, b, :], ALU.add).then_inc(rope_ready, 1)

            def q_low(n, b, which):
                dve.wait_ge(qhi_ready, n + 1)
                stt(qklo[:, b, which, :], qraw[:, n % 2, :], (QSCALE, 1.0)[which],
                    f32(qkhi[:, b, which, :]), ALU.mult, ALU.subtract).then_inc(q_ready, 1)

            def maxima(kind, g):
                nb = band(kind, g % 4)[1]
                for s in range(2):
                    n = SC0[kind] + 2 * g + s
                    dve.wait_ge(score_done, n + 1)
                    src, c = PS[:, score_bank(kind, n), 0:nb * P], n % 4
                    if kind == 2:
                        own.step(dve.tensor_reduce(nmax[:, 4 + c:5 + c], src, AX, ALU.max))
                    else:
                        dve.tensor_reduce(nmax[:, c:c + 1], src, AX, ALU.max, negate=True)\
                            .then_inc(max_ready, 1)
                if kind == 2:
                    own.wait()
                    for s in range(2):
                        c = (SC0[2] + 2 * g + s) % 4
                        ts(nmax[:, c:c + 1], nmax[:, 4 + c:5 + c], cpar("sinks", head_of(g // 4, s)),
                           -1.0, ALU.max, ALU.mult).then_inc(max_ready, 1)

            def normalise(kind, g):
                n = SC0[kind] + 2 * g
                nb = band(kind, g % 4)[1]
                pr, c, b = probs(kind), n % 4, 2 * (g % 2)
                dve.wait_ge(exp_ready, n + 2)
                if kind == 2:
                    dve.wait_ge(sink_ready, g + 1)
                    own.step(tt(rsum[:, c:c + 2], rsum[:, c:c + 2], rsum[:, 4 + c:6 + c], ALU.add))
                    own.wait()
                own.step(dve.reciprocal(rinv[:, c:c + 2], rsum[:, c:c + 2]))
                own.wait()
                if kind == 1:
                    own.step(tt(rinv[:, c + 1:c + 2], rinv[:, c + 1:c + 2], lam[:, 5:6], ALU.mult))
                    own.step(ts(pr[:, b, :], pr[:, b, :], rinv[:, c:c + 1], None, ALU.mult))
                    own.wait()
                    stt(pr[:, b + 1, :], pr[:, b + 1, :], rinv[:, c + 1:c + 2], pr[:, b, :],
                        ALU.mult, ALU.add).then_inc(prob_ready, 1)
                else:
                    for s in range(2):
                        v = pr[:, b + s, 0:nb * P]
                        ts(v, v, rinv[:, c + s:c + s + 1], None, ALU.mult).then_inc(prob_ready, 1)

            def prob_low(kind, g):
                blocks = band(kind, g % 4)[1]
                for s in range(HP[kind]):
                    n = PB0[kind] + HP[kind] * g + s
                    dve.wait_ge(pthi_ready, n + 1)
                    tt(ptlo[:, n % 4, 0:blocks * P], PS[:, 2 + n % 2, 0:blocks * P],
                       f32(pthi[:, n % 4, 0:blocks * P]), ALU.subtract).then_inc(pt_ready, 1)

            def norm_output(h):
                dve.wait_ge(obc_done, h + 1)
                tt(OA[:, h, :], OA[:, h, :], PS[:, spread_bank(h), :], ALU.mult).then_inc(onorm_ready, 1)

            def normed_low(h):
                dve.wait_ge(ohi_ready, h + 1)
                stt(chunks(Blo[0])[:, h, :], OA[:, h, :], gs[:, 0:1], f32(chunks(Bhi[0])[:, h, :]),
                    ALU.mult, ALU.subtract).then_inc(o_split, 1)

            def invert_output_root(last):
                dve.wait_ge(oroot_ready, 2 if last else 1)
                dve.reciprocal((acc if last else R)[0:8, :], acc[0:8, :]).then_inc(orinv_ready, 1)

            def output_low(src, c):
                hi, lo = ((pthi[:, c, :], ptlo[:, c, :]) if src is OA3 else
                          (chunks(Bhi[0])[:, c, :], chunks(Blo[0])[:, c, :]))
                dve.wait_ge(ohi_ready, OP0[3 if src is OA3 else 2] + c + 1)
                tt(lo, src[:, c, :], f32(hi), ALU.subtract).then_inc(o_split, 1)

            def attention(kind):
                steps = 4 * PAIRS[kind]
                maxima(kind, 0)
                for g in range(steps):
                    normalise(kind, g)
                    begun, halfway = finished(kind, g - 1), finished(kind, g - 2)
                    if kind < 3 and begun is not None:
                        rope(PROJ[kind], begun, place_of(kind, begun)[0])
                    if kind == 3 and begun is not None:
                        head_scaled(begun)
                    if kind == 3 and halfway is not None:
                        head_norm(halfway)
                    if g + 1 < steps:
                        maxima(kind, g + 1)
                    if kind < 3 and begun is not None:
                        q_low(*place_of(kind, begun))
                    if kind == 3 and halfway is not None:
                        head_low(halfway)
                    if kind == 1:
                        if g == 4 * OFIRST + 2:
                            invert_output_root(False)
                        for h in SPREAD.get(g, ()):
                            norm_output(h)
                        for h in SPREAD.get(g - 1, ()):
                            normed_low(h)
                    prob_low(kind, g)
                    if kind == 3:
                        taps(TAPS_A_STEP)
                    if kind == 2:
                        for c in OSPLIT.get(g, ()):
                            output_low(OA, c)

            def feed_forward(l):
                factor(f"ffn{l}")
                n0 = l * FC
                for p, n in enumerate(PARTS):
                    stage = f"up{l}.{p}"

                    def body(i):
                        for pair in range(2):
                            q = PART0[p] + 2 * i + pair
                            for u in range(2):
                                done(stage, i, 2 * pair + u)
                                scaled(us[:, 2 * pair + u, :], stage, i, 2 * pair + u)
                            if l < 2:
                                for u in range(2):
                                    c, x = cv[:, 2 * pair + u, :], us[:, 2 * pair + u, :]
                                    dve.wait_ge(mid_ready, 2 * (n0 + q) + u + 1)
                                    own.step(stt(c[:, 1:T], x[:, 0:T - 1], conv_w[:, l, 0, u, bass.ds(q, 1)],
                                                 c[:, 1:T], ALU.mult, ALU.add))
                                    own.wait()
                                    stt(c[:, 0:T - 1], x[:, 1:T], conv_w[:, l, 2, u, bass.ds(q, 1)],
                                        c[:, 0:T - 1], ALU.mult, ALU.add).then_inc(conv_done, 1)
                                dve.wait_ge(conv_done, 2 * (n0 + q) + 2)
                            dve.wait_ge(silu_ready, n0 + q + 1)
                            if l < 2:
                                g, v = us[:, 2 * pair, :], cv[:, 2 * pair + 1, :]
                            else:
                                g, v = cv[:, 2 * pair, :], us[:, 2 * pair + 1, :]
                                bank, before = tile_of(stage, i, 2 * pair + 1)
                                dve.wait_ge(tile_free[bank], before + 2)
                            own.wait()
                            tt(av[:, pair, :], g, v, ALU.mult).then_inc(act_ready, 1)
                            dve.wait_ge(ahi_ready, n0 + q + 1)
                            k = 2 * i + pair
                            b = ABUF[l]
                            tt(chunks(Blo[b])[:, k, :], av[:, pair, :], f32(chunks(Bhi[b])[:, k, :]),
                               ALU.subtract).then_inc(act_split, 1)
                            dve.wait_ge(act_split, n0 + q + 1)
                    rounds(n // 2, 4 if l < 2 else 0, body)
                    if p == 0 and l < 2:
                        for k in range(2):
                            dve.wait_ge(phi_ready, 2 * l + k + 1)
                            tt(qklo[:, 0, k, :], PT[:, k, :], f32(qkhi[:, 0, k, :]), ALU.subtract)\
                                .then_inc(p_split, 1)
                    norm = {0: "ple0", 1: "ple1", 2: None}[l] if p == 2 else None
                    residual(f"down{l}.{p}", norm)

            def embedding(l, nxt):
                factor(f"ple{l}")
                clear_sum()

                def body(i):
                    for j in range(4):
                        m = 4 * i + j
                        done(f"gate{l}", i, j)
                        scaled(gt[:, j % 2, :], f"gate{l}", i, j)
                        dve.wait_ge(sig_ready, KC * l + m + 1)
                        own.step(tt(gu[:, j % 2, :], gt[:, j % 2, :], pp[:, m, :], ALU.mult))
                        own.wait()
                        tt(X[:, m, :], X[:, m, :], gu[:, j % 2, :], ALU.add).then_inc(ple_added, 1)
                        dve.wait_ge(ple_added, KC * l + m + 1)
                        add_and_low(nxt, m, j % 2)
                rounds(2, 0, body)

            for b in range(BANKS):
                dve.memset(credit[:, b:b + 1], 0.0).then_inc(tile_free[b], 1)
            own.step(dve.memset(f32(cc[:, :]), 0.0))
            dve.memset(eps[:, :], EPS).then_inc(consts_ready, 1)
            clear_sum()
            dve.wait_ge(par_in, 16)
            own.step(tt(gfm[:, :], cpar("final_norm", 0, KC), cpar("g_mix", 0, KC), ALU.mult))
            for q in range(4):
                dve.wait_ge(x_in[q], 16)
                for m in (2 * q, 2 * q + 1):
                    add_and_low("attn0", m, m % 2)
            dve.wait_ge(con_in, 16)
            dve.tensor_copy(constR[:, :, :], con_sb[:, 0:3 * P].rearrange("p (n c) -> p n c", n=3))\
               .then_inc(consts_ready, 1)
            dve.tensor_copy(minusR[:, :, :], con_sb[:, CCOLS["minus"][0]:CCOLS["minus"][1]]
                            .rearrange("p (n c) -> p n c", c=1).broadcast_to((P, 8, P)))\
               .then_inc(consts_ready, 1)
            dve.wait_ge(consts_ready, 3)
            dve.wait_ge(pos_in, 16)
            A = angs
            MAGIC = 1.5 * 2.0 ** 23
            own.step(dve.tensor_copy(A[:, 1, :], A[:, 0, :].bitcast(I32)))
            own.wait()
            own.step(ts(A[:, 1, :], A[:, 1, :], ccon("freq"), None, ALU.mult))
            own.wait()
            own.step(ts(A[:, 3, :], A[:, 1, :], 1.0 / (2 * np.pi), MAGIC, ALU.mult, ALU.add))
            own.wait()
            own.step(ts(A[:, 3, :], A[:, 3, :], MAGIC, None, ALU.subtract))
            own.wait()
            c1 = 6.28125
            c2 = float(np.float32(int((2 * np.pi - c1) * 2 ** 20) / 2 ** 20))
            c3 = 2 * np.pi - c1 - c2
            for c in (c1, c2, c3):
                own.step(stt(A[:, 1, :], A[:, 3, :], -c, A[:, 1, :], ALU.mult, ALU.add))
                own.wait()
            own.step(ts(A[:, 1, :], A[:, 1, :], float(np.float32(3.1415925)),
                        float(np.float32(-3.1415925)), ALU.min, ALU.max))
            own.wait()
            own.step(ts(A[:, 2, :], A[:, 1, :], -1.0, None, ALU.mult))
            own.wait()
            own.step(tt(A[:, 2, :], A[:, 1, :], A[:, 2, :], ALU.max))
            own.wait()
            own.step(ts(A[:, 2, :], A[:, 2, :], -1.0, np.pi / 2, ALU.mult, ALU.add))
            dve.wait_ge(lam_in, 16)
            L = AR[:, 4096:4096 + 256].rearrange("p (a b c) -> p a b c", a=2, b=2)
            M = AR[:, 4608:4608 + 128].rearrange("p (a c) -> p a c", a=2)
            own.step(tt(M, L[:, :, 0, :], L[:, :, 1, :], ALU.mult))
            own.wait()
            dve.tensor_reduce(lam[:, 0:2], M, AX, ALU.add).then_inc(consts_ready, 1)
            dve.wait_ge(trig_ready, 3)
            own.step(tt(lam[:, 4:5], lam[:, 3:4], lam[:, 2:3], ALU.subtract))
            own.wait()
            own.step(ts(lam[:, 5:6], lam[:, 4:5], -LAM_INIT, None, ALU.add))
            own.step(ts(gs[:, 0:1], cpar("subln"), 1.0 - LAM_INIT, None, ALU.mult))
            own.step(ts(gs[:, 1:2], cpar("g_q"), QSCALE, None, ALU.mult))
            own.step(dve.tensor_copy(gs[:, 2:3], cpar("g_k")))
            own.step(ts(sinT[:, :], sinT[:, :], ccon("sign"), None, ALU.mult))
            own.wait()

            def rope_tables():
                own.step(tt(rC, cosT[:, :], R[:, :], ALU.mult))
                own.step(tt(rS, sinT[:, :], R[:, :], ALU.mult))
                own.wait()

            factor("attn0")
            rope_tables()
            columns(1)
            values_low("v1", 2, T)
            attention(1)
            invert_output_root(True)
            for h in (6, 7):
                norm_output(h)
            for h in (6, 7):
                normed_low(h)
            residual("o1", "ffn0")
            feed_forward(0)
            embedding(0, "attn1")
            zero_padding("v2")
            factor("attn1")
            rope_tables()
            columns(2)
            values_low("v2", 1, 256)
            for t in range(2):
                rope("kq2a", t, QT0[2] + t)
            for t in range(2):
                q_low(QT0[2] + t, 0, 1 - t)
            attention(2)
            output_low(OA, 7)
            residual("o2", "ffn1")
            feed_forward(1)
            embedding(1, "final")
            own.step(dve.memset(apad[:, :, 0:TAPS - 1], 0.0))
            factor("final")
            clear_sum()
            for m in range(KC):
                stt(X[:, m, :], X[:, m, :], cpar("final_norm", m), R[:, :], ALU.mult, ALU.mult)\
                    .then_inc(y_ready, 1)
                if m:
                    add_and_low("mix", m - 1, m % 2)
            add_and_low("mix", KC - 1, KC % 2)
            dve.wait_ge(root_ready, NORMS.index("mix") + 1)
            own.step(dve.reciprocal(cosT[:, :], sq[:, 0, :]))
            own.wait()
            tt(R[:, :], R[:, :], cosT[:, :], ALU.mult).then_inc(r_ready, 1)
            dve.wait_ge(r_ready, NORMS.index("mix") + 1)
            queue = [(c + u, w) for c in (0, 2) for w in range(TAPS) for u in range(2)]

            def taps(n):
                for _ in range(min(n, len(queue))):
                    c, w = queue.pop(0)
                    src, out = apad[:, c, w:w + T], cvo[:, c, :]
                    k = cpar("w_dw", w * CT + c)
                    if w == 0:
                        ins = ts(out, src, k, cpar("b_dw", c), ALU.mult, ALU.add)
                    else:
                        dve.wait_ge(dve_tap[c], w)
                        ins = stt(out, src, k, out, ALU.mult, ALU.add)
                    if w == TAPS - 1:
                        ins.then_inc(taps_done, 1)
                    else:
                        ins.then_inc(dve_tap[c], 1)

            for q in range(4):
                for u in range(2):
                    done("a3", 0, 2 * q + u)
                    if u == 0 and q:
                        dve.wait_ge(a_ready, q)
                    scaled(atmp[:, u, :], "a3", 0, 2 * q + u)
                dve.wait_ge(asig_ready, q + 1)
                bank, before = tile_of("a3", 0, 2 * q)
                dve.wait_ge(tile_free[bank], before + 2)
                tt(apad[:, q, TAPS - 1:], atmp[:, 0, :], atmp[:, 2, :], ALU.mult).then_inc(a_ready, 1)
                dve.wait_ge(a_ready, q + 1)
            dve.wait_ge(phi_ready, 5)
            tt(wflo[:, :], cpar("w_f", 0, KC * 8), f32(wfhi[:, :]), ALU.subtract).then_inc(p_split, 1)
            columns(3)
            zero_padding("v3")
            taps(20)
            values_low("v3", 1, T)
            dve.wait_ge(f_done, 1)
            for t in range(TB):
                c = slice(8 * t, 8 * t + 8)
                own.step(stt(fl[:, 0, c], PS[:, 6, c], rcol[:, t:t + 1], cpar("b_forget", 0, 8),
                             ALU.mult, ALU.add))
            own.wait()
            ts(fl[:, 2, :], fl[:, 0, :], 0.0, None, ALU.min).then_inc(f_lin, 1)
            dve.wait_ge(f_lin, 1)
            taps(6)
            dve.wait_ge(f_exp, 1)
            tt(fl[:, 2, :], fl[:, 2, :], fl[:, 1, :], ALU.subtract).then_inc(f_log, 1)

            def head_scaled(t):
                done("qk3", 0, t)
                bank, _ = tile_of("qk3", 0, t)
                if t >= 2:
                    dve.wait_ge(q_ready, QT0[3] + t - 1)
                tt(qraw3[:, t % 2, :], PS[:, bank, :], R[:, :], ALU.mult).then_inc(rope_ready, 1)

            def head_norm(t):
                bank, before = tile_of("qk3", 0, t)
                dve.wait_ge(tile_free[bank], before + 2)
                if t:
                    dve.wait_ge(hroot_ready, t)
                dve.reciprocal(cosT[:, :], sinT[:, :]).then_inc(orinv_ready, 1)
                dve.wait_ge(orinv_ready, t + 3)
                dve.wait_ge(rope_ready, QT0[3] + t + 1)
                tt(qraw3[:, t % 2, :], qraw3[:, t % 2, :], cosT[:, :], ALU.mult).then_inc(hroot_ready, 1)

            def head_low(t):
                _, b, u = place_of(3, t)
                dve.wait_ge(qhi_ready, QT0[3] + t + 1)
                stt(qklo[:, b, u, :], qraw3[:, u, :], gs[:, 1 + u:2 + u], f32(qkhi[:, b, u, :]),
                    ALU.mult, ALU.subtract).then_inc(q_ready, 1)

            for t in range(2):
                head_scaled(t)
            taps(4)
            dve.wait_ge(cum_done, 1)
            dve.tensor_copy(fl[:, 3, :], PS[:, 7, 0:TB * 8]).then_inc(cum_ready, 1)
            for t in range(2):
                head_norm(t)
            for t in range(2):
                head_low(t)
            head_scaled(2)
            dve.wait_ge(cchi_ready, 1)
            tt(cc[32:40, :], PS[0:8, 7, :], f32(cc[0:8, :]), ALU.subtract).then_inc(cc_ready, 1)
            attention(3)
            for c in range(4):
                output_low(OA3, c)
            dve.wait_ge(o_split, 20)
            for m in range(8):
                done("gb3", 0, m)
                if m >= 2:
                    dve.wait_ge(sig_ready, 2 * KC + m - 1)
                scaled(t3[:, m % 2, :], "gb3", 0, m)
                taps(-(-len(queue) // (8 - m)))
            dve.wait_ge(mean_done, 1)
            for c in range(CT):
                stt(cvo[:, c, :], PS[:, 5, :], -1.0 / CONV, cvo[:, c, :], ALU.mult, ALU.add)\
                    .then_inc(cen_ready, 1)
            dve.wait_ge(croot_ready, 1)
            own.step(dve.reciprocal(cosT[:, :], sinT[:, :]))
            own.wait()
            dve.wait_ge(cen_ready, CT)
            for c in range(CT):
                tt(cvo[:, c, :], cvo[:, c, :], cosT[:, :], ALU.mult).then_inc(cn_ready, 1)
            for c in range(CT):
                dve.wait_ge(chi_ready, c + 1)
                tt(qklo[:, c // 2, c % 2, :], cvo[:, c, :], f32(qkhi[:, c // 2, c % 2, :]),
                   ALU.subtract).then_inc(c_split, 1)
            dve.wait_ge(sig_ready, 3 * KC)
            for m in range(8):
                if m % 2 == 0:
                    done("ao3", 0, m // 2)
                bank, _ = tile_of("ao3", 0, m)
                tt(G[:, m, :], G[:, m, :], PS[:, bank, :], ALU.mult).then_inc(tile_free[bank], 1)
            for q in range(4):
                own.wait()
                for u in range(2):
                    done("gc3", 0, 3 * q + u)
                    if q:
                        dve.wait_ge(a_ready, CT + 2 * q - 1 + u)
                    scaled(t3[:, u, :], "gc3", 0, 4 * q + u)
                done("gc3", 0, 3 * q + 2)
                for u in range(2):
                    m = 2 * q + u
                    dve.wait_ge(sig_ready, 3 * KC + m + 1)
                    bank, before = tile_of("gc3", 0, 4 * q + 2 + u)
                    tt(t3[:, u, :], t3[:, u, :], PS[:, bank, :], ALU.mult).then_inc(tile_free[bank], 1)
                    dve.wait_ge(tile_free[bank], before + 2)
                    tt(G[:, m, :], G[:, m, :], t3[:, u, :], ALU.add).then_inc(a_ready, 1)
                for u in range(2):
                    m = 2 * q + u
                    dve.wait_ge(chi_ready, CT + m + 1)
                    tt(chunks(Blo[1])[:, m, :], G[:, m, :], f32(chunks(Bhi[1])[:, m, :]), ALU.subtract)\
                        .then_inc(c_split, 1)
            residual("out3", "ffn2")
            feed_forward(2)


def slabs_of(inputs):
    out = np.empty((SLABS, P, D), np.float32)
    at = [0]

    def put(a):
        out[at[0]] = a.reshape(P, -1)
        at[0] += 1

    def tiles(w, cols, nk=KC, rows=None):
        w = w[:, cols] if rows is None else w[rows][:, cols]
        w = w.reshape(nk, P, P).transpose(1, 0, 2)
        s = np.zeros((P, KC, P), np.float32)
        s[:, :nk] = w
        put(s)

    def wide(w, cols, slabs):
        w = w[:, cols]
        kk = KC // slabs
        for q in range(slabs):
            put(w[q * kk * P:(q + 1) * kk * P].reshape(kk, P, -1).transpose(1, 0, 2))

    def group(w, nk, per):
        n = w.shape[1] // P
        v = w.reshape(nk, P, n, P).transpose(1, 2, 0, 3)
        for q in range(0, n, per):
            put(v[:, q:q + per])

    col = lambda m, base=0: slice(base + m * P, base + m * P + P)

    def feed(up, down):
        ff = FC * P
        for p, n in enumerate(PARTS):
            for c in range(PART0[p], PART0[p] + n):
                tiles(up, col(c))
                tiles(up, col(c, ff))
            for m in range(KC):
                tiles(down, col(m), n, slice(PART0[p] * P, (PART0[p] + n) * P))

    def layer_tail(l):
        feed(inputs["ffn_w_up"][l], inputs["ffn_w_down"][l])
        group(inputs["ple_w_proj"][l], 2, 4)
        for m in range(KC):
            tiles(inputs["ple_w_gate"][l], col(m))

    w = inputs["diff_w_qkv"][0]
    for h in range(8):
        tiles(w, col(h))
        tiles(w, col(h, D))
        if h == 0:
            for hf in range(2):
                wide(w, slice(2 * D + hf * T, 2 * D + hf * T + T), 4)
    for m in range(KC):
        tiles(inputs["diff_w_o"][0], col(m))
    layer_tail(0)
    pairs = [(j, j + 4) if j < 4 else (j + 4, j + 8) for j in range(8)]
    order = np.concatenate([np.arange(64) + 64 * h for pair in pairs for h in pair])
    w = inputs["swa_w_qkv"][0]
    for m in range(8):
        if m < 2:
            tiles(w, col(m, D))
        tiles(w, order[m * P:m * P + P])
        if m == 0:
            wide(w, slice(1280, 1536), 2)
    for m in range(KC):
        tiles(inputs["swa_w_o"][0][order], col(m))
    layer_tail(1)
    w = inputs["w_in_2"][0]
    for c in range(CT):
        tiles(w, col(c))
        tiles(w, col(c, CONV))
    wide(w, slice(2048, 2560), 4)
    for j in range(4):
        tiles(w, col(j, 1024))
        tiles(w, col(j, 1536))
    for m in range(KC):
        tiles(w, col(m, 3592))
    group(inputs["w_attn_out_2"][0], 4, 2)
    for q in range(4):
        for m in (2 * q, 2 * q + 1):
            tiles(w, col(m, 2568))
        group(inputs["w_conv_out_2"][0][:, 2 * q * P:2 * q * P + 2 * P], 4, 2)
    for m in range(KC):
        tiles(inputs["w_out_2"][0], col(m))
    feed(inputs["w_ffn_in_2"][0], inputs["w_ffn_out_2"][0])
    assert at[0] == SLABS
    return out


def small_parameters(inputs):
    out = np.empty((P, NPAR), np.float32)

    def put(name, a):
        lo, hi = PCOLS[name]
        out[:, lo:hi] = a.reshape(P, hi - lo)

    def columns(v):
        return v.reshape(-1, P).T

    def spread(v):
        return np.broadcast_to(v.reshape(1, -1), (P, v.size))

    for name in ("attn_norm", "ffn_norm", "ple_norm", "final_norm"):
        put(name, columns(inputs[name]))
    put("g_mix", columns(inputs["g_mix_2"]))
    put("g_ffn", columns(inputs["g_ffn_2"]))
    put("subln", columns(inputs["diff_subln"]))
    cw = np.concatenate([inputs["ffn_conv_w"], inputs["ffn_conv_b"][:, None]], axis=1)
    put("conv_w", columns(cw))
    put("sinks", spread(inputs["swa_sinks"]))
    put("b_forget", spread(inputs["b_forget_2"]))
    put("w_dw", columns(inputs["w_dw_2"]))
    put("b_dw", columns(inputs["b_dw_2"]))
    put("g_ln", columns(inputs["g_conv_ln_2"]))
    put("b_ln", columns(inputs["b_conv_ln_2"]))
    put("g_q", np.concatenate([inputs["g_q_2"][0]] * 2)[:, None])
    put("g_k", np.concatenate([inputs["g_k_2"][0]] * 2)[:, None])
    put("w_f", inputs["w_in_2"][0][:, 2560:2568].reshape(KC, P, 8).transpose(1, 0, 2))
    return out


def kernel(**inputs):
    import concourse.bacc as _bacc
    from concourse.bass_utils import run_bass_kernel_spmd as _run

    inputs = {k: np.asarray(v) for k, v in inputs.items()}
    arrays = {
        "xT": np.ascontiguousarray(inputs["x"][0].T.reshape(KC, P, T).transpose(1, 0, 2)),
        "pT": np.ascontiguousarray(
            inputs["p"][:, 0].transpose(0, 2, 1).reshape(2, 2, P, T).transpose(0, 2, 1, 3)),
        "positions": np.ascontiguousarray(np.broadcast_to(inputs["positions"], (P, T))),
        "weights": slabs_of(inputs),
        "parameters": small_parameters(inputs),
        "constants": constants(),
        "lambdas": np.ascontiguousarray(
            np.broadcast_to(inputs["diff_lambda"].reshape(1, 256), (P, 256))),
    }
    nc = _bacc.Bacc("TRN2", target_bir_lowering=False, num_devices=1, dynamic_dma_scratch_size=4096)
    args = [nc.dram_tensor(f"in_{name}", a.shape, mybir.dt.from_np(a.dtype), kind="ExternalInput").ap()
            for name, a in arrays.items()]
    out = nc.dram_tensor("out_0", (P, KC, T), F32, kind="ExternalOutput").ap()
    build(nc, *args, out)
    r = _run(nc, [{f"in_{name}": a for name, a in arrays.items()}], core_ids=[0])
    got = r.results[0]["out_0"]
    return np.ascontiguousarray(got.transpose(2, 1, 0).reshape(1, T, D))
```

```python
from contextlib import ExitStack

import numpy as np

import concourse.bass as bass
from concourse import mybir

ALU = mybir.AluOpType
ACT = mybir.ActivationFunctionType
F32 = mybir.dt.float32
F32R = mybir.dt.float32r
I32 = mybir.dt.int32
AX = mybir.AxisListType.X

P = 128
T = 512
TB = T // P
D = 1024
KC = D // P
FC = 2816 // P
PARTS = (8, 8, 6)
PART0 = (0, 8, 16)
RING = 4
RAWS = 2
BANKS = 7
EPS = 1e-6
TAPS = 31
CONV = 512
CT = CONV // P
PADW = T + TAPS - 1
LAM_INIT = 0.8 - 0.6 * float(np.exp(-0.3 * 0))
QSCALE = 64.0 ** -0.5
NEG = -1e30

STAGES = [("qk1a", 2, 2), ("v1", 8, 8), ("qk1", 14, 14), ("o1", 8, 8)]
for _l in range(3):
    if _l == 1:
        STAGES += [("kq2a", 2, 2), ("v2", 2, 4), ("kq2", 8, 8), ("o2", 8, 8)]
    if _l == 2:
        STAGES += [("a3", 8, 8), ("v3", 4, 4), ("qk3", 8, 8), ("gb3", 8, 8), ("ao3", 4, 8),
                   ("gc3", 12, 16), ("out3", 8, 8)]
    for _p, _n in enumerate(PARTS):
        STAGES += [(f"up{_l}.{_p}", 2 * _n, 2 * _n), (f"down{_l}.{_p}", 8, 8)]
    if _l < 2:
        STAGES += [(f"pp{_l}", 2, 8), (f"gate{_l}", 8, 8)]
STAGE_BANKS = {"qk1a": (4, 5), "v1": (0, 1, 2, 3, 6, 2, 3, 0), "qk1": (1, 0),
               "kq2a": (4, 5), "v2": (2, 3, 6, 0), "kq2": (1, 0, 0, 0, 0, 0, 0, 0),
               "a3": (0, 1, 2, 3, 4, 5), "v3": (2, 3, 4, 5), "qk3": (0, 1)}
SLAB0, BEFORE = {}, {}
_s, _count = 0, [0] * BANKS
for _name, _ns, _nt in STAGES:
    SLAB0[_name] = _s
    BEFORE[_name] = tuple(_count)
    _s = _s + _ns
    _banks = STAGE_BANKS.get(_name, (0, 1, 2, 3))
    for _t in range(_nt):
        _count[_banks[_t % len(_banks)]] += 1
SLABS = _s
assert SLABS % RING == 0

JOIN = ([("gate", m) for m in range(6)] + [("conv", 0), ("gate", 6), ("gate", 7)]
        + [("conv", q) for q in range(1, 4)])
JOIN_SLAB, JOIN_TILE = {}, {}
_t = 0
for _s, _what in enumerate(JOIN):
    JOIN_SLAB[_what], JOIN_TILE[_what] = _s, _t
    _t += 1 if _what[0] == "gate" else 2

PCOLS = {}
_c = 0
for _name, _n in (("attn_norm", 16), ("ffn_norm", 16), ("ple_norm", 16), ("final_norm", 8),
                  ("g_mix", 8), ("g_ffn", 8), ("subln", 1), ("conv_w", 2 * 4 * 2 * FC),
                  ("sinks", 16), ("b_forget", 1), ("w_dw", TAPS * CT), ("b_dw", CT),
                  ("g_ln", CT), ("b_ln", CT), ("g_q", 1), ("g_k", 1), ("w_f", KC * 8)):
    PCOLS[_name] = (_c, _c + _n)
    _c += _n
NPAR = _c
CCOLS = {}
_c = 0
for _name, _n in (("ident", P), ("before", P), ("after", P), ("ones", P), ("heads", P),
                  ("pick", 16), ("minus", 8), ("freq", 1), ("sign", 1)):
    CCOLS[_name] = (_c, _c + _n)
    _c += _n
NCON = _c


def constants():
    c = np.zeros((P, NCON), np.float32)
    i = np.arange(P)

    def put(name, a):
        c[:, CCOLS[name][0]:CCOLS[name][1]] = a

    put("ident", np.eye(P))
    put("before", np.where(i[None, :] >= i[:, None], 0, NEG))
    put("after", np.where(i[None, :] <= i[:, None], 0, NEG))
    put("ones", 1)
    put("heads", i[:, None] // 64 == i[None, :] // 64)
    put("pick", np.arange(16)[None, :] == 7)
    minus = np.zeros((P, 8))
    for h in range(8):
        minus[h, h] = minus[32 + h, h] = -1
    put("minus", minus)
    inv = np.float32(10000.0) ** (-np.arange(0, 64, 2, dtype=np.float32) / np.float32(64))
    put("freq", inv.astype(np.float32)[i % 32][:, None])
    put("sign", np.where(i % 64 < 32, -1, 1)[:, None])
    return c


class Own:

    def __init__(self, eng, sem):
        self.eng, self.sem, self.n = eng, sem, 0

    def step(self, ins):
        ins.then_inc(self.sem, 1)
        self.n = self.n + 1

    def wait(self):
        self.eng.wait_ge(self.sem, self.n)

    def rounds(self, first, end, per, body):
        base = self.n
        if end - first == 1:
            body(first)
        else:
            with self.eng.Fori(first, end) as i:
                self.n = base + (i - first) * per if per else base
                body(i)
        self.n = base + (end - first) * per


def slab_of(stage, i, j):
    s = SLAB0[stage] + j
    return s + 4 * i, s % RING, s // RAWS + (4 // RAWS) * i


def tile_of(stage, i, j):
    banks = STAGE_BANKS.get(stage, (0, 1, 2, 3))
    bank = banks[j % len(banks)]
    earlier = sum(banks[t % len(banks)] == bank for t in range(j))
    return bank, BEFORE[stage][bank] + earlier + i


def build(nc, xT, pT, posd, wts, par, con, lamd, outT):
    ctx = ExitStack()
    with ctx:
        def sb(name, shape, dt=F32):
            return ctx.enter_context(nc.sbuf_tensor(name, shape, dt))

        def sem(name):
            return ctx.enter_context(nc.semaphore(name))

        raw = sb("raw", [P, RAWS, D])
        whi = sb("whi", [P, RING, D], F32R)
        wlo = sb("wlo", [P, RING, D], F32R)
        X = sb("X", [P, KC, T])
        Bhi = [sb(f"Bhi{n}", [P, KC * T], F32R) for n in range(2)]
        Blo = [sb(f"Blo{n}", [P, KC * T], F32R) for n in range(2)]
        qkhi = sb("qkhi", [P, 2, 2, T], F32R)
        qklo = sb("qklo", [P, 2, 2, T], F32R)
        pthi = sb("pthi", [P, 4, T], F32R)
        ptlo = sb("ptlo", [P, 4, T], F32R)
        R = sb("R", [P, T])
        acc = sb("acc", [P, T])
        sq = sb("sq", [P, 2, T])
        cosT = sb("cosT", [P, T])
        sinT = sb("sinT", [P, T])
        AR = sb("AR", [P, 9344])
        par_sb = sb("par_sb", [P, NPAR])
        con_sb = sb("con_sb", [P, NCON])
        constR = sb("constR", [P, 3, P], F32R)
        minusR = sb("minusR", [P, 8, P], F32R)
        cc = sb("cc", [P, T], F32R)
        wfhi = sb("wfhi", [P, KC * 8], F32R)
        wflo = sb("wflo", [P, KC * 8], F32R)
        nmax = sb("nmax", [P, 8])
        nsink = sb("nsink", [P, 16])
        sdiff = sb("sdiff", [P, 4])
        rsum = sb("rsum", [P, 8])
        rinv = sb("rinv", [P, 8])
        rcol = sb("rcol", [P, TB])
        lam = sb("lam", [P, 8])
        gs = sb("gs", [P, 4])
        eps = sb("eps", [P, 1])
        gfm = sb("gfm", [P, KC])
        credit = sb("credit", [P, BANKS + 2])
        PS = ctx.enter_context(nc.psum_tensor("PS", [P, 8, T], F32))

        def chunks(b):
            return b[:, :].rearrange("p (k t) -> p k t", k=KC)

        def ar(off, n=1):
            v = AR[:, off:off + n * T]
            return v.rearrange("p (n t) -> p n t", n=n)

        def cpar(name, k=0, n=1):
            o = PCOLS[name][0]
            return par_sb[:, o + k:o + k + n]

        def gain(name, col, m):
            if name == "both":
                return gfm[:, bass.ds(m, 1)]
            return par_sb[:, bass.ds(PCOLS[name][0] + col + m, 1)]

        def ccon(name, a=0, b=None):
            o, e = CCOLS[name]
            return con_sb[:, o + a:(e if b is None else o + b)]

        def f32(a):
            return a.bitcast(F32)

        conv_w = par_sb[:, PCOLS["conv_w"][0]:PCOLS["conv_w"][1]]\
            .rearrange("p (l t u c) -> p l t u c", l=2, t=4, u=2)
        identR, beforeR, afterR = constR[:, 0, :], constR[:, 1, :], constR[:, 2, :]
        ident = f32(identR)
        ones = ccon("ones")

        rC, rS = ar(0)[:, 0, :], ar(512)[:, 0, :]
        swap, qraw = ar(1024, 2), ar(2048, 2)
        prob = ar(3072, 4)
        OA = ar(5120, 8)
        us, cv, av = ar(0, 4), ar(2048, 4), ar(4096, 2)
        PT = ar(8192, 2)
        gt, gu, pp = ar(0, 2), ar(1024, 2), ar(4096, 8)
        atmp, prob3, qraw3, OA3 = ar(0, 6), ar(0, 4), ar(2048, 2), ar(3072, 4)
        G, t3, t6 = ar(0, 8), ar(4096, 2), ar(4096, 6)
        apad = AR[:, 5120:5120 + CT * PADW].rearrange("p (c t) -> p c t", c=CT)
        cvo = ar(7296, 4)
        frow = AR[0:8, 3072:3072 + 3 * T].rearrange("p (n t) -> p n t", n=3)
        angs = ar(0, 6)

        raw_ready = [sem(f"raw_ready{n}") for n in range(RAWS)]
        hi_ready = sem("hi_ready")
        lo_ready = sem("lo_ready")
        slab_done = sem("slab_done")
        tile_free = [sem(f"tile_free{n}") for n in range(BANKS)]
        par_in, con_in, pos_in, lam_in, p_in = (
            sem("par_in"), sem("con_in"), sem("pos_in"), sem("lam_in"), sem("p_in"))
        x_in = [sem(f"x_in{n}") for n in range(4)]
        consts_ready = sem("consts_ready")
        trig_ready = sem("trig_ready")
        sq_ready, sq_used = sem("sq_ready"), sem("sq_used")
        xhi_ready, x_split = sem("xhi_ready"), sem("x_split")
        ss_done, root_ready, r_ready = sem("ss_done"), sem("root_ready"), sem("r_ready")
        rcol_done, rcol_ready = sem("rcol_done"), sem("rcol_ready")
        vhi_ready, pad_ready = sem("vhi_ready"), sem("pad_ready")
        swap_ready, rope_ready, qhi_ready, q_ready = (
            sem("swap_ready"), sem("rope_ready"), sem("qhi_ready"), sem("q_ready"))
        score_done, max_ready, exp_ready, prob_ready = (
            sem("score_done"), sem("max_ready"), sem("exp_ready"), sem("prob_ready"))
        trans_done, pthi_ready, pt_ready, pv_done, o_ready = (
            sem("trans_done"), sem("pthi_ready"), sem("pt_ready"), sem("pv_done"), sem("o_ready"))
        osq_ready, osum_done, oroot_ready, orinv_ready = (
            sem("osq_ready"), sem("osum_done"), sem("oroot_ready"), sem("orinv_ready"))
        obc_done, onorm_ready, ohi_ready, o_split = (
            sem("obc_done"), sem("onorm_ready"), sem("ohi_ready"), sem("o_split"))
        mid_ready, conv_done, silu_ready, act_ready, ahi_ready, act_split = (
            sem("mid_ready"), sem("conv_done"), sem("silu_ready"), sem("act_ready"),
            sem("ahi_ready"), sem("act_split"))
        phi_ready, p_split = sem("phi_ready"), sem("p_split")
        sig_ready = sem("sig_ready")
        sdiff_ready, sink_ready = sem("sdiff_ready"), sem("sink_ready")
        ple_added = sem("ple_added")
        y_ready = sem("y_ready")
        asig_ready, a_ready, taps_done = sem("asig_ready"), sem("a_ready"), sem("taps_done")
        mean_done, cen_ready, csq_ready, var_done, croot_ready, cn_ready = (
            sem("mean_done"), sem("cen_ready"), sem("csq_ready"), sem("var_done"),
            sem("croot_ready"), sem("cn_ready"))
        chi_ready, c_split = sem("chi_ready"), sem("c_split")
        f_done, f_lin, f_exp, cum_ready, cchi_ready, cc_ready = (
            sem("f_done"), sem("f_lin"), sem("f_exp"), sem("cum_ready"), sem("cchi_ready"),
            sem("cc_ready"))
        hsum_done, hsq_ready, hroot_ready = sem("hsum_done"), sem("hsq_ready"), sem("hroot_ready")
        dve_tap = [sem(f"dve_tap{c}") for c in range(CT)]
        dve_step, act_step = sem("dve_step"), sem("act_step")
        out_stored = sem("out_stored")
        block = ctx.enter_context(nc.Block())

        NORMS = ["attn0", "ffn0", "ple0", "attn1", "ffn1", "ple1", "final", "mix", "ffn2"]
        SPLITS = [n for n in NORMS if n != "mix"]
        GAIN = {"attn0": ("attn_norm", 0), "attn1": ("attn_norm", 8), "ffn0": ("ffn_norm", 0),
                "ffn1": ("ffn_norm", 8), "ple0": ("ple_norm", 0), "ple1": ("ple_norm", 8),
                "final": ("both", 0), "ffn2": ("g_ffn", 0)}
        BUF = {"attn0": 0, "ffn0": 1, "ple0": 1, "attn1": 0, "ffn1": 1, "ple1": 1, "final": 0, "ffn2": 0}
        TAPS_A_TILE = 8
        ABUF = {0: 0, 1: 0, 2: 1}

        PAIRS = {1: 8, 2: 8, 3: 4}

        def padded(stage, B, src, t):
            nh = 4 if stage == "v2" else 8
            v = B[1][:, 0:TB * nh * P].rearrange("p (k n c) -> p k n c", k=TB, n=nh)[:, t]
            v = v.rearrange("p (n two) c -> p n two c", two=2)
            s = src.rearrange("p (n two c) -> p n two c", two=2, c=64)
            return [(v[:, :, u, 64 * u:64 * u + 64], s[:, :, u, :]) for u in range(2)]

        def band(kind, qb):
            if kind == 1:
                return 0, TB, []
            if kind == 2:
                lo, hi = max(qb - 1, 0), min(qb + 1, TB - 1)
                masks = [(qb - 1 - lo, beforeR)] * (qb > 0) + [(qb + 1 - lo, afterR)] * (qb < TB - 1)
                return lo, hi - lo + 1, masks
            return 0, qb + 1, [(qb, afterR)]

        SC0 = {1: 0, 2: 64, 3: 128}
        PB0 = {1: 0, 2: 32, 3: 96}
        GROUP = {1: 4, 2: 2, 3: 2}
        PV0 = {1: 0, 2: 8, 3: 24}
        OP0 = {1: 0, 2: 8, 3: 16}
        QT0 = {1: 0, 2: 16, 3: 26}

        def piece(kind, g):
            first = 7 if kind == 1 else 8
            p, r = (g + first) // 4, (g + first) % 4
            t, part, parts = {1: (2 * p - 2 + r // 2, r % 2, 2), 2: (p, r - 1, 3),
                              3: (2 * p + r // 2, r % 2, 2)}[kind]
            return (t, part, parts) if t < NPROJ[kind] and part >= 0 else None

        PROJ = {1: "qk1", 2: "kq2", 3: "qk3"}
        AHEAD = {1: 1, 2: 2, 3: 1}
        HP = {1: 1, 2: 2, 3: 2}
        OFIRST = 6
        SPREAD = {28: (0, 1), 29: (2, 3), 30: (4, 5)}
        OSPLIT = {29: (0, 1, 2), 30: (3, 4), 31: (5, 6)}
        BEGUN = {1: {}, 2: {-2: 0, -1: 1}, 3: {-2: 2, -1: 3}}
        NPROJ = {1: 14, 2: 8, 3: 8}

        def score_bank(kind, n):
            return (4, 5)[n % 2] if kind == 1 else \
                (4, 5, 6, 1)[n % 4] if kind == 2 else (4, 5, 6)[(n - SC0[3]) % 3]

        def spread_bank(h):
            return h % 2 + (0 if h < OFIRST else 4)

        def finished(kind, g):
            if g < 0:
                return BEGUN[kind].get(g)
            p = piece(kind, g)
            return p[0] if p and p[1] == p[2] - 1 else None

        def probs(kind):
            return prob3 if kind == 3 else prob

        def place_of(kind, t):
            if kind == 1:
                return t + 2, (t // 2 + 1) % 2, t % 2
            if kind == 2:
                return QT0[2] + 2 + t, t % 2 if t else 1, 0 if t else 1
            return QT0[3] + t, (t // 2) % 2, t % 2

        def transposed(buf, kind, g, s):
            qb = g % 4
            first, nb, _ = band(kind, qb)
            if kind == 1:
                return buf[:, :, qb * P:qb * P + P]
            k0 = 4 * s + first - band(kind, qb - qb % 2)[0]
            c = qb % 2 * P
            return buf.rearrange("p a (b c) -> p (a b) c", c=2 * P)[:, k0:k0 + nb, c:c + P]

        def head_of(j, s):
            return (j if j < 4 else j + 4) + 4 * s

        @block.sync
        def _(sp):
            def load(s, slot, freed):
                if freed is not None:
                    sp.wait_ge(lo_ready, freed)
                sp.dma_start(raw[:, slot, :], wts[s]).then_inc(raw_ready[slot], 16)

            for s in range(4):
                load(s, s % RAWS, s - 1 if s >= RAWS else None)
            with sp.Fori(1, SLABS // 4) as i:
                for j in range(4):
                    load(4 * i + j, j % RAWS, 4 * i + j - 1)
            for m in range(KC):
                bank, before = tile_of("down2.2", m // 4, m % 4)
                sp.wait_ge(tile_free[bank], before + 2)
                sp.dma_start(outT[:, m, :], X[:, m, :]).then_inc(out_stored, 16)
            sp.wait_ge(out_stored, 16 * KC)

        @block.gpsimd
        def _(pool):
            with pool.Fori(0, SLABS // 4) as i:
                for j in range(4):
                    pool.wait_ge(hi_ready, 4 * i + j + 1)
                    pool.tensor_tensor(wlo[:, j, :], raw[:, j % RAWS, :], f32(whi[:, j, :]),
                                       ALU.subtract).then_inc(lo_ready, 1)

        @block.tensor
        def _(pe):
            def mm(out, w, x, start, stop):
                return pe.matmul(out, w, x, start=start, stop=stop)

            def mm3(out, ahi, alo, bhi, blo, start, stop):
                mm(out, ahi, bhi, start, False)
                mm(out, ahi, blo, False, False)
                return mm(out, alo, bhi, False, stop)

            def weights(s):
                pe.wait_ge(lo_ready, s + 1)

            def open_tile(stage, i, j):
                bank, before = tile_of(stage, i, j)
                pe.wait_ge(tile_free[bank], before + 1)
                return PS[:, bank, :]

            def tile(stage, i, j, hi, lo, nk, ready=None):
                s, slot, _ = slab_of(stage, i, j)
                weights(s)
                out = open_tile(stage, i, j)
                for k in range(nk):
                    if ready is not None:
                        pe.wait_ge(ready[0], ready[1] + k + 1)
                    last = mm3(out, whi[:, slot, k * P:k * P + P], wlo[:, slot, k * P:k * P + P],
                               hi[:, k, :], lo[:, k, :], k == 0, k == nk - 1)
                last.then_inc(slab_done, 1)

            def norm_sum(norm):
                pe.wait_ge(sq_used, KC * (NORMS.index(norm) + 1))
                mm(PS[:, 7, :], ones, acc[:, :], True, True).then_inc(ss_done, 1)

            def tiles(stage, n, hi, lo, nk, ready, norm=None, lead=2, late=1,
                      meanwhile=None):
                if ready is None:
                    lead = 0
                outs = []
                for ks in (range(nk - late), range(nk - late, nk)):
                    for j in range(lead):
                        s, slot, _ = slab_of(stage, 0, j)
                        if len(outs) < lead:
                            weights(s)
                            outs.append(open_tile(stage, 0, j))
                        for k in ks:
                            if j == 0:
                                pe.wait_ge(ready[0], ready[1] + k + 1)
                            last = mm3(outs[j], whi[:, slot, k * P:k * P + P],
                                       wlo[:, slot, k * P:k * P + P],
                                       hi[:, k, :], lo[:, k, :], k == 0, k == nk - 1)
                        if ks[-1] == nk - 1:
                            last.then_inc(slab_done, 1)
                    if ks[0] == 0 and meanwhile:
                        meanwhile()
                if norm:
                    norm_sum(norm)
                for j in range(lead, 4):
                    tile(stage, 0, j, hi, lo, nk)
                if n > 8:
                    with pe.Fori(1, n // 4) as i:
                        for j in range(4):
                            tile(stage, i, j, hi, lo, nk)
                elif n > 4:
                    for j in range(4):
                        tile(stage, 1, j, hi, lo, nk)

            def split_of(norm):
                b = BUF[norm]
                return chunks(Bhi[b]), chunks(Blo[b]), (x_split, KC * SPLITS.index(norm))

            def values(stage, norm, slabs, width, parts, half=0, tell=True):
                hi, lo, _ = split_of(norm)
                kk = KC // slabs
                for q in parts:
                    s, slot, _ = slab_of(stage, 0, half * slabs + q)
                    weights(s)
                    for t in range(TB):
                        if q == 0:
                            open_tile(stage, 0, half * TB + t)
                        out = PS[:, tile_of(stage, 0, half * TB + t)[0], 0:width]
                        for k in range(q * kk, q * kk + kk):
                            c = (k - q * kk) * width
                            tk = slice(t * P, t * P + P)
                            w, v = whi[:, slot, c:c + width], wlo[:, slot, c:c + width]
                            last = mm3(out, hi[:, k, tk], lo[:, k, tk], w, v, k == 0, k == KC - 1)
                    if tell:
                        last.then_inc(slab_done, 1)

            def row_to_column():
                row_to_column.n += 1
                pe.wait_ge(r_ready, row_to_column.norms[row_to_column.n - 1] + 1)
                for t in range(TB):
                    last = mm(PS[:, 7, t:t + 1], R[0:1, t * P:t * P + P], ones[0:1, 0:1], True, True)
                last.then_inc(rcol_done, 1)
            row_to_column.n = 0
            row_to_column.norms = [NORMS.index(n) for n in ("attn0", "attn1", "mix")]

            def project_qk(stage, norm, t, part=0, parts=1):
                hi, lo, _ = split_of(norm)
                s, slot, _ = slab_of(stage, 0, t)
                out = PS[:, tile_of(stage, 0, t)[0], :]
                if part == 0:
                    weights(s)
                    open_tile(stage, 0, t)
                for k in range(part * KC // parts, (part + 1) * KC // parts):
                    last = mm3(out, whi[:, slot, k * P:k * P + P], wlo[:, slot, k * P:k * P + P],
                               hi[:, k, :], lo[:, k, :], k == 0, k == KC - 1)
                if part == parts - 1:
                    last.then_inc(slab_done, 1)

            def first_pair(stage, norm, meanwhile=None):
                hi, lo, ready = split_of(norm)
                for k in range(KC):
                    if k == KC - 1 and meanwhile:
                        meanwhile()
                    pe.wait_ge(ready[0], ready[1] + k + 1)
                    for t in range(2):
                        s, slot, _ = slab_of(stage, 0, t)
                        if k == 0:
                            weights(s)
                            open_tile(stage, 0, t)
                        c = slice(k * P, k * P + P)
                        last = mm3(PS[:, tile_of(stage, 0, t)[0], :], whi[:, slot, c],
                                   wlo[:, slot, c], hi[:, k, :], lo[:, k, :], k == 0, k == KC - 1)
                        if k == KC - 1:
                            last.then_inc(slab_done, 1 + (t == 1 and meanwhile is not None))

            def all_values(kind):
                stage = f"v{kind}"
                for t in range(4, 8) if kind == 1 else range(4):
                    bank, before = tile_of(stage, 0, t)
                    pe.wait_ge(tile_free[bank], before + 2)

            def scores(kind, g):
                j, qb = g // 4, g % 4
                b = j % 2
                kb = j // 4 if kind == 2 else b
                first, nb, masks = band(kind, qb)
                if g == 0 and kind > 1:
                    all_values(kind)
                if qb == 0:
                    pe.wait_ge(q_ready, QT0[kind] + {1: 2 * j + 2, 2: 2 if j == 0 else j + 3,
                                                     3: 2 * j + 2}[kind])
                    if kind == 3 and j == 0:
                        pe.wait_ge(cc_ready, 1)
                for s in range(2):
                    n = SC0[kind] + 2 * g + s
                    back = {1: 2, 2: 4, 3: 3}[kind]
                    if n >= back:
                        pe.wait_ge(exp_ready, n - back + 1)
                    if kind == 2 and g == 1 and s == 1:
                        bank, before = tile_of("kq2", 0, 0)
                        pe.wait_ge(tile_free[bank], before + 2)
                    rows, cols = slice(64 * s, 64 * s + 64), slice(qb * P, qb * P + P)
                    keys = slice(first * P, (first + nb) * P)
                    out = PS[:, score_bank(kind, n), 0:nb * P]
                    last = mm3(out, qkhi[rows, b, 0, cols], qklo[rows, b, 0, cols],
                               qkhi[rows, kb, 1, keys], qklo[rows, kb, 1, keys], True, kind == 1)
                    if kind == 3:
                        mm(out, minusR[:, 2 * j + s, :], cc[:, keys], False, False)
                    for q, (at, mask) in enumerate(masks):
                        last = mm(out[:, at * P:at * P + P], identR, mask, False, q == len(masks) - 1)
                    last.then_inc(score_done, 1)

            def transposes(kind, g):
                nb = band(kind, g % 4)[1]
                if g == 0 and kind == 1:
                    all_values(1)
                for s in range(HP[kind]):
                    n = PB0[kind] + HP[kind] * g + s
                    pe.wait_ge(prob_ready, n + 1)
                    if n >= 2:
                        pe.wait_ge(pt_ready, n - 1)
                    source = probs(kind)[:, 2 * (g % 2) + (1 if kind == 1 else s), :]
                    for k in range(nb):
                        last = pe.transpose(PS[:, 2 + n % 2, k * P:k * P + P],
                                            source[:, k * P:k * P + P], ident)
                    last.then_inc(trans_done, 1)

            def outputs(kind, g):
                j, last_qb = g // 4, g % 4
                heads = HP[kind]
                pe.wait_ge(pt_ready, PB0[kind] + heads * (g + 1))
                if last_qb == GROUP[kind] - 1 and OP0[kind] + j:
                    pe.wait_ge(o_ready, OP0[kind] + j)
                nh = {1: 8, 2: 4, 3: 8}[kind]
                vhi = Bhi[1][:, 0:TB * nh * P].rearrange("p (k n c) -> p k n c", k=TB, n=nh)
                vlo = Blo[1][:, 0:TB * nh * P].rearrange("p (k n c) -> p k n c", k=TB, n=nh)
                if kind == 1:
                    work = [(k, 0, TB, 0) for k in range(TB)]
                else:
                    q0 = last_qb - 1
                    spans = []
                    for k in range(TB):
                        qs = [q for q in (q0, last_qb)
                              if band(kind, q)[0] <= k < band(kind, q)[0] + band(kind, q)[1]]
                        if qs:
                            spans.append((len(qs) == 2, k, qs[0], qs[-1] + 1))
                    spans.sort(reverse=True)
                    work = [(k, a, b, 0) for _, k, a, b in spans]
                    work += [(k, a, b, 1) for _, k, a, b in reversed(spans)]
                for n, (k, a, b, s) in enumerate(work):
                    head = {1: j, 2: 2 * (j // 4) + s, 3: 2 * j + s}[kind]
                    if kind == 1:
                        xs = [buf[:, k, :] for buf in (pthi, ptlo)]
                    else:
                        row = 4 * s + k - band(kind, q0)[0]
                        xs = [buf[:, row // 2, (row % 2) * 2 * P + (a - q0) * P:
                                  (row % 2) * 2 * P + (b - q0) * P] for buf in (pthi, ptlo)]
                    last = mm3(PS[:, 7, a * P:b * P], vhi[:, k, head, :], vlo[:, k, head, :],
                               xs[0], xs[1], n == 0, n == len(work) - 1)
                last.then_inc(pv_done, 1)

            def output_squares(h):
                if h == OFIRST:
                    pe.wait_ge(oroot_ready, 1)
                pe.wait_ge(osq_ready, h + 1)
                mm(PS[0:8, 6, :], ccon("pick", 7 - h, 15 - h), sq[:, h % 2, :],
                   h in (0, OFIRST), h in (OFIRST - 1, 7)).then_inc(osum_done, 1)

            def spread_factor(h):
                pe.wait_ge(orinv_ready, 1 if h < OFIRST else 2)
                if h >= 2:
                    pe.wait_ge(onorm_ready, h - 1)
                row = CCOLS["ident"][0] + h
                mm(PS[:, spread_bank(h), :], con_sb[0:8, row:row + 1].broadcast_to((8, P)),
                   (R if h < OFIRST else acc)[0:8, :], True, True).then_inc(obc_done, 1)

            def attention(kind, norm, begin):
                steps = 4 * PAIRS[kind]
                if kind == 1:
                    scores(kind, 0)
                for t, part, parts in begin:
                    project_qk(PROJ[kind], norm, t, part, parts)
                if kind > 1:
                    scores(kind, 0)
                if kind == 2:
                    scores(kind, 1)
                if kind == 3:
                    head_sums(2)
                for g in range(steps):
                    if g + AHEAD[kind] < steps:
                        scores(kind, g + AHEAD[kind])
                    if piece(kind, g):
                        project_qk(PROJ[kind], norm, *piece(kind, g))
                    if kind == 1:
                        if g % 4 == 1 and g > 4:
                            output_squares(g // 4 - 1)
                        for h in SPREAD.get(g, ()):
                            spread_factor(h)
                    transposes(kind, g)
                    if g and g % GROUP[kind] == 0:
                        outputs(kind, g - 1)
                    if kind == 3 and finished(kind, g - 1) is not None:
                        head_sums(finished(kind, g - 1))
                outputs(kind, steps - 1)

            def head_sums(t):
                bank, before = tile_of("qk3", 0, t)
                pe.wait_ge(hsq_ready, t + 1)
                mm(PS[:, bank, :], ccon("heads"), sq[:, t % 2, :], True, True).then_inc(hsum_done, 1)

            def feed_forward(l):
                norm = f"ffn{l}"
                hi, lo, ready = split_of(norm)
                ab = ABUF[l]
                for p, n in enumerate(PARTS):
                    tiles(f"up{l}.{p}", 2 * n, hi, lo, KC, ready if p == 0 else None,
                          norm if p == 0 else None)
                    tiles(f"down{l}.{p}", KC, chunks(Bhi[ab]), chunks(Blo[ab]), n,
                          (act_split, l * FC + PART0[p]))

            def embedding(l):
                stage = f"pp{l}"
                pe.wait_ge(p_split, 2 * l + 2)
                for q in range(2):
                    s, slot, _ = slab_of(stage, 0, q)
                    weights(s)
                    for m in range(4):
                        out = open_tile(stage, 0, 4 * q + m)
                        for k in range(2):
                            c = (2 * m + k) * P
                            last = mm3(out, whi[:, slot, c:c + P], wlo[:, slot, c:c + P],
                                       qkhi[:, 0, k, :], qklo[:, 0, k, :], k == 0, k == 1)
                    last.then_inc(slab_done, 1)
                hi, lo, ready = split_of(f"ple{l}")
                tiles(f"gate{l}", KC, hi, lo, KC, ready, f"ple{l}")

            first_pair("qk1a", "attn0")
            pe.wait_ge(consts_ready, 3)
            values("v1", "attn0", 4, T, (0,))
            norm_sum("attn0")
            values("v1", "attn0", 4, T, (1, 2))
            row_to_column()
            values("v1", "attn0", 4, T, (3,))
            values("v1", "attn0", 4, T, range(4), half=1)
            attention(1, "attn0", ((0, 0, 1), (1, 0, 2)))
            output_squares(7)
            tiles("o1", KC, chunks(Bhi[0]), chunks(Blo[0]), KC, (o_split, 0), lead=3,
                  late=8 - OFIRST, meanwhile=lambda: [spread_factor(h) for h in range(OFIRST, 8)])
            feed_forward(0)
            embedding(0)
            first_pair("kq2a", "attn1", lambda: values("v2", "attn1", 2, 256, (0,), tell=False))
            norm_sum("attn1")
            values("v2", "attn1", 2, 256, (1,))
            project_qk("kq2", "attn1", 0)
            row_to_column()
            attention(2, "attn1", ((1, 0, 1),))
            tiles("o2", KC, chunks(Bhi[0]), chunks(Blo[0]), KC, (o_split, 8))
            feed_forward(1)
            embedding(1)
            hi, lo, ready = split_of("final")
            tiles("a3", 4, hi, lo, KC, ready, "final", lead=3)
            for t in range(4, 8):
                tile("a3", 0, t, hi, lo, KC)
                if t == 5:
                    norm_sum("mix")
            row_to_column()
            values("v3", "final", 4, T, range(4))
            pe.wait_ge(p_split, 5)
            pe.wait_ge(tile_free[6], 3)
            for k in range(KC):
                last = mm3(PS[0:8, 6, :], wfhi[:, 8 * k:8 * k + 8], wflo[:, 8 * k:8 * k + 8],
                           hi[:, k, :], lo[:, k, :], k == 0, k == KC - 1)
            last.then_inc(f_done, 1)
            for t in range(2):
                project_qk("qk3", "final", t)
            head_sums(0)
            project_qk("qk3", "final", 2)
            head_sums(1)
            attention(3, "final", ((3, 0, 2), (3, 1, 2)))
            tiles("gb3", 8, hi, lo, KC, None)
            def mean():
                for c in range(CT):
                    pe.wait_ge(taps_done, c + 1)
                    last = mm(PS[:, 5, :], ones, cvo[:, c, :], c == 0, c == CT - 1)
                last.then_inc(mean_done, 1)

            def variance():
                for c in range(CT):
                    pe.wait_ge(csq_ready, c + 1)
                    last = mm(PS[:, 6, :], ones, sq[:, c % 2, :], c == 0, c == CT - 1)
                    last.then_inc(var_done, 1)

            def two_tiles(stage, s, slot, first, xhi, xlo):
                weights(s)
                for m in range(2):
                    out = open_tile(stage, 0, first + m)
                    for k in range(4):
                        c = (4 * m + k) * P
                        last = mm3(out, whi[:, slot, c:c + P], wlo[:, slot, c:c + P],
                                   xhi(k), xlo(k), k == 0, k == 3)
                last.then_inc(slab_done, 1)
            pe.wait_ge(o_split, 20)
            for q in range(4):
                s, slot, _ = slab_of("ao3", 0, q)
                two_tiles("ao3", s, slot, 2 * q, lambda k: pthi[:, k, :], lambda k: ptlo[:, k, :])
            for what, n in JOIN:
                s, slot, _ = slab_of("gc3", 0, JOIN_SLAB[what, n])
                first = JOIN_TILE[what, n]
                if what == "gate":
                    weights(s)
                    out = open_tile("gc3", 0, first)
                    for k in range(KC):
                        c = slice(k * P, k * P + P)
                        last = mm3(out, whi[:, slot, c], wlo[:, slot, c], hi[:, k, :], lo[:, k, :],
                                   k == 0, k == KC - 1)
                    last.then_inc(slab_done, 1)
                else:
                    if n == 0:
                        pe.wait_ge(c_split, CT)
                    two_tiles("gc3", s, slot, first, lambda k: qkhi[:, k // 2, k % 2, :],
                              lambda k: qklo[:, k // 2, k % 2, :])
                if (what, n) == ("gate", 1):
                    mean()
                if (what, n) == ("gate", 3):
                    variance()
            tiles("out3", 8, chunks(Bhi[1]), chunks(Blo[1]), KC, (c_split, CT))
            feed_forward(2)

        @block.scalar
        def _(act):
            own = Own(act, act_step)

            def high(s, slot, half):
                act.wait_ge(raw_ready[slot % RAWS], 16 * half + 16)
                act.activation(whi[:, slot, :], raw[:, slot % RAWS, :], ACT.Copy)\
                   .then_inc(hi_ready, 1)

            def used(stage, i, j, more=True):
                s, slot, half = slab_of(stage, i, j)
                act.wait_ge(slab_done, s + 1)
                if more:
                    high(s + RING, slot, half + RING // RAWS)

            def freed(stage, i, j):
                bank, before = tile_of(stage, i, j)
                act.wait_ge(tile_free[bank], before + 2)

            def square_and_high(norm, m, slot):
                n = NORMS.index(norm)
                c = KC * n + m
                if norm in GAIN:
                    name, col = GAIN[norm]
                    act.activation(chunks(Bhi[BUF[norm]])[:, m, :], X[:, m, :], ACT.Copy,
                                   scale=gain(name, col, m)).then_inc(xhi_ready, 1)
                if not (n == 0 and m < 2):
                    act.wait_ge(sq_used, c - 1)
                act.activation(sq[:, slot, :], X[:, m, :], ACT.Square).then_inc(sq_ready, 1)

            def root(norm):
                n = NORMS.index(norm)
                act.wait_ge(ss_done, n + 1)
                act.activation(sq[:, 0, :], PS[:, 7, :], ACT.Sqrt, scale=1.0 / D, bias=eps[:, 0:1])\
                   .then_inc(root_ready, 1)

            def rounds(n, body):
                if n == 1:
                    body(0)
                elif n == 2:
                    body(0)
                    body(1)
                else:
                    with act.Fori(0, n) as i:
                        body(i)

            def residual(stage, norm, last=False):
                if norm:
                    act.wait_ge(r_ready, NORMS.index(norm))

                def body(i):
                    for j in range(4):
                        used(stage, i, j, not (last and i == 1))
                        if norm:
                            freed(stage, i, j)
                            square_and_high(norm, 4 * i + j, j % 2)
                rounds(2, body)

            def values(stage, halves, slabs, width):
                for hf in range(halves):
                    for q in range(slabs):
                        used(stage, 0, hf * slabs + q)
                    if hf == 0:
                        act.wait_ge(rcol_ready, int(stage[1]))
                        if stage != "v1":
                            act.wait_ge(pad_ready, {"v2": 4, "v3": 8}[stage])
                    for t in range(TB):
                        bank, _ = tile_of(stage, 0, hf * TB + t)
                        if stage == "v1":
                            outs = [(Bhi[1][:, :].rearrange("p (k n) -> p k n", k=TB)
                                     [:, t, hf * T:hf * T + T], PS[:, bank, :])]
                        else:
                            outs = padded(stage, Bhi, PS[:, bank, 0:width], t)
                        for out, src in outs:
                            last = act.activation(out, src, ACT.Copy, scale=rcol[:, t:t + 1])
                        last.then_inc(vhi_ready, 1)
                    if stage == "v1" and hf == 0:
                        for t in range(2):
                            swap_halves("qk1a", t, t)
                        for t in range(2):
                            q_high(t, 0, t)

            def swap_halves(stage, t, n):
                if stage not in ("qk1a", "kq2a"):
                    used(stage, 0, t)
                bank, _ = tile_of(stage, 0, t)
                if n >= 2:
                    act.wait_ge(rope_ready, n - 1)
                for to, of in ((0, 32), (32, 0), (64, 96), (96, 64)):
                    last = act.activation(swap[to:to + 32, n % 2, :], PS[of:of + 32, bank, :], ACT.Copy)
                last.then_inc(swap_ready, 1)

            def q_high(n, b, which):
                act.wait_ge(rope_ready, n + 1)
                act.activation(qkhi[:, b, which, :], qraw[:, n % 2, :], ACT.Copy,
                               scale=(QSCALE, 1.0)[which]).then_inc(qhi_ready, 1)

            def exps(kind, g):
                for s in range(2):
                    n = SC0[kind] + 2 * g + s
                    nb = band(kind, g % 4)[1]
                    act.wait_ge(max_ready, n + 1)
                    if g >= 2:
                        act.wait_ge(trans_done, PB0[kind] + HP[kind] * (g - 2)
                                    + (s + 1 if HP[kind] == 2 else 1))
                    act.activation(probs(kind)[:, 2 * (g % 2) + s, 0:nb * P],
                                   PS[:, score_bank(kind, n), 0:nb * P], ACT.Exp,
                                   bias=nmax[:, n % 4:n % 4 + 1], accum_out=rsum[:, n % 4:n % 4 + 1])\
                       .then_inc(exp_ready, 1)
                if kind == 2:
                    c = (SC0[2] + 2 * g) % 4
                    act.wait_ge(sdiff_ready, g + 1)
                    act.activation(rsum[:, 4 + c:6 + c], sdiff[:, c:c + 2], ACT.Exp)\
                       .then_inc(sink_ready, 1)

            def prob_high(kind, g):
                blocks = band(kind, g % 4)[1]
                for s in range(HP[kind]):
                    n = PB0[kind] + HP[kind] * g + s
                    act.wait_ge(trans_done, n + 1)
                    if PV0[kind] + g // GROUP[kind]:
                        act.wait_ge(pv_done, PV0[kind] + g // GROUP[kind])
                    act.activation(transposed(pthi, kind, g, s), PS[:, 2 + n % 2, 0:blocks * P]
                                   .rearrange("p (k q) -> p k q", k=blocks), ACT.Copy)\
                       .then_inc(pthi_ready, 1)

            def evacuate(kind, j):
                act.wait_ge(pv_done, PV0[kind] + (j + 1) * (4 // GROUP[kind]))
                act.activation((OA3 if kind == 3 else OA)[:, j, :], PS[:, 7, :], ACT.Copy)\
                   .then_inc(o_ready, 1)

            def output_square(h):
                act.wait_ge(o_ready, h + 1)
                if h >= 2:
                    act.wait_ge(osum_done, h - 1)
                act.activation(sq[:, h % 2, :], OA[:, h, :], ACT.Square).then_inc(osq_ready, 1)

            def output_root(last):
                act.wait_ge(osum_done, 8 if last else OFIRST)
                if last:
                    act.wait_ge(orinv_ready, 1)
                act.activation(acc[0:8, :], PS[0:8, 6, :], ACT.Sqrt, scale=1.0 / P,
                               bias=eps[0:8, 0:1]).then_inc(oroot_ready, 1)

            def normed_high(h):
                act.wait_ge(onorm_ready, h + 1)
                act.activation(chunks(Bhi[0])[:, h, :], OA[:, h, :], ACT.Copy, scale=gs[:, 0:1])\
                   .then_inc(ohi_ready, 1)

            def attention(kind):
                steps = 4 * PAIRS[kind]
                exps(kind, 0)
                if kind == 3:
                    used("qk3", 0, 3)
                    head_root(2)
                for g in range(steps):
                    begun, halfway = finished(kind, g - 1), finished(kind, g - 2)
                    if g + 1 < steps:
                        exps(kind, g + 1)
                    if kind == 3 and begun is not None:
                        head_square(begun)
                    if kind == 3 and halfway is not None:
                        head_high(halfway)
                    prob_high(kind, g)
                    if kind < 3 and begun is not None:
                        q_high(*place_of(kind, begun))
                    if kind == 2:
                        for c in OSPLIT.get(g, ()):
                            output_high(OA, c)
                    if g % 4 == 0 and g:
                        evacuate(kind, g // 4 - 1)
                        if kind == 1:
                            output_square(g // 4 - 1)
                    if kind == 1:
                        for h in SPREAD.get(g, ()):
                            normed_high(h)
                        if g == 4 * OFIRST + 1:
                            output_root(False)
                    if kind == 3 and begun is not None:
                        head_root(begun)
                    done = finished(kind, g)
                    if done is not None and kind < 3:
                        swap_halves(PROJ[kind], done, place_of(kind, done)[0])
                    if done is not None and kind == 3:
                        used("qk3", 0, done)
                evacuate(kind, PAIRS[kind] - 1)

            def output_high(src, c):
                hi = pthi[:, c, :] if src is OA3 else chunks(Bhi[0])[:, c, :]
                act.wait_ge(o_ready, (OP0[3] if src is OA3 else OP0[2]) + c + 1)
                act.activation(hi, src[:, c, :], ACT.Copy).then_inc(ohi_ready, 1)

            def feed_forward(l, last=False):
                root(f"ffn{l}")
                n0 = l * FC
                for p, n in enumerate(PARTS):
                    stage = f"up{l}.{p}"

                    def body(i):
                        for pair in range(2):
                            q = PART0[p] + 2 * i + pair
                            for u in range(2):
                                used(stage, i, 2 * pair + u)
                                if l < 2:
                                    freed(stage, i, 2 * pair + u)
                                    act.activation(cv[:, 2 * pair + u, :], us[:, 2 * pair + u, :],
                                                   ACT.Identity, scale=conv_w[:, l, 1, u, bass.ds(q, 1)],
                                                   bias=conv_w[:, l, 3, u, bass.ds(q, 1)])\
                                       .then_inc(mid_ready, 1)
                            if l < 2:
                                act.wait_ge(conv_done, 2 * (n0 + q) + 1)
                                src = cv
                            else:
                                freed(stage, i, 2 * pair)
                                src = us
                            act.activation(us[:, 2 * pair, :] if l < 2 else cv[:, 2 * pair, :],
                                           src[:, 2 * pair, :], ACT.Silu).then_inc(silu_ready, 1)
                            act.wait_ge(act_ready, n0 + q + 1)
                            act.activation(chunks(Bhi[ABUF[l]])[:, 2 * i + pair, :], av[:, pair, :],
                                           ACT.Copy).then_inc(ahi_ready, 1)
                    rounds(n // 2, body)
                    if p == 0 and l < 2:
                        split_p(l)
                    norm = {0: "ple0", 1: "ple1", 2: None}[l] if p == 2 else None
                    residual(f"down{l}.{p}", norm, last=(l == 2 and p == 2))

            def embedding(l, nxt):
                for q in range(2):
                    used(f"pp{l}", 0, q)
                    for m in range(4):
                        bank, _ = tile_of(f"pp{l}", 0, 4 * q + m)
                        act.activation(pp[:, 4 * q + m, :], PS[:, bank, :], ACT.Copy)\
                           .then_inc(tile_free[bank], 1)
                root(f"ple{l}")
                act.wait_ge(r_ready, NORMS.index(nxt))

                def body(i):
                    for j in range(4):
                        m = 4 * i + j
                        if m < 2:
                            used(f"gate{l}", i, j)
                        freed(f"gate{l}", i, j)
                        act.activation(gt[:, j % 2, :], gt[:, j % 2, :], ACT.Sigmoid)\
                           .then_inc(sig_ready, 1)
                        act.wait_ge(ple_added, KC * l + m + 1)
                        square_and_high(nxt, m, j % 2)
                        if m >= 2:
                            used(f"gate{l}", i, j)
                rounds(2, body)

            def split_p(l):
                act.wait_ge(p_in, 16 * l + 16)
                for k in range(2):
                    act.activation(qkhi[:, 0, k, :], PT[:, k, :], ACT.Copy).then_inc(phi_ready, 1)

            def fetch_p(l):
                act.dma_start(PT, pT[l]).then_inc(p_in, 16)

            act.dma_start(par_sb[:, :], par).then_inc(par_in, 16)
            for q in range(4):
                act.dma_start(X[:, 2 * q:2 * q + 2, :], xT[:, 2 * q:2 * q + 2, :]).then_inc(x_in[q], 16)
            act.dma_start(con_sb[:, :], con).then_inc(con_in, 16)
            act.dma_start(AR[:, 0:T].bitcast(I32), posd).then_inc(pos_in, 16)
            act.dma_start(AR[:, 4096:4096 + 256], lamd).then_inc(lam_in, 16)
            act.wait_ge(par_in, 16)
            for m in range(KC):
                if m % 2 == 0:
                    act.wait_ge(x_in[m // 2], 16)
                    high(m // 2, m // 2, m // 2 // RAWS)
                square_and_high("attn0", m, m % 2)
            act.wait_ge(consts_ready, 4)
            act.activation(sinT[:, :], angs[:, 1, :], ACT.Sin).then_inc(trig_ready, 1)
            act.activation(cosT[:, :], angs[:, 2, :], ACT.Sin).then_inc(trig_ready, 1)
            act.activation(lam[:, 2:4], lam[:, 0:2], ACT.Exp).then_inc(trig_ready, 1)
            root("attn0")
            for t in range(2):
                used("qk1a", 0, t)
            values("v1", 2, 4, T)
            swap_halves("qk1", 0, 2)
            q_high(*place_of(1, 0))
            attention(1)
            output_square(7)
            output_root(True)
            for h in (6, 7):
                normed_high(h)
            residual("o1", "ffn0")
            fetch_p(0)
            feed_forward(0)
            embedding(0, "attn1")
            for t in range(2):
                used("kq2a", 0, t)
                if t == 0:
                    root("attn1")
            values("v2", 1, 2, 256)
            for t in range(2):
                swap_halves("kq2a", t, QT0[2] + t)
            for t in range(2):
                q_high(QT0[2] + t, 0, 1 - t)
            swap_halves("kq2", 0, QT0[2] + 2)
            q_high(*place_of(2, 0))
            swap_halves("kq2", 1, QT0[2] + 3)
            attention(2)
            output_high(OA, 7)
            residual("o2", "ffn1")
            fetch_p(1)
            feed_forward(1)
            embedding(1, "final")
            for t in range(2):
                used("a3", 0, t)
            root("final")
            for m in range(KC):
                act.wait_ge(y_ready, m + 1)
                square_and_high("mix", m, (m + 1) % 2)
            for t in range(2, 4):
                used("a3", 0, t)
            root("mix")
            for t in range(4, 8):
                used("a3", 0, t)
            for q in range(4):
                freed("a3", 0, 2 * q + 1)
                act.activation(atmp[:, 3 * (q % 2) + 2, :], atmp[:, 3 * (q % 2) + 1, :], ACT.Sigmoid)\
                   .then_inc(asig_ready, 1)
            act.activation(wfhi[:, :], cpar("w_f", 0, KC * 8), ACT.Copy).then_inc(phi_ready, 1)
            values("v3", 1, 4, T)
            act.wait_ge(f_lin, 1)
            own.step(act.activation(frow[:, 1, :], frow[:, 0, :], ACT.Abs))
            own.wait()
            own.step(act.activation(frow[:, 1, :], frow[:, 1, :], ACT.Exp, scale=-1.0))
            own.wait()
            act.activation(frow[:, 1, :], frow[:, 1, :], ACT.Ln, bias=1.0).then_inc(f_exp, 1)

            def head_square(t):
                act.wait_ge(rope_ready, QT0[3] + t + 1)
                if t >= 2:
                    act.wait_ge(hsum_done, t - 1)
                act.activation(sq[:, t % 2, :], qraw3[:, t % 2, :], ACT.Square).then_inc(hsq_ready, 1)

            def head_root(t):
                bank, _ = tile_of("qk3", 0, t)
                act.wait_ge(hsum_done, t + 1)
                if t:
                    act.wait_ge(orinv_ready, 2 + t)
                act.activation(sinT[:, :], PS[:, bank, :], ACT.Sqrt, scale=1.0 / 64, bias=eps[:, 0:1])\
                   .then_inc(tile_free[bank], 1)

            def head_high(t):
                _, b, u = place_of(3, t)
                act.wait_ge(hroot_ready, t + 1)
                act.activation(qkhi[:, b, u, :], qraw3[:, u, :], ACT.Copy, scale=gs[:, 1 + u:2 + u])\
                   .then_inc(qhi_ready, 1)

            for t in range(2):
                used("qk3", 0, t)
                head_square(t)
            head_root(0)
            used("qk3", 0, 2)
            head_root(1)
            act.wait_ge(cum_ready, 1)
            act.activation(cc[0:8, :], frow[:, 0, :], ACT.Copy).then_inc(cchi_ready, 1)
            for t in range(2):
                head_high(t)
            head_square(2)
            attention(3)
            for c in range(4):
                output_high(OA3, c)
            for m in range(8):
                used("gb3", 0, m)
                freed("gb3", 0, m)
                act.activation(G[:, m, :], t3[:, m % 2, :], ACT.Sigmoid).then_inc(sig_ready, 1)
            for q in range(4):
                used("ao3", 0, q)

            def join_gate(m):
                used("gc3", 0, JOIN_SLAB["gate", m])
                freed("gc3", 0, JOIN_TILE["gate", m])
                act.activation(t6[:, m % 6, :], t6[:, m % 6, :], ACT.Sigmoid).then_inc(sig_ready, 1)

            def join_conv(q):
                used("gc3", 0, JOIN_SLAB["conv", q])
                for m in (2 * q, 2 * q + 1):
                    act.wait_ge(a_ready, CT + m + 1)
                    act.activation(chunks(Bhi[1])[:, m, :], G[:, m, :], ACT.Copy)\
                       .then_inc(chi_ready, 1)

            for m in range(2):
                join_gate(m)
            for c in range(CT):
                act.wait_ge(cen_ready, c + 1)
                if c >= 2:
                    act.wait_ge(var_done, c - 1)
                act.activation(sq[:, c % 2, :], cvo[:, c, :], ACT.Square).then_inc(csq_ready, 1)
            for m in (2, 3):
                used("gc3", 0, JOIN_SLAB["gate", m])
            act.wait_ge(var_done, CT)
            act.activation(sinT[:, :], PS[:, 6, :], ACT.Sqrt, scale=1.0 / CONV, bias=eps[:, 0:1])\
               .then_inc(croot_ready, 1)
            for m in (2, 3):
                freed("gc3", 0, JOIN_TILE["gate", m])
                act.activation(t6[:, m, :], t6[:, m, :], ACT.Sigmoid).then_inc(sig_ready, 1)
            used("gc3", 0, JOIN_SLAB["gate", 4])
            for c in range(CT):
                act.wait_ge(cn_ready, c + 1)
                own.step(act.activation(cvo[:, c, :], cvo[:, c, :], ACT.Silu,
                                        scale=cpar("g_ln", c), bias=cpar("b_ln", c)))
            own.wait()
            for c in range(CT):
                act.activation(qkhi[:, c // 2, c % 2, :], cvo[:, c, :], ACT.Copy)\
                   .then_inc(chi_ready, 1)
            used("gc3", 0, JOIN_SLAB["gate", 5])
            for m in (4, 5):
                freed("gc3", 0, JOIN_TILE["gate", m])
                act.activation(t6[:, m, :], t6[:, m, :], ACT.Sigmoid).then_inc(sig_ready, 1)
            for what, n in JOIN[6:]:
                if what == "gate":
                    join_gate(n)
                else:
                    join_conv(n)
            residual("out3", "ffn2")
            feed_forward(2)

        @block.vector
        def _(dve):
            own = Own(dve, dve_step)
            tt, stt, ts = dve.tensor_tensor, dve.scalar_tensor_tensor, dve.tensor_scalar

            def done(stage, i, j):
                dve.wait_ge(slab_done, slab_of(stage, i, j)[0] + 1)

            def scaled(out, stage, i, j):
                bank, _ = tile_of(stage, i, j)
                tt(out, PS[:, bank, :], R[:, :], ALU.mult).then_inc(tile_free[bank], 1)

            def low(norm, m):
                if norm in GAIN:
                    name, col = GAIN[norm]
                    k = KC * SPLITS.index(norm) + m
                    dve.wait_ge(xhi_ready, k + 1)
                    b = BUF[norm]
                    stt(chunks(Blo[b])[:, m, :], X[:, m, :], gain(name, col, m),
                        f32(chunks(Bhi[b])[:, m, :]), ALU.mult, ALU.subtract).then_inc(x_split, 1)

            def add_square(norm, m, slot):
                c = KC * NORMS.index(norm) + m
                dve.wait_ge(sq_ready, c + 1)
                tt(acc[:, :], acc[:, :], sq[:, slot, :], ALU.add).then_inc(sq_used, 1)
                dve.wait_ge(sq_used, c + 1)

            def low_and_add(norm, m, slot):
                low(norm, m)
                add_square(norm, m, slot)

            def clear_sum():
                own.step(dve.memset(acc[:, :], 0.0))
                own.wait()

            def factor(norm):
                n = NORMS.index(norm)
                dve.wait_ge(root_ready, n + 1)
                dve.reciprocal(R[:, :], sq[:, 0, :]).then_inc(r_ready, 1)
                dve.wait_ge(r_ready, n + 1)

            def rounds(n, per, body):
                if n <= 2:
                    for i in range(n):
                        body(i)
                else:
                    own.rounds(0, n, per, body)

            def residual(stage, norm):
                if norm:
                    clear_sum()

                def body(i):
                    for j in range(4):
                        m = 4 * i + j
                        done(stage, i, j)
                        bank, before = tile_of(stage, i, j)
                        tt(X[:, m, :], X[:, m, :], PS[:, bank, :], ALU.add)\
                            .then_inc(tile_free[bank], 1)
                        if norm:
                            low_and_add(norm, m, j % 2)
                rounds(2, 0, body)

            def columns(n):
                dve.wait_ge(rcol_done, n)
                dve.tensor_copy(rcol[:, :], PS[:, 7, 0:TB]).then_inc(rcol_ready, 1)
                dve.wait_ge(rcol_ready, n)

            def values_low(stage, halves, width):
                n0 = {"v1": 0, "v2": 2 * TB, "v3": 3 * TB}[stage]
                for hf in range(halves):
                    for t in range(TB):
                        bank, _ = tile_of(stage, 0, hf * TB + t)
                        dve.wait_ge(vhi_ready, n0 + hf * TB + t + 1)
                        if stage == "v1":
                            v = [b[:, :].rearrange("p (k n) -> p k n", k=TB)[:, t, hf * T:hf * T + T]
                                 for b in (Blo[1], Bhi[1])]
                            parts = [(v[0], PS[:, bank, :], v[1])]
                        else:
                            lo = padded(stage, Blo, PS[:, bank, 0:width], t)
                            hi = padded(stage, Bhi, PS[:, bank, 0:width], t)
                            parts = [(a, s, b) for (a, s), (b, _) in zip(lo, hi)]
                        for q, (out, src, hi) in enumerate(parts):
                            ins = stt(out, src, rcol[:, t:t + 1], f32(hi), ALU.mult, ALU.subtract)
                            if q == 0 and len(parts) == 2:
                                own.step(ins)
                        ins.then_inc(tile_free[bank], 1)
                    if stage == "v1" and hf == 0:
                        for t in range(2):
                            rope("qk1a", t, t)
                        for t in range(2):
                            q_low(t, 0, t)

            def zero_padding(stage):
                nh = 4 if stage == "v2" else 8
                for b in (Bhi[1], Blo[1]):
                    v = b[:, 0:TB * nh * P].rearrange("p (k two c) -> p k two c", two=2, c=P)
                    for u in range(2):
                        dve.memset(f32(v[:, :, u, 64 - 64 * u:P - 64 * u]), 0.0).then_inc(pad_ready, 1)

            def rope(stage, t, n):
                bank, before = tile_of(stage, 0, t)
                b = n % 2
                dve.wait_ge(swap_ready, n + 1)
                if n >= 2:
                    dve.wait_ge(q_ready, n - 1)
                    dve.wait_ge(qhi_ready, n - 1)
                tt(qraw[:, b, :], PS[:, bank, :], rC, ALU.mult).then_inc(tile_free[bank], 1)
                own.step(tt(swap[:, b, :], swap[:, b, :], rS, ALU.mult))
                own.wait()
                dve.wait_ge(tile_free[bank], before + 2)
                tt(qraw[:, b, :], qraw[:, b, :], swap[:, b, :], ALU.add).then_inc(rope_ready, 1)

            def q_low(n, b, which):
                dve.wait_ge(qhi_ready, n + 1)
                stt(qklo[:, b, which, :], qraw[:, n % 2, :], (QSCALE, 1.0)[which],
                    f32(qkhi[:, b, which, :]), ALU.mult, ALU.subtract).then_inc(q_ready, 1)

            def maxima(kind, g):
                nb = band(kind, g % 4)[1]
                for s in range(2):
                    n = SC0[kind] + 2 * g + s
                    dve.wait_ge(score_done, n + 1)
                    src, c = PS[:, score_bank(kind, n), 0:nb * P], n % 4
                    if kind == 2:
                        own.step(dve.tensor_reduce(nmax[:, 4 + c:5 + c], src, AX, ALU.max,
                                                   negate=True))
                    else:
                        dve.tensor_reduce(nmax[:, c:c + 1], src, AX, ALU.max, negate=True)\
                            .then_inc(max_ready, 1)
                if kind == 2:
                    own.wait()
                    c = (SC0[2] + 2 * g) % 4
                    h = head_of(g // 4, 0)
                    minus_sinks = nsink[:, h:h + 5:4]
                    tt(nmax[:, c:c + 2], nmax[:, 4 + c:6 + c], minus_sinks, ALU.min)\
                        .then_inc(max_ready, 2)
                    dve.wait_ge(max_ready, SC0[2] + 2 * g + 2)
                    tt(sdiff[:, c:c + 2], nmax[:, c:c + 2], minus_sinks, ALU.subtract)\
                        .then_inc(sdiff_ready, 1)

            def normalise(kind, g):
                n = SC0[kind] + 2 * g
                nb = band(kind, g % 4)[1]
                pr, c, b = probs(kind), n % 4, 2 * (g % 2)
                dve.wait_ge(exp_ready, n + 2)
                if kind == 2:
                    dve.wait_ge(sink_ready, g + 1)
                    own.step(tt(rsum[:, c:c + 2], rsum[:, c:c + 2], rsum[:, 4 + c:6 + c], ALU.add))
                    own.wait()
                own.step(dve.reciprocal(rinv[:, c:c + 2], rsum[:, c:c + 2]))
                own.wait()
                if kind == 1:
                    own.step(tt(rinv[:, c + 1:c + 2], rinv[:, c + 1:c + 2], lam[:, 5:6], ALU.mult))
                    own.step(ts(pr[:, b, :], pr[:, b, :], rinv[:, c:c + 1], None, ALU.mult))
                    own.wait()
                    stt(pr[:, b + 1, :], pr[:, b + 1, :], rinv[:, c + 1:c + 2], pr[:, b, :],
                        ALU.mult, ALU.add).then_inc(prob_ready, 1)
                else:
                    for s in range(2):
                        v = pr[:, b + s, 0:nb * P]
                        ts(v, v, rinv[:, c + s:c + s + 1], None, ALU.mult).then_inc(prob_ready, 1)

            def prob_low(kind, g):
                blocks = band(kind, g % 4)[1]
                for s in range(HP[kind]):
                    n = PB0[kind] + HP[kind] * g + s
                    dve.wait_ge(pthi_ready, n + 1)
                    tt(transposed(ptlo, kind, g, s), PS[:, 2 + n % 2, 0:blocks * P]
                       .rearrange("p (k q) -> p k q", k=blocks), f32(transposed(pthi, kind, g, s)),
                       ALU.subtract).then_inc(pt_ready, 1)

            def norm_output(h):
                dve.wait_ge(obc_done, h + 1)
                tt(OA[:, h, :], OA[:, h, :], PS[:, spread_bank(h), :], ALU.mult).then_inc(onorm_ready, 1)

            def normed_low(h):
                dve.wait_ge(ohi_ready, h + 1)
                stt(chunks(Blo[0])[:, h, :], OA[:, h, :], gs[:, 0:1], f32(chunks(Bhi[0])[:, h, :]),
                    ALU.mult, ALU.subtract).then_inc(o_split, 1)

            def invert_output_root(last):
                dve.wait_ge(oroot_ready, 2 if last else 1)
                dve.reciprocal((acc if last else R)[0:8, :], acc[0:8, :]).then_inc(orinv_ready, 1)

            def output_low(src, c):
                hi, lo = ((pthi[:, c, :], ptlo[:, c, :]) if src is OA3 else
                          (chunks(Bhi[0])[:, c, :], chunks(Blo[0])[:, c, :]))
                dve.wait_ge(ohi_ready, OP0[3 if src is OA3 else 2] + c + 1)
                tt(lo, src[:, c, :], f32(hi), ALU.subtract).then_inc(o_split, 1)

            def attention(kind):
                steps = 4 * PAIRS[kind]
                for g in range(AHEAD[kind]):
                    maxima(kind, g)
                for g in range(steps):
                    begun, halfway = finished(kind, g - 1), finished(kind, g - 2)
                    normalise(kind, g)
                    if g + AHEAD[kind] < steps:
                        maxima(kind, g + AHEAD[kind])
                    if kind < 3 and begun is not None:
                        rope(PROJ[kind], begun, place_of(kind, begun)[0])
                    if kind < 3 and halfway is not None:
                        q_low(*place_of(kind, halfway))
                    if kind == 3 and begun is not None:
                        head_scaled(begun)
                    if kind == 3 and halfway is not None:
                        head_norm(halfway)
                        head_low(halfway)
                    if kind == 1:
                        if g == 4 * OFIRST + 2:
                            invert_output_root(False)
                        for h in SPREAD.get(g, ()):
                            norm_output(h)
                        for h in SPREAD.get(g - 1, ()):
                            normed_low(h)
                    prob_low(kind, g)
                    if kind == 2:
                        for c in OSPLIT.get(g, ()):
                            output_low(OA, c)

            def feed_forward(l):
                factor(f"ffn{l}")
                n0 = l * FC
                for p, n in enumerate(PARTS):
                    stage = f"up{l}.{p}"

                    def body(i):
                        for pair in range(2):
                            q = PART0[p] + 2 * i + pair
                            for u in range(2):
                                done(stage, i, 2 * pair + u)
                                scaled(us[:, 2 * pair + u, :], stage, i, 2 * pair + u)
                            if l < 2:
                                for u in range(2):
                                    c, x = cv[:, 2 * pair + u, :], us[:, 2 * pair + u, :]
                                    dve.wait_ge(mid_ready, 2 * (n0 + q) + u + 1)
                                    own.step(stt(c[:, 1:T], x[:, 0:T - 1], conv_w[:, l, 0, u, bass.ds(q, 1)],
                                                 c[:, 1:T], ALU.mult, ALU.add))
                                    own.wait()
                                    stt(c[:, 0:T - 1], x[:, 1:T], conv_w[:, l, 2, u, bass.ds(q, 1)],
                                        c[:, 0:T - 1], ALU.mult, ALU.add).then_inc(conv_done, 1)
                                dve.wait_ge(conv_done, 2 * (n0 + q) + 2)
                            dve.wait_ge(silu_ready, n0 + q + 1)
                            if l < 2:
                                g, v = us[:, 2 * pair, :], cv[:, 2 * pair + 1, :]
                            else:
                                g, v = cv[:, 2 * pair, :], us[:, 2 * pair + 1, :]
                                bank, before = tile_of(stage, i, 2 * pair + 1)
                                dve.wait_ge(tile_free[bank], before + 2)
                            own.wait()
                            tt(av[:, pair, :], g, v, ALU.mult).then_inc(act_ready, 1)
                            dve.wait_ge(ahi_ready, n0 + q + 1)
                            k = 2 * i + pair
                            b = ABUF[l]
                            tt(chunks(Blo[b])[:, k, :], av[:, pair, :], f32(chunks(Bhi[b])[:, k, :]),
                               ALU.subtract).then_inc(act_split, 1)
                            dve.wait_ge(act_split, n0 + q + 1)
                    rounds(n // 2, 4 if l < 2 else 0, body)
                    if p == 0 and l < 2:
                        for k in range(2):
                            dve.wait_ge(phi_ready, 2 * l + k + 1)
                            tt(qklo[:, 0, k, :], PT[:, k, :], f32(qkhi[:, 0, k, :]), ALU.subtract)\
                                .then_inc(p_split, 1)
                    norm = {0: "ple0", 1: "ple1", 2: None}[l] if p == 2 else None
                    residual(f"down{l}.{p}", norm)

            def embedding(l, nxt):
                factor(f"ple{l}")
                clear_sum()

                def body(i):
                    for j in range(4):
                        m = 4 * i + j
                        done(f"gate{l}", i, j)
                        scaled(gt[:, j % 2, :], f"gate{l}", i, j)
                        if m:
                            add_square(nxt, m - 1, (j - 1) % 2)
                        dve.wait_ge(sig_ready, KC * l + m + 1)
                        own.step(tt(gu[:, j % 2, :], gt[:, j % 2, :], pp[:, m, :], ALU.mult))
                        own.wait()
                        tt(X[:, m, :], X[:, m, :], gu[:, j % 2, :], ALU.add).then_inc(ple_added, 1)
                        dve.wait_ge(ple_added, KC * l + m + 1)
                        low(nxt, m)
                rounds(2, 0, body)
                add_square(nxt, KC - 1, (KC - 1) % 2)

            for b in range(BANKS):
                dve.memset(credit[:, b:b + 1], 0.0).then_inc(tile_free[b], 1)
            own.step(dve.memset(f32(cc[:, :]), 0.0))
            dve.memset(eps[:, :], EPS).then_inc(consts_ready, 1)
            clear_sum()
            dve.wait_ge(par_in, 16)
            own.step(tt(gfm[:, :], cpar("final_norm", 0, KC), cpar("g_mix", 0, KC), ALU.mult))
            own.step(ts(nsink[:, :], cpar("sinks", 0, 16), -1.0, None, ALU.mult))
            for q in range(4):
                dve.wait_ge(x_in[q], 16)
                for m in (2 * q, 2 * q + 1):
                    low_and_add("attn0", m, m % 2)
            dve.wait_ge(con_in, 16)
            dve.tensor_copy(constR[:, :, :], con_sb[:, 0:3 * P].rearrange("p (n c) -> p n c", n=3))\
               .then_inc(consts_ready, 1)
            dve.tensor_copy(minusR[:, :, :], con_sb[:, CCOLS["minus"][0]:CCOLS["minus"][1]]
                            .rearrange("p (n c) -> p n c", c=1).broadcast_to((P, 8, P)))\
               .then_inc(consts_ready, 1)
            dve.wait_ge(consts_ready, 3)
            dve.wait_ge(pos_in, 16)
            A = angs
            MAGIC = 1.5 * 2.0 ** 23
            own.step(dve.tensor_copy(A[:, 1, :], A[:, 0, :].bitcast(I32)))
            own.wait()
            own.step(ts(A[:, 1, :], A[:, 1, :], ccon("freq"), None, ALU.mult))
            own.wait()
            own.step(ts(A[:, 3, :], A[:, 1, :], 1.0 / (2 * np.pi), MAGIC, ALU.mult, ALU.add))
            own.wait()
            own.step(ts(A[:, 3, :], A[:, 3, :], MAGIC, None, ALU.subtract))
            own.wait()
            c1 = 6.28125
            c2 = float(np.float32(int((2 * np.pi - c1) * 2 ** 20) / 2 ** 20))
            c3 = 2 * np.pi - c1 - c2
            for c in (c1, c2, c3):
                own.step(stt(A[:, 1, :], A[:, 3, :], -c, A[:, 1, :], ALU.mult, ALU.add))
                own.wait()
            own.step(ts(A[:, 1, :], A[:, 1, :], float(np.float32(3.1415925)),
                        float(np.float32(-3.1415925)), ALU.min, ALU.max))
            own.wait()
            own.step(ts(A[:, 2, :], A[:, 1, :], -1.0, None, ALU.mult))
            own.wait()
            own.step(tt(A[:, 2, :], A[:, 1, :], A[:, 2, :], ALU.max))
            own.wait()
            own.step(ts(A[:, 2, :], A[:, 2, :], -1.0, np.pi / 2, ALU.mult, ALU.add))
            dve.wait_ge(lam_in, 16)
            L = AR[:, 4096:4096 + 256].rearrange("p (a b c) -> p a b c", a=2, b=2)
            M = AR[:, 4608:4608 + 128].rearrange("p (a c) -> p a c", a=2)
            own.step(tt(M, L[:, :, 0, :], L[:, :, 1, :], ALU.mult))
            own.wait()
            dve.tensor_reduce(lam[:, 0:2], M, AX, ALU.add).then_inc(consts_ready, 1)
            dve.wait_ge(trig_ready, 3)
            own.step(tt(lam[:, 4:5], lam[:, 3:4], lam[:, 2:3], ALU.subtract))
            own.wait()
            own.step(ts(lam[:, 5:6], lam[:, 4:5], -LAM_INIT, None, ALU.add))
            own.step(ts(gs[:, 0:1], cpar("subln"), 1.0 - LAM_INIT, None, ALU.mult))
            own.step(ts(gs[:, 1:2], cpar("g_q"), QSCALE, None, ALU.mult))
            own.step(dve.tensor_copy(gs[:, 2:3], cpar("g_k")))
            own.step(ts(sinT[:, :], sinT[:, :], ccon("sign"), None, ALU.mult))
            own.wait()

            def rope_tables():
                own.step(tt(rC, cosT[:, :], R[:, :], ALU.mult))
                own.step(tt(rS, sinT[:, :], R[:, :], ALU.mult))
                own.wait()

            factor("attn0")
            rope_tables()
            columns(1)
            values_low("v1", 2, T)
            rope("qk1", 0, 2)
            q_low(*place_of(1, 0))
            attention(1)
            invert_output_root(True)
            for h in (6, 7):
                norm_output(h)
            for h in (6, 7):
                normed_low(h)
            residual("o1", "ffn0")
            feed_forward(0)
            embedding(0, "attn1")
            zero_padding("v2")
            factor("attn1")
            rope_tables()
            columns(2)
            values_low("v2", 1, 256)
            for t in range(2):
                rope("kq2a", t, QT0[2] + t)
            for t in range(2):
                q_low(QT0[2] + t, 0, 1 - t)
            rope("kq2", 0, QT0[2] + 2)
            attention(2)
            output_low(OA, 7)
            residual("o2", "ffn1")
            feed_forward(1)
            embedding(1, "final")
            own.step(dve.memset(apad[:, :, 0:TAPS - 1], 0.0))
            factor("final")
            clear_sum()
            for m in range(KC):
                stt(X[:, m, :], X[:, m, :], cpar("final_norm", m), R[:, :], ALU.mult, ALU.mult)\
                    .then_inc(y_ready, 1)
                if m:
                    low_and_add("mix", m - 1, m % 2)
            low_and_add("mix", KC - 1, KC % 2)
            dve.wait_ge(root_ready, NORMS.index("mix") + 1)
            own.step(dve.reciprocal(cosT[:, :], sq[:, 0, :]))
            own.wait()
            tt(R[:, :], R[:, :], cosT[:, :], ALU.mult).then_inc(r_ready, 1)
            dve.wait_ge(r_ready, NORMS.index("mix") + 1)
            queue = [(c + u, w) for c in (0, 2) for w in range(TAPS) for u in range(2)]

            def taps(n):
                for _ in range(min(n, len(queue))):
                    c, w = queue.pop(0)
                    src, out = apad[:, c, w:w + T], cvo[:, c, :]
                    k = cpar("w_dw", w * CT + c)
                    if w == 0:
                        ins = ts(out, src, k, cpar("b_dw", c), ALU.mult, ALU.add)
                    else:
                        dve.wait_ge(dve_tap[c], w)
                        ins = stt(out, src, k, out, ALU.mult, ALU.add)
                    if w == TAPS - 1:
                        ins.then_inc(taps_done, 1)
                    else:
                        ins.then_inc(dve_tap[c], 1)

            def gate_a(q):
                b = 3 * (q % 2)
                dve.wait_ge(asig_ready, q + 1)
                bank, before = tile_of("a3", 0, 2 * q)
                dve.wait_ge(tile_free[bank], before + 2)
                tt(apad[:, q, TAPS - 1:], atmp[:, b, :], atmp[:, b + 2, :], ALU.mult)\
                    .then_inc(a_ready, 1)

            for q in range(4):
                if q >= 2:
                    dve.wait_ge(a_ready, q - 1)
                for u in (1, 0):
                    done("a3", 0, 2 * q + u)
                    scaled(atmp[:, 3 * (q % 2) + u, :], "a3", 0, 2 * q + u)
                if q:
                    gate_a(q - 1)
            gate_a(3)
            dve.wait_ge(a_ready, 4)
            def head_scaled(t):
                done("qk3", 0, t)
                bank, _ = tile_of("qk3", 0, t)
                if t >= 2:
                    dve.wait_ge(q_ready, QT0[3] + t - 1)
                tt(qraw3[:, t % 2, :], PS[:, bank, :], R[:, :], ALU.mult).then_inc(rope_ready, 1)

            dve.wait_ge(phi_ready, 5)
            tt(wflo[:, :], cpar("w_f", 0, KC * 8), f32(wfhi[:, :]), ALU.subtract).then_inc(p_split, 1)
            columns(3)
            zero_padding("v3")
            taps(22)
            values_low("v3", 1, T)
            taps(4)
            dve.wait_ge(f_done, 1)
            own.step(tt(frow[:, 0, :], PS[0:8, 6, :], R[0:8, :], ALU.mult))
            own.wait()
            own.step(ts(frow[:, 0, :], frow[:, 0, :], cpar("b_forget")[0:8], None, ALU.add))
            own.wait()
            ts(frow[:, 2, :], frow[:, 0, :], 0.0, None, ALU.min).then_inc(f_lin, 1)
            dve.wait_ge(f_lin, 1)
            head_scaled(0)
            dve.wait_ge(f_exp, 1)
            own.step(tt(frow[:, 2, :], frow[:, 2, :], frow[:, 1, :], ALU.subtract))
            own.wait()
            own.step(dve.memset(frow[:, 1, :], 1.0))
            own.wait()
            dve.tensor_tensor_scan(frow[:, 0, :], frow[:, 1, :], frow[:, 2, :], 0.0, ALU.mult, ALU.add)\
                .then_inc(cum_ready, 1)
            dve.wait_ge(cum_ready, 1)

            def head_norm(t):
                bank, before = tile_of("qk3", 0, t)
                dve.wait_ge(tile_free[bank], before + 2)
                if t:
                    dve.wait_ge(hroot_ready, t)
                dve.reciprocal(cosT[:, :], sinT[:, :]).then_inc(orinv_ready, 1)
                dve.wait_ge(orinv_ready, t + 3)
                dve.wait_ge(rope_ready, QT0[3] + t + 1)
                tt(qraw3[:, t % 2, :], qraw3[:, t % 2, :], cosT[:, :], ALU.mult).then_inc(hroot_ready, 1)

            def head_low(t):
                _, b, u = place_of(3, t)
                dve.wait_ge(qhi_ready, QT0[3] + t + 1)
                stt(qklo[:, b, u, :], qraw3[:, u, :], gs[:, 1 + u:2 + u], f32(qkhi[:, b, u, :]),
                    ALU.mult, ALU.subtract).then_inc(q_ready, 1)

            head_scaled(1)
            for t in range(2):
                head_norm(t)
            dve.wait_ge(cchi_ready, 1)
            tt(cc[32:40, :], frow[:, 0, :], f32(cc[0:8, :]), ALU.subtract).then_inc(cc_ready, 1)
            for t in range(2):
                head_low(t)
            head_scaled(2)
            attention(3)
            for c in range(4):
                output_low(OA3, c)
            dve.wait_ge(o_split, 20)
            for m in range(8):
                done("gb3", 0, m)
                if m >= 2:
                    dve.wait_ge(sig_ready, 2 * KC + m - 1)
                scaled(t3[:, m % 2, :], "gb3", 0, m)
                taps(TAPS_A_TILE)
            dve.wait_ge(sig_ready, 3 * KC)

            def gate_attention(q):
                done("ao3", 0, q)
                for m in (2 * q, 2 * q + 1):
                    bank, _ = tile_of("ao3", 0, m)
                    tt(G[:, m, :], G[:, m, :], PS[:, bank, :], ALU.mult).then_inc(tile_free[bank], 1)

            for q in range(4):
                gate_attention(q)
                taps(-(-len(queue) // (4 - q)))

            def join_scaled(m):
                done("gc3", 0, JOIN_SLAB["gate", m])
                if m >= 6:
                    dve.wait_ge(a_ready, CT + m - 5)
                scaled(t6[:, m % 6, :], "gc3", 0, JOIN_TILE["gate", m])

            def join_conv(q):
                done("gc3", 0, JOIN_SLAB["conv", q])
                for u in range(2):
                    m = 2 * q + u
                    dve.wait_ge(sig_ready, 3 * KC + m + 1)
                    bank, before = tile_of("gc3", 0, JOIN_TILE["conv", q] + u)
                    t = t6[:, m % 6, :]
                    tt(t, t, PS[:, bank, :], ALU.mult).then_inc(tile_free[bank], 1)
                    dve.wait_ge(tile_free[bank], before + 2)
                    tt(G[:, m, :], G[:, m, :], t, ALU.add).then_inc(a_ready, 1)
                for u in range(2):
                    m = 2 * q + u
                    dve.wait_ge(chi_ready, CT + m + 1)
                    tt(chunks(Blo[1])[:, m, :], G[:, m, :], f32(chunks(Bhi[1])[:, m, :]), ALU.subtract)\
                        .then_inc(c_split, 1)

            dve.wait_ge(taps_done, CT)
            for m in range(2):
                join_scaled(m)
            dve.wait_ge(mean_done, 1)
            for c in range(CT):
                stt(cvo[:, c, :], PS[:, 5, :], -1.0 / CONV, cvo[:, c, :], ALU.mult, ALU.add)\
                    .then_inc(cen_ready, 1)
            for m in (2, 3):
                join_scaled(m)
            dve.wait_ge(croot_ready, 1)
            own.step(dve.reciprocal(cosT[:, :], sinT[:, :]))
            own.wait()
            dve.wait_ge(cen_ready, CT)
            for c in range(CT):
                tt(cvo[:, c, :], cvo[:, c, :], cosT[:, :], ALU.mult).then_inc(cn_ready, 1)
            join_scaled(4)
            for c in range(CT):
                dve.wait_ge(chi_ready, c + 1)
                tt(qklo[:, c // 2, c % 2, :], cvo[:, c, :], f32(qkhi[:, c // 2, c % 2, :]),
                   ALU.subtract).then_inc(c_split, 1)
            join_scaled(5)
            own.wait()
            for what, n in JOIN[6:]:
                if what == "gate":
                    join_scaled(n)
                else:
                    join_conv(n)
            residual("out3", "ffn2")
            feed_forward(2)


def slabs_of(inputs):
    out = np.empty((SLABS, P, D), np.float32)
    at = [0]

    def put(a):
        out[at[0]] = a.reshape(P, -1)
        at[0] += 1

    def tiles(w, cols, nk=KC, rows=None):
        w = w[:, cols] if rows is None else w[rows][:, cols]
        w = w.reshape(nk, P, P).transpose(1, 0, 2)
        s = np.zeros((P, KC, P), np.float32)
        s[:, :nk] = w
        put(s)

    def wide(w, cols, slabs):
        w = w[:, cols]
        kk = KC // slabs
        for q in range(slabs):
            put(w[q * kk * P:(q + 1) * kk * P].reshape(kk, P, -1).transpose(1, 0, 2))

    def group(w, nk, per):
        n = w.shape[1] // P
        v = w.reshape(nk, P, n, P).transpose(1, 2, 0, 3)
        for q in range(0, n, per):
            put(v[:, q:q + per])

    col = lambda m, base=0: slice(base + m * P, base + m * P + P)

    def feed(up, down):
        ff = FC * P
        for p, n in enumerate(PARTS):
            for c in range(PART0[p], PART0[p] + n):
                tiles(up, col(c))
                tiles(up, col(c, ff))
            for m in range(KC):
                tiles(down, col(m), n, slice(PART0[p] * P, (PART0[p] + n) * P))

    def layer_tail(l):
        feed(inputs["ffn_w_up"][l], inputs["ffn_w_down"][l])
        group(inputs["ple_w_proj"][l], 2, 4)
        for m in range(KC):
            tiles(inputs["ple_w_gate"][l], col(m))

    w = inputs["diff_w_qkv"][0]
    for h in range(8):
        tiles(w, col(h))
        tiles(w, col(h, D))
        if h == 0:
            for hf in range(2):
                wide(w, slice(2 * D + hf * T, 2 * D + hf * T + T), 4)
    for m in range(KC):
        tiles(inputs["diff_w_o"][0], col(m))
    layer_tail(0)
    pairs = [(j, j + 4) if j < 4 else (j + 4, j + 8) for j in range(8)]
    order = np.concatenate([np.arange(64) + 64 * h for pair in pairs for h in pair])
    w = inputs["swa_w_qkv"][0]
    for m in range(8):
        if m < 2:
            tiles(w, col(m, D))
        tiles(w, order[m * P:m * P + P])
        if m == 0:
            wide(w, slice(1280, 1536), 2)
    for m in range(KC):
        tiles(inputs["swa_w_o"][0][order], col(m))
    layer_tail(1)
    w = inputs["w_in_2"][0]
    for c in range(CT):
        tiles(w, col(c))
        tiles(w, col(c, CONV))
    wide(w, slice(2048, 2560), 4)
    for j in range(4):
        tiles(w, col(j, 1024))
        tiles(w, col(j, 1536))
    for m in range(KC):
        tiles(w, col(m, 3592))
    group(inputs["w_attn_out_2"][0], 4, 2)
    for what, n in JOIN:
        if what == "gate":
            tiles(w, col(n, 2568))
        else:
            group(inputs["w_conv_out_2"][0][:, 2 * n * P:2 * n * P + 2 * P], 4, 2)
    for m in range(KC):
        tiles(inputs["w_out_2"][0], col(m))
    feed(inputs["w_ffn_in_2"][0], inputs["w_ffn_out_2"][0])
    assert at[0] == SLABS
    return out


def small_parameters(inputs):
    out = np.empty((P, NPAR), np.float32)

    def put(name, a):
        lo, hi = PCOLS[name]
        out[:, lo:hi] = a.reshape(P, hi - lo)

    def columns(v):
        return v.reshape(-1, P).T

    def spread(v):
        return np.broadcast_to(v.reshape(1, -1), (P, v.size))

    for name in ("attn_norm", "ffn_norm", "ple_norm", "final_norm"):
        put(name, columns(inputs[name]))
    put("g_mix", columns(inputs["g_mix_2"]))
    put("g_ffn", columns(inputs["g_ffn_2"]))
    put("subln", columns(inputs["diff_subln"]))
    cw = np.concatenate([inputs["ffn_conv_w"], inputs["ffn_conv_b"][:, None]], axis=1)
    put("conv_w", columns(cw))
    put("sinks", spread(inputs["swa_sinks"]))
    put("b_forget", np.concatenate([inputs["b_forget_2"][0], np.zeros(P - 8, np.float32)])[:, None])
    put("w_dw", columns(inputs["w_dw_2"]))
    put("b_dw", columns(inputs["b_dw_2"]))
    put("g_ln", columns(inputs["g_conv_ln_2"]))
    put("b_ln", columns(inputs["b_conv_ln_2"]))
    put("g_q", np.concatenate([inputs["g_q_2"][0]] * 2)[:, None])
    put("g_k", np.concatenate([inputs["g_k_2"][0]] * 2)[:, None])
    put("w_f", inputs["w_in_2"][0][:, 2560:2568].reshape(KC, P, 8).transpose(1, 0, 2))
    return out


def kernel(**inputs):
    import concourse.bacc as _bacc
    from concourse.bass_utils import run_bass_kernel_spmd as _run

    inputs = {k: np.asarray(v) for k, v in inputs.items()}
    arrays = {
        "xT": np.ascontiguousarray(inputs["x"][0].T.reshape(KC, P, T).transpose(1, 0, 2)),
        "pT": np.ascontiguousarray(
            inputs["p"][:, 0].transpose(0, 2, 1).reshape(2, 2, P, T).transpose(0, 2, 1, 3)),
        "positions": np.ascontiguousarray(np.broadcast_to(inputs["positions"], (P, T))),
        "weights": slabs_of(inputs),
        "parameters": small_parameters(inputs),
        "constants": constants(),
        "lambdas": np.ascontiguousarray(
            np.broadcast_to(inputs["diff_lambda"].reshape(1, 256), (P, 256))),
    }
    nc = _bacc.Bacc("TRN2", target_bir_lowering=False, num_devices=1, dynamic_dma_scratch_size=4096)
    args = [nc.dram_tensor(f"in_{name}", a.shape, mybir.dt.from_np(a.dtype), kind="ExternalInput").ap()
            for name, a in arrays.items()]
    out = nc.dram_tensor("out_0", (P, KC, T), F32, kind="ExternalOutput").ap()
    build(nc, *args, out)
    r = _run(nc, [{f"in_{name}": a for name, a in arrays.items()}], core_ids=[0])
    got = r.results[0]["out_0"]
    return np.ascontiguousarray(got.transpose(2, 1, 0).reshape(1, T, D))
```
